# Optimizing a Trainium2 kernel written in Bass

```python
import math, functools
import jax, jax.numpy as jnp
from jax import lax
import numpy as np

D_MODEL = 1024
BATCH = 1
SEQ = 1024
DEPTH = 1
DEC_BATCH = 8
DEC_SEQ = 8
PAST_LEN = 1024
PAGE_SIZE = 128

HEAD_DIM = 64
D_MIX = D_MODEL
D_ATTN = D_MIX // 2
D_SSD = D_MIX - D_ATTN
N_ATTN_HEADS = D_ATTN // HEAD_DIM
N_SSD_HEADS = D_SSD // HEAD_DIM
SSD_GROUPS = 2
HEADS_PER_GROUP = N_SSD_HEADS // SSD_GROUPS
D_STATE = 128
CONV_W = 4
CONV_DIM = D_SSD + 2 * SSD_GROUPS * D_STATE
SSD_CHUNK = 128
DILATED_PAIRS = ((128, 1), (512, 4), (2048, 16))
MAX_WINDOW = 2048
D_FF = 4 * D_MODEL
D_PLE = 256
LN_EPS = 1e-5
DEEPNORM_ALPHA = (2 * DEPTH) ** 0.25
DEEPNORM_BETA = (8 * DEPTH) ** -0.25
D_IN_PROJ = 3 * D_ATTN + D_SSD + CONV_DIM + N_SSD_HEADS
IN_SPLITS = [D_ATTN, 2 * D_ATTN, 3 * D_ATTN, 3 * D_ATTN + D_SSD, 3 * D_ATTN + D_SSD + CONV_DIM]

kernel_name = "hymba_dilated_ssd_deepnorm_step"

def alibi_slopes(n_heads):
    return np.array([2.0 ** (-8.0 * (h + 1) / n_heads) for h in range(n_heads)], dtype=np.float32)

def layer_norm(x, g, b):
    xf = x.astype(jnp.float32)
    mu = jnp.mean(xf, -1, keepdims=True)
    var = jnp.mean(jnp.square(xf - mu), -1, keepdims=True)
    return ((xf - mu) * lax.rsqrt(var + LN_EPS) * g + b).astype(x.dtype)

def dilated_branch_prompt(q, k, v, window, dil, slopes):
    bsz, seq, nh, hd = q.shape
    nw = window // dil
    qb = nw
    sub = seq // dil
    nb = -(-sub // qb)
    lp = nb * qb

    def strided(t):
        t = t.reshape(bsz, sub, dil, nh, hd).transpose(0, 2, 1, 3, 4)
        return jnp.pad(t, ((0, 0), (0, 0), (0, lp - sub), (0, 0), (0, 0)))

    def band(t):
        prev = jnp.pad(t, ((0, 0), (0, 0), (qb, 0), (0, 0), (0, 0)))[:, :, :lp]
        return jnp.concatenate([prev.reshape(bsz, dil, nb, qb, nh, hd),
                                t.reshape(bsz, dil, nb, qb, nh, hd)], axis=3)

    qs, ks, vs = strided(q), strided(k), strided(v)
    qblk = qs.reshape(bsz, dil, nb, qb, nh, hd)
    kblk, vblk = band(ks), band(vs)
    scores = jnp.einsum('brnqhd,brnkhd->brnhqk', qblk, kblk).astype(jnp.float32) * (hd ** -0.5)
    dist = np.arange(qb)[:, None] - np.arange(2 * qb)[None, :] + qb
    key_sub = np.arange(nb)[:, None] * qb - qb + np.arange(2 * qb)[None, :]
    valid = ((dist >= 0) & (dist <= nw))[None] & (key_sub >= 0)[:, None, :]
    bias = -slopes[:, None, None] * (dist * dil).astype(np.float32)[None]
    scores = jnp.where(valid[None, None, :, None], scores + bias[None, None, None], -jnp.inf)
    m = jnp.max(scores, -1)
    e = jnp.exp(scores - m[..., None])
    s = jnp.sum(e, -1)
    acc = jnp.einsum('brnhqk,brnkhd->brnqhd', e, vblk.astype(jnp.float32))

    def unstride(t):
        t = t.reshape((bsz, dil, lp) + t.shape[4:])[:, :, :sub]
        t = jnp.moveaxis(t, 1, 2)
        return t.reshape((bsz, seq) + t.shape[3:])

    return unstride(acc), unstride(jnp.swapaxes(m, -1, -2)), unstride(jnp.swapaxes(s, -1, -2))

def dilated_branch_sample(q, kc, vc, window, dil, slopes, w_buf):
    t_new, hd = q.shape[1], q.shape[3]
    nw = window // dil
    i = np.arange(t_new)[:, None]
    back = np.arange(nw + 1)[None, :] * dil
    idx = w_buf + i - back
    valid = (PAST_LEN + i - back >= 0) & (idx >= 0)
    idx = np.clip(idx, 0, None)
    kg = kc[:, idx]
    vg = vc[:, idx]
    scores = jnp.einsum('bthd,btkhd->bhtk', q, kg).astype(jnp.float32) * (hd ** -0.5)
    bias = -slopes[:, None, None] * back.astype(np.float32)[None]
    scores = jnp.where(valid[None, None], scores + bias[None], -jnp.inf)
    m = jnp.max(scores, -1)
    e = jnp.exp(scores - m[..., None])
    s = jnp.sum(e, -1)
    acc = jnp.einsum('bhtk,btkhd->bthd', e, vg.astype(jnp.float32))
    return acc, jnp.swapaxes(m, 1, 2), jnp.swapaxes(s, 1, 2)

def combine_dilated(branches):
    m_max = functools.reduce(jnp.maximum, [m for _, m, _ in branches])
    scaled = [s * jnp.exp(m - m_max) for _, m, s in branches]
    total = functools.reduce(jnp.add, scaled)
    outs = [(sd / total)[..., None] * (acc / s[..., None])
            for (acc, _, s), sd in zip(branches, scaled)]
    return functools.reduce(jnp.add, outs)

def dilated_attention_prompt(q, k, v, slopes):
    return combine_dilated([dilated_branch_prompt(q, k, v, w, r, slopes) for (w, r) in DILATED_PAIRS])

def dilated_attention_sample(q, k, v, cache_k_l, cache_v_l, slopes):
    w_buf = cache_k_l.shape[1]
    kc = jnp.concatenate([cache_k_l.astype(k.dtype), k], axis=1)
    vc = jnp.concatenate([cache_v_l.astype(v.dtype), v], axis=1)
    return combine_dilated([dilated_branch_sample(q, kc, vc, w, r, slopes, w_buf) for (w, r) in DILATED_PAIRS])

def causal_dwconv(xpad, w, b):
    out = lax.conv_general_dilated(xpad, w[:, None, :], window_strides=(1,), padding='VALID',
                                   dimension_numbers=('NWC', 'WIO', 'NWC'),
                                   feature_group_count=xpad.shape[-1])
    return out + b

def segsum(a):
    t = a.shape[-1]
    x = jnp.broadcast_to(a[..., :, None], a.shape + (t,))
    x = jnp.where(np.tril(np.ones((t, t), dtype=bool), -1), x, 0.0)
    xs = jnp.cumsum(x, axis=-2)
    return jnp.where(np.tril(np.ones((t, t), dtype=bool)), xs, -jnp.inf)

def ssd_scan(xdt, adt, b, c, h0):
    n, seq, nh, hp = xdt.shape
    cl = min(SSD_CHUNK, seq)
    nc = -(-seq // cl)
    pad = nc * cl - seq
    padl = lambda t: jnp.pad(t, ((0, 0), (0, pad)) + ((0, 0),) * (t.ndim - 2))
    x = padl(xdt).reshape(n, nc, cl, nh, hp)
    a = padl(adt).reshape(n, nc, cl, nh).transpose(0, 3, 1, 2)
    bb = padl(b).reshape(n, nc, cl, nh, -1)
    cc = padl(c).reshape(n, nc, cl, nh, -1)
    a_cs = jnp.cumsum(a, axis=-1)
    lmat = jnp.exp(segsum(a))
    y_diag = jnp.einsum('bclhn,bcshn,bhcls,bcshp->bclhp', cc, bb, lmat, x)
    decay_states = jnp.exp(a_cs[..., -1:] - a_cs)
    states = jnp.einsum('bclhn,bhcl,bclhp->bchpn', bb, decay_states, x)
    states = jnp.concatenate([h0[:, None], states], axis=1)
    decay_chunk = jnp.exp(segsum(jnp.pad(a_cs[..., -1], ((0, 0), (0, 0), (1, 0)))))
    new_states = jnp.einsum('bhzc,bchpn->bzhpn', decay_chunk, states)
    states, h_final = new_states[:, :-1], new_states[:, -1]
    y_off = jnp.einsum('bclhn,bchpn,bhcl->bclhp', cc, states, jnp.exp(a_cs))
    y = (y_diag + y_off).reshape(n, nc * cl, nh, hp)[:, :seq]
    return y, h_final

def ssd_mixer(z, xbc, dt, conv_prev, h0, conv_w, conv_b, dt_bias, a_log, d_skip, norm_w):
    n, seq, _ = xbc.shape
    xpad = jnp.concatenate([conv_prev.astype(xbc.dtype), xbc], axis=1)
    conv_new = xpad[:, -(CONV_W - 1):]
    xbc_c = jax.nn.silu(causal_dwconv(xpad, conv_w, conv_b)).astype(jnp.float32)
    xs = xbc_c[..., :D_SSD].reshape(n, seq, N_SSD_HEADS, HEAD_DIM)
    bs = xbc_c[..., D_SSD:D_SSD + SSD_GROUPS * D_STATE].reshape(n, seq, SSD_GROUPS, D_STATE)
    cs = xbc_c[..., D_SSD + SSD_GROUPS * D_STATE:].reshape(n, seq, SSD_GROUPS, D_STATE)
    bs = jnp.repeat(bs, HEADS_PER_GROUP, axis=2)
    cs = jnp.repeat(cs, HEADS_PER_GROUP, axis=2)
    dt = jax.nn.softplus(dt.astype(jnp.float32) + dt_bias)
    a = -jnp.exp(a_log.astype(jnp.float32))
    y, h_new = ssd_scan(xs * dt[..., None], dt * a, bs, cs, h0.astype(jnp.float32))
    y = y + d_skip[:, None] * xs
    y = y.reshape(n, seq, D_SSD) * jax.nn.silu(z.astype(jnp.float32))
    yg = y.reshape(n, seq, SSD_GROUPS, D_SSD // SSD_GROUPS)
    yg = yg * lax.rsqrt(jnp.mean(jnp.square(yg), -1, keepdims=True) + LN_EPS)
    y = yg.reshape(n, seq, D_SSD) * norm_w
    return y.astype(z.dtype), conv_new, h_new.astype(h0.dtype)

def trunk_layer(x, pe, attend, conv_prev, ssm_prev, lw):
    (w_in, conv_w, conv_b, dt_bias, a_log, d_skip, ssd_norm_w, w_out,
     ln1_g, ln1_b, w_up, w_down, ln2_g, ln2_b, w_gate, w_ple, ln3_g, ln3_b) = lw
    n, seq, _ = x.shape
    proj = x @ w_in
    q, k, v, z, xbc, dt = jnp.split(proj, IN_SPLITS, axis=-1)
    heads = lambda t: t.reshape(n, seq, N_ATTN_HEADS, HEAD_DIM)
    q, k, v = heads(q), heads(k), heads(v)
    attn = attend(q, k, v).reshape(n, seq, D_ATTN).astype(x.dtype)
    ssd, conv_new, ssm_new = ssd_mixer(z, xbc, dt, conv_prev, ssm_prev, conv_w, conv_b,
                                       dt_bias, a_log, d_skip, ssd_norm_w)
    mix = jnp.concatenate([attn, ssd], axis=-1) @ w_out
    h = layer_norm(DEEPNORM_ALPHA * x + mix, ln1_g, ln1_b)
    u = jnp.square(jax.nn.relu(h @ w_up)) @ w_down
    h = layer_norm(DEEPNORM_ALPHA * h + u, ln2_g, ln2_b)
    g = jax.nn.sigmoid(h @ w_gate) * (pe @ w_ple)
    h = layer_norm(DEEPNORM_ALPHA * h + g, ln3_g, ln3_b)
    return h, k, v, conv_new, ssm_new

def setup_inputs(seed: int = 0) -> dict:
    key = jax.random.key(seed)
    ks = jax.random.split(key, 32)
    f32 = jnp.float32
    nrm = lambda kk, shape, scale: scale * jax.random.normal(kk, shape, f32)
    w_buf = min(MAX_WINDOW, PAST_LEN)
    dt0 = jnp.exp(jax.random.uniform(ks[8], (DEPTH, N_SSD_HEADS), f32, math.log(1e-3), math.log(1e-1)))
    return {
        "x_prompt": nrm(ks[0], (BATCH, SEQ, D_MODEL), 1.0),
        "x_sample": nrm(ks[1], (DEC_BATCH, DEC_SEQ, D_MODEL), 1.0),
        "cache_k": nrm(ks[2], (DEPTH, DEC_BATCH, w_buf, N_ATTN_HEADS, HEAD_DIM), 1.0),
        "cache_v": nrm(ks[3], (DEPTH, DEC_BATCH, w_buf, N_ATTN_HEADS, HEAD_DIM), 1.0),
        "state_conv": nrm(ks[4], (DEPTH, DEC_BATCH, CONV_W - 1, CONV_DIM), 1.0),
        "state_ssm": nrm(ks[5], (DEPTH, DEC_BATCH, N_SSD_HEADS, HEAD_DIM, D_STATE), 0.2),
        "p_prompt": nrm(ks[6], (DEPTH, BATCH, SEQ, D_PLE), 1.0),
        "p_sample": nrm(ks[7], (DEPTH, DEC_BATCH, DEC_SEQ, D_PLE), 1.0),
        "ln_in_g": 1.0 + nrm(ks[9], (D_MODEL,), 0.1),
        "ln_in_b": nrm(ks[10], (D_MODEL,), 0.02),
        "w_in": nrm(ks[11], (DEPTH, D_MODEL, D_IN_PROJ), D_MODEL ** -0.5),
        "conv_w": nrm(ks[12], (DEPTH, CONV_W, CONV_DIM), CONV_W ** -0.5),
        "conv_b": nrm(ks[13], (DEPTH, CONV_DIM), 0.02),
        "dt_bias": dt0 + jnp.log(-jnp.expm1(-dt0)),
        "a_log": jnp.log(jax.random.uniform(ks[14], (DEPTH, N_SSD_HEADS), f32, 1.0, 16.0)),
        "d_skip": 1.0 + nrm(ks[15], (DEPTH, N_SSD_HEADS), 0.1),
        "ssd_norm_w": 1.0 + nrm(ks[16], (DEPTH, D_SSD), 0.1),
        "w_out": nrm(ks[17], (DEPTH, D_MIX, D_MODEL), D_MIX ** -0.5 * DEEPNORM_BETA),
        "ln1_g": 1.0 + nrm(ks[18], (DEPTH, D_MODEL), 0.1),
        "ln1_b": nrm(ks[19], (DEPTH, D_MODEL), 0.02),
        "w_up": nrm(ks[20], (DEPTH, D_MODEL, D_FF), D_MODEL ** -0.5),
        "w_down": nrm(ks[21], (DEPTH, D_FF, D_MODEL), D_FF ** -0.5 * DEEPNORM_BETA),
        "ln2_g": 1.0 + nrm(ks[22], (DEPTH, D_MODEL), 0.1),
        "ln2_b": nrm(ks[23], (DEPTH, D_MODEL), 0.02),
        "w_gate": nrm(ks[24], (DEPTH, D_MODEL, D_MODEL), D_MODEL ** -0.5),
        "w_ple": nrm(ks[25], (DEPTH, D_PLE, D_MODEL), D_PLE ** -0.5 * DEEPNORM_BETA),
        "ln3_g": 1.0 + nrm(ks[26], (DEPTH, D_MODEL), 0.1),
        "ln3_b": nrm(ks[27], (DEPTH, D_MODEL), 0.02),
    }

def reference(x_prompt, x_sample, cache_k, cache_v, state_conv, state_ssm, p_prompt, p_sample,
              ln_in_g, ln_in_b, w_in, conv_w, conv_b, dt_bias, a_log, d_skip, ssd_norm_w, w_out,
              ln1_g, ln1_b, w_up, w_down, ln2_g, ln2_b, w_gate, w_ple, ln3_g, ln3_b):
    slopes = alibi_slopes(N_ATTN_HEADS)
    hp = layer_norm(x_prompt, ln_in_g, ln_in_b)
    hs = layer_norm(x_sample, ln_in_g, ln_in_b)
    kp_l, vp_l, ks_l, vs_l, cp_l, cs_l, sp_l, ss_l = [], [], [], [], [], [], [], []
    attend_prompt = functools.partial(dilated_attention_prompt, slopes=slopes)
    for i in range(DEPTH):
        lw = (w_in[i], conv_w[i], conv_b[i], dt_bias[i], a_log[i], d_skip[i], ssd_norm_w[i], w_out[i],
              ln1_g[i], ln1_b[i], w_up[i], w_down[i], ln2_g[i], ln2_b[i], w_gate[i], w_ple[i],
              ln3_g[i], ln3_b[i])
        nbp = hp.shape[0]
        conv0 = jnp.zeros((nbp, CONV_W - 1, CONV_DIM), hp.dtype)
        ssm0 = jnp.zeros((nbp, N_SSD_HEADS, HEAD_DIM, D_STATE), hp.dtype)
        hp, kp, vp, cp, sp = trunk_layer(hp, p_prompt[i], attend_prompt, conv0, ssm0, lw)
        attend_sample = functools.partial(dilated_attention_sample, cache_k_l=cache_k[i],
                                          cache_v_l=cache_v[i], slopes=slopes)
        hs, kn, vn, cn, sn = trunk_layer(hs, p_sample[i], attend_sample, state_conv[i], state_ssm[i], lw)
        keep = min(MAX_WINDOW, kp.shape[1])
        kp_l.append(kp[:, -keep:])
        vp_l.append(vp[:, -keep:])
        ks_l.append(kn)
        vs_l.append(vn)
        cp_l.append(cp)
        cs_l.append(cn)
        sp_l.append(sp)
        ss_l.append(sn)
    new_k_prompt = jnp.stack(kp_l)
    new_v_prompt = jnp.stack(vp_l)
    new_k_sample = jnp.stack(ks_l)
    new_v_sample = jnp.stack(vs_l)
    new_conv_prompt = jnp.stack(cp_l)
    new_conv_sample = jnp.stack(cs_l)
    new_ssm_prompt = jnp.stack(sp_l)
    new_ssm_sample = jnp.stack(ss_l)
    return (hp, hs, new_k_prompt, new_v_prompt, new_k_sample, new_v_sample,
            new_conv_prompt, new_conv_sample, new_ssm_prompt, new_ssm_sample)


_drawn_inputs = setup_inputs


def setup_inputs(seed=0):
    import zlib

    import numpy as np

    out = dict(_drawn_inputs(seed))
    spreads = {}
    factors = {'d_skip': 5.662, 'ln1_b': 2.81, 'ln2_b': 3.028, 'ln3_b': 3.135}
    for name, (base, spread) in spreads.items():
        noise = np.random.default_rng([zlib.crc32(name.encode()), seed]).standard_normal(out[name].shape)
        drawn = base * np.exp(spread * noise) if base else spread * noise
        out[name] = __import__('jax').numpy.asarray(drawn.astype(out[name].dtype))
    for name, factor in factors.items():
        out[name] = (out[name] * factor).astype(out[name].dtype)
    return out
```

```python
from contextlib import ExitStack

import concourse.bass as bass
import numpy as np
from concourse import mybir

F32 = mybir.dt.float32
F32R = mybir.dt.float32r
ALU = mybir.AluOpType
ACT = mybir.ActivationFunctionType
AX = mybir.AxisListType
ds = bass.ds

P = 128
D = 1024
KD = D // P
SEQ = 1024
NQB = SEQ // P
DB, DT = 8, 8
NS = DB * DT
TOK = SEQ + NS
NB = NQB + 1
PAST = 1024
HD = 64
NH = 8
DA = NH * HD
NPAIR = DA // P
NSTATE = 128
NGROUP = 2
HPG = NH // NGROUP
CW = 4
CD = DA + 2 * NGROUP * NSTATE
NXBC = CD // P
DIN = 3 * DA + DA + CD + NH
DFF = 4 * D
DPLE = 256
KPLE = DPLE // P
EPS = 1e-5
ALPHA = 2.0 ** 0.25
BRANCHES = ((128, 1), (512, 4), (2048, 16))
NEG = -1e30

GROUPS = [(0, 364), (364, 364), (728, 360)]

SBUF_START = 16512


class Place:

    def __init__(self, nc, offset, limit=None, then=None):
        self.nc, self.offset, self.limit, self.then = nc, offset, limit, then

    def __call__(self, name, shape, dtype=F32):
        size = 4 * int(np.prod(shape[1:]))
        if self.limit is not None and self.offset + size > self.limit:
            self.offset, self.limit = self.then, None
        t = self.nc.alloc_sbuf_tensor_at(name, list(shape), dtype, offset=self.offset)
        self.offset += -(-size // 32) * 32
        return t


def take_statistics(dve, out, last_count, done, value):
    dve.wait_ge(done, value)
    dve.tensor_copy(out, last_count)


def w_raw_view(w, col, n):
    return w[:, ds(col, n)].rearrange("(k p) n -> p k n", p=P)


def stage_input_norm(nc, sem, io, ident, hT_hi, hT_lo, place):
    X = place("in_x", [P, 2, D])
    H = place("in_h", [P, 2, D])
    G = place("in_g", [P, D])
    B = place("in_b", [P, D])
    stats = place("in_stats", [P, 2, 2, 6])
    mv = place("in_mv", [P, 2, 2])
    veps = place("in_veps", [P, 2, 1])
    rstd = place("in_rstd", [P, 2, 1])
    nmr = place("in_nmr", [P, 2, 1])
    mhalf, eps, taken = place("in_mhalf", [P, 1]), place("in_eps", [P, 1]), place("in_taken", [P, 1])
    g_loaded, b_loaded, const_set = sem("in_g_loaded"), sem("in_b_loaded"), sem("in_const_set")
    x_loaded = [sem(f"in_x_loaded{s}") for s in range(2)]
    stored = [sem(f"in_stored{s}") for s in range(2)]
    stats_done = [sem(f"in_stats_done{s}") for s in range(2)]
    aggr_done = [sem(f"in_aggr_done{s}") for s in range(2)]
    veps_done = [sem(f"in_veps_done{s}") for s in range(2)]
    rstd_done = [sem(f"in_rstd_done{s}") for s in range(2)]
    nmr_done = [sem(f"in_nmr_done{s}") for s in range(2)]
    xn_done = [sem(f"in_xn_done{s}") for s in range(2)]
    gain_done = [sem(f"in_gain_done{s}") for s in range(2)]
    h_done = [sem(f"in_h_done{s}") for s in range(2)]
    t_done = [sem(f"in_t_done{s}") for s in range(2)]
    hi_done = [sem(f"in_hi_done{s}") for s in range(2)]
    lo_done = [sem(f"in_lo_done{s}") for s in range(2)]
    h0 = io["h0"]
    with ExitStack() as ctx:
        T = ctx.enter_context(nc.psum_tensor("in_T", [P, 2, KD, P], F32))
        block = ctx.enter_context(nc.Block())

        @block.sync
        def _(sp):
            def load(src, s, i, rows):
                sp.wait_ge(xn_done[s], i)
                sp.dma_start(X[0:rows, s, :], src).then_inc(x_loaded[s], 16)

            def store(row, s, i, rows):
                sp.wait_ge(h_done[s], i + 1)
                sp.dma_start(h0[ds(row, rows), :], H[0:rows, s, :]).then_inc(stored[s], 16)

            x = io["x_prompt"]
            load(x[0:P, :], 0, 0, P)
            load(x[P:2 * P, :], 1, 0, P)
            sp.dma_start(G[:, :], io["ln_in_g"].partition_broadcast(P)).then_inc(g_loaded, 16)
            sp.dma_start(B[:, :], io["ln_in_b"].partition_broadcast(P)).then_inc(b_loaded, 16)
            with sp.Fori(0, NQB // 2 - 1) as i:
                for s in range(2):
                    load(x[ds(i * (2 * P) + (2 + s) * P, P), :], s, i + 1, P)
                    store(i * (2 * P) + s * P, s, i, P)
            load(io["x_sample"], 0, NQB // 2, NS)
            for s in range(2):
                store(SEQ - 2 * P + s * P, s, NQB // 2 - 1, P)
            store(SEQ, 0, NQB // 2, NS)
            sp.wait_ge(stored[0], 16 * (NQB // 2 + 1))
            sp.wait_ge(stored[1], 16 * (NQB // 2))

        def pipelined(engine, front, back):
            half = NQB // 2
            front(0, 0, P)
            with engine.Fori(0, half - 1) as i:
                front(1, i, P)
                back(0, i, P, i * (2 * P))
                front(0, i + 1, P)
                back(1, i, P, i * (2 * P) + P)
            front(1, half - 1, P)
            back(0, half - 1, P, SEQ - 2 * P)
            front(0, half, NS)
            back(1, half - 1, P, SEQ - P)
            back(0, half, NS, SEQ)

        @block.gpsimd
        def _(pool):
            pool.memset(mhalf[:, :], -0.5).then_inc(const_set, 1)
            pool.memset(eps[:, :], EPS).then_inc(const_set, 1)
            pool.wait_ge(const_set, 2)

            def front(s, i, r):
                pool.wait_ge(aggr_done[s], i + 1)
                pool.tensor_tensor(veps[0:r, s, :], mv[0:r, s, 1:2], eps[0:r, :], ALU.add).then_inc(veps_done[s], 1)
                pool.wait_ge(veps_done[s], i + 1)
                pool.tensor_tensor(rstd[0:r, s, :], veps[0:r, s, :], mhalf[0:r, :], ALU.pow).then_inc(rstd_done[s], 1)

            pipelined(pool, front, lambda *a: None)

        @block.vector
        def _(dve):
            dve.wait_ge(g_loaded, 16)
            dve.wait_ge(b_loaded, 16)

            def front(s, i, r):
                dve.wait_ge(x_loaded[s], 16 * (i + 1))
                dve.bn_stats(stats[0:r, s, 0, :], X[0:r, s, 0:512])
                dve.bn_stats(stats[0:r, s, 1, :], X[0:r, s, 512:D]).then_inc(stats_done[s], 1)
                take_statistics(dve, taken[0:r, :], stats[0:r, s, 1, 0:1], stats_done[s], i + 1)
                dve.bn_aggr(mv[0:r, s, :], stats[0:r, s, :, :]).then_inc(aggr_done[s], 1)
                dve.wait_ge(rstd_done[s], i + 1)
                dve.tensor_scalar(nmr[0:r, s, :], mv[0:r, s, 0:1], rstd[0:r, s, :], -1.0, ALU.mult,
                                  ALU.mult).then_inc(nmr_done[s], 1)

            def back(s, i, r, col):
                dve.wait_ge(xn_done[s], i + 1)
                dve.tensor_tensor(H[0:r, s, :], H[0:r, s, :], G[0:r, :], ALU.mult).then_inc(gain_done[s], 1)
                dve.wait_ge(gain_done[s], i + 1)
                dve.tensor_tensor(H[0:r, s, :], H[0:r, s, :], B[0:r, :], ALU.add).then_inc(h_done[s], 1)
                dve.wait_ge(hi_done[s], i + 1)
                dve.tensor_tensor(hT_lo[:, :, ds(col, r)], T[:, s, :, 0:r],
                                  hT_hi[:, :, ds(col, r)].bitcast(F32), ALU.subtract).then_inc(lo_done[s], 1)

            pipelined(dve, front, back)

        @block.scalar
        def _(act):
            def front(s, i, r):
                act.wait_ge(nmr_done[s], i + 1)
                act.wait_ge(t_done[s], i)
                act.wait_ge(stored[s], 16 * i)
                act.activation(H[0:r, s, :], X[0:r, s, :], ACT.Identity, bias=nmr[0:r, s, :],
                               scale=rstd[0:r, s, :]).then_inc(xn_done[s], 1)

            def back(s, i, r, col):
                act.wait_ge(t_done[s], i + 1)
                act.activation(hT_hi[:, :, ds(col, r)], T[:, s, :, 0:r], ACT.Copy).then_inc(hi_done[s], 1)

            pipelined(act, front, back)

        @block.tensor
        def _(pe):
            def back(s, i, r, col):
                pe.wait_ge(h_done[s], i + 1)
                pe.wait_ge(lo_done[s], i)
                for k in range(KD):
                    last = pe.transpose(T[:, s, k, 0:r], H[0:r, s, k * P:(k + 1) * P], ident[0:r, 0:r])
                last.then_inc(t_done[s], 1)

            pipelined(pe, lambda *a: None, back)
def stage_projection(nc, sem, io, ident, hT_hi, hT_lo, qT, kT, Xt, Bt, BT, CT, dt_raw, place):
    KINDS = ["dt"] + ["q"] * 4 + ["k"] * 4 + ["v"] * 4 + ["z"] * 4 + ["x"] * 4 + ["B"] * 2 + ["C"] * 2
    NBLK = len(KINDS)
    TURNED = ("dt", "k", "v", "z", "x", "B")
    STORED = ("k", "v", "z")
    CONV = ("x", "B", "C")
    COPIED = ("k", "B")
    LAST = CW - 1
    TAIL = LAST * (1 + DB)

    def column(n):
        return DIN - P if n == 0 else (n - 1) * P

    def before(n, kinds):
        return sum(KINDS[m] in kinds for m in range(n % 2, n, 2))

    def turned_before(n):
        return sum(KINDS[m] in TURNED for m in range(n))

    raw = place("pj_raw", [P, 2, KD, P])
    w_hi = [place(f"pj_w_hi{s}", [P, KD, P], F32R) for s in range(2)]
    w_lo = [place(f"pj_w_lo{s}", [P, KD, P], F32R) for s in range(2)]
    fT = place("pj_fT", [P, 2, TOK])
    SX = LAST + SEQ
    cv = place("pj_cv", [P, 2, SX + DB * (LAST + DT)])
    cc = place("pj_cc", [P, 2, TOK])
    stage = place("pj_stage", [P, 2, NB, P])
    conv_w = place("pj_conv_w", [P, NXBC, CW])
    conv_b = place("pj_conv_b", [P, NXBC])
    stateT = place("pj_stateT", [P, NXBC, DB * LAST])
    tail = place("pj_tail", [P, NXBC, TAIL])

    small_loaded, tail_stored, tcopy_done = sem("pj_small_loaded"), sem("pj_tail_stored"), sem("pj_tcopy_done")
    pad_set, v_chain = sem("pj_pad_set"), sem("pj_v_chain")
    two = lambda name: [sem(f"pj_{name}{s}") for s in range(2)]
    loaded, hi_done, lo_done, mm_done, ev_done = two("loaded"), two("hi_done"), two("lo_done"), two("mm_done"), two("ev_done")
    t_done, stored, kept, conv_done, silu_done = two("t_done"), two("stored"), two("kept"), two("conv_done"), two("silu_done")
    tail_done, fill_done, tap = two("tail_done"), two("fill_done"), two("tap")

    def sample_view(ap, width):
        return ap.rearrange("p (b t) -> p b t", t=width)

    with ExitStack() as ctx:
        mm = ctx.enter_context(nc.psum_tensor("pj_mm", [P, 2, 3, 512], F32))
        T = ctx.enter_context(nc.psum_tensor("pj_T", [P, NQB, P], F32))
        Ts = [mm[0:NS, s, 2, 384:384 + P] for s in range(2)]
        block = ctx.enter_context(nc.Block())

        def steps(engine, step):
            n = 0
            while n < NBLK:
                if KINDS[n:n + 4] == [KINDS[n]] * 4:
                    with engine.Fori(0, 2) as i:
                        for u in range(2):
                            step(n + u, i, i * 2 + u)
                    n += 4
                else:
                    step(n, 0, n - KINDS.index(KINDS[n]))
                    n += 1

        @block.sync
        def _(sp):
            def load(n, i, ahead=0):
                m = n + ahead
                s = m % 2
                sp.wait_ge(lo_done[s], i + m // 2)
                col = column(m) if m == 0 else i * (2 * P) + column(m)
                sp.dma_start(raw[:, s, :, :], w_raw_view(io["w_in"], col, P)).then_inc(loaded[s], 16)

            load(0, 0)
            load(1, 0)
            sp.dma_start(conv_w[:, :, :], io["conv_wT"]).then_inc(small_loaded, 16)
            sp.dma_start(conv_b[:, :], io["conv_bT"]).then_inc(small_loaded, 16)
            sp.dma_start(stateT[:, :, :], io["state_convT"]).then_inc(small_loaded, 16)
            load(2, 0)

            def step(n, i, j):
                if n + 3 < NBLK:
                    load(n, i, 3)
                if KINDS[n] in STORED:
                    s = n % 2
                    to = io[{"k": "new_k", "v": "new_v", "z": "z_act"}[KINDS[n]]]
                    sp.wait_ge(tcopy_done, i * 2 + (turned_before(n) + 1))
                    sp.dma_start(to[0:SEQ, ds(j * P, P)].rearrange("(b p) f -> p b f", p=P),
                                 stage[:, s, 0:NQB, :]).then_inc(stored[s], 16)
                    sp.dma_start(to[SEQ:TOK, ds(j * P, P)], stage[0:NS, s, NQB, :]).then_inc(stored[s], 16)

            steps(sp, step)
            for s in range(2):
                sp.wait_ge(tail_done[s], NXBC // 2)
            sp.dma_start(io["new_convT"], tail[:, :, :]).then_inc(tail_stored, 16)
            sp.wait_ge(tail_stored, 16)
            for s in range(2):
                sp.wait_ge(stored[s], 32 * (len([k for k in KINDS if k in STORED]) // 2))

        @block.scalar
        def _(act):
            def split(n, i, ahead=0):
                m = n + ahead
                s = m % 2
                act.wait_ge(loaded[s], i * 16 + 16 * (m // 2 + 1))
                act.wait_ge(mm_done[s], i + m // 2)
                act.activation(w_hi[s][:, :, :], raw[:, s, :, :], ACT.Copy).then_inc(hi_done[s], 1)

            def step(n, i, j):
                s, kind = n % 2, KINDS[n]
                if n + 2 < NBLK:
                    split(n, i, 2)
                act.wait_ge(mm_done[s], i + (n // 2 + 1))
                fT_free = kind in TURNED
                if kind in CONV:
                    act.wait_ge(conv_done[s], i + before(n, CONV))
                    act.wait_ge(tail_done[s], i + before(n, CONV))
                elif fT_free:
                    act.wait_ge(t_done[s], i + before(n, TURNED))
                    act.wait_ge(kept[s], i + before(n, COPIED) if kind == "k" else before(n, COPIED))
                for g, (c, w) in enumerate(GROUPS):
                    w_prompt = min(w, SEQ - c)
                    if kind in CONV:
                        last = act.activation(cv[:, s, LAST + c:LAST + c + w_prompt], mm[:, s, g, 0:w_prompt], ACT.Copy)
                        if w_prompt < w:
                            last = act.activation(sample_view(cv[:, s, SX:], LAST + DT)[:, :, LAST:],
                                                  sample_view(mm[:, s, g, w_prompt:w], DT), ACT.Copy)
                    else:
                        to = qT[:, ds(j, 1), c:c + w].squeeze(1) if kind == "q" else fT[:, s, c:c + w]
                        last = act.activation(to, mm[:, s, g, 0:w], ACT.Copy)
                last.then_inc(ev_done[s], 1)
                if kind == "z":
                    act.wait_ge(t_done[s], i + (before(n, TURNED) + 1))
                    act.wait_ge(stored[s], i * 32 + 32 * before(n, STORED))
                    act.activation(stage[:, s, 0:NQB, :], T[:, :, :], ACT.Silu)
                    act.activation(stage[0:NS, s, NQB, :], Ts[s], ACT.Silu).then_inc(tcopy_done, 1)
                if kind in CONV:
                    act.wait_ge(conv_done[s], i + (before(n, CONV) + 1))
                    if kind != "C":
                        act.wait_ge(t_done[s], i + before(n, TURNED))
                        act.wait_ge(kept[s], before(n, COPIED))
                    to = CT[:, j, :] if kind == "C" else fT[:, s, :]
                    act.activation(to, cc[:, s, :], ACT.Silu).then_inc(silu_done[s], 1)

            split(0, 0)
            split(1, 0)
            steps(act, step)

        @block.gpsimd
        def _(pool):
            for s in range(2):
                pool.memset(cv[:, s, 0:LAST], 0.0).then_inc(pad_set, 1)
            pool.wait_ge(small_loaded, 48)

            def step(n, i, j):
                s, kind = n % 2, KINDS[n]
                if kind in CONV:
                    jx = n + 2 * 0 - KINDS.index("x")
                    jx = j if kind == "x" else jx
                    pool.wait_ge(conv_done[s], i + before(n, CONV))
                    pool.tensor_copy(sample_view(cv[:, s, SX:], LAST + DT)[:, :, 0:LAST],
                                     sample_view(stateT[:, ds(jx, 1), :].squeeze(1), LAST)).then_inc(fill_done[s], 1)
                    pool.wait_ge(ev_done[s], i + (n // 2 + 1))
                    pool.tensor_copy(tail[:, ds(jx, 1), 0:LAST].squeeze(1), cv[:, s, SEQ:SEQ + LAST])
                    pool.tensor_copy(sample_view(tail[:, ds(jx, 1), LAST:].squeeze(1), LAST),
                                     sample_view(cv[:, s, SX:], LAST + DT)[:, :, DT:]).then_inc(tail_done[s], 1)
                if kind == "k":
                    pool.wait_ge(ev_done[s], i + (n // 2 + 1))
                    pool.tensor_copy(kT[:, ds(j, 1), :].squeeze(1), fT[:, s, :]).then_inc(kept[s], 1)
                if kind == "B":
                    pool.wait_ge(silu_done[s], before(n, CONV) + 1)
                    pool.tensor_copy(BT[:, j, :], fT[:, s, :]).then_inc(kept[s], 1)

            steps(pool, step)

        @block.vector
        def _(dve):
            def split(n, i, ahead=0):
                m = n + ahead
                s = m % 2
                dve.wait_ge(hi_done[s], i + (m // 2 + 1))
                dve.tensor_tensor(w_lo[s][:, :, :], raw[:, s, :, :], w_hi[s][:, :, :].bitcast(F32),
                                  ALU.subtract).then_inc(lo_done[s], 1)

            def step(n, i, j):
                s, kind = n % 2, KINDS[n]
                if n + 2 < NBLK:
                    split(n, i, 2)
                if kind in CONV:
                    jx = j if kind == "x" else n - KINDS.index("x")
                    dve.wait_ge(ev_done[s], i + (n // 2 + 1))
                    dve.wait_ge(fill_done[s], i + (before(n, CONV) + 1))
                    dve.wait_ge(silu_done[s], i + before(n, CONV))
                    base = i * LAST + LAST * before(n, CONV)
                    for t in range(CW):
                        cw = conv_w[:, ds(jx, 1), t:t + 1].squeeze(1)
                        src = cv[:, s, t:t + SEQ]
                        src_s = sample_view(cv[:, s, SX:], LAST + DT)[:, :, t:t + DT]
                        out, out_s = cc[:, s, 0:SEQ], sample_view(cc[:, s, SEQ:], DT)
                        if t == 0:
                            cb = conv_b[:, ds(jx, 1)]
                            dve.tensor_scalar(out, src, cw, cb, ALU.mult, ALU.add)
                            dve.tensor_scalar(out_s, src_s, cw, cb, ALU.mult, ALU.add).then_inc(tap[s], 1)
                        else:
                            dve.wait_ge(tap[s], base + t)
                            dve.scalar_tensor_tensor(out, src, cw, out, ALU.mult, ALU.add)
                            last = dve.scalar_tensor_tensor(out_s, src_s, cw, out_s, ALU.mult, ALU.add)
                            last.then_inc(tap[s] if t < CW - 1 else conv_done[s], 1)
                if kind in TURNED and kind != "z":
                    dve.wait_ge(t_done[s], i + (before(n, TURNED) + 1))
                    if kind in STORED:
                        dve.wait_ge(stored[s], i * 32 + 32 * before(n, STORED))
                        to, to_s = stage[:, s, 0:NQB, :], stage[0:NS, s, NQB, :]
                    elif kind == "x":
                        to = Xt[:, 0:NQB, ds(j * P, P)]
                        to_s = Xt[0:NS, NQB, ds(j * P, P)]
                    elif kind == "B":
                        to, to_s = Bt[:, 0:NQB, j * P:(j + 1) * P], Bt[0:NS, NQB, j * P:(j + 1) * P]
                    else:
                        to, to_s = dt_raw[:, 0:NQB, :], dt_raw[0:NS, NQB, :]
                    c = P - NH if kind == "dt" else 0
                    dve.tensor_copy(to, T[:, :, c:])
                    dve.tensor_copy(to_s, Ts[s][:, c:]).then_inc(tcopy_done, 1)

            dve.wait_ge(small_loaded, 48)
            dve.wait_ge(pad_set, 2)
            split(0, 0)
            split(1, 0)
            steps(dve, step)

        @block.tensor
        def _(pe):
            def product(n, i, turned=0):
                s = n % 2
                pe.wait_ge(lo_done[s], i + (n // 2 + 1))
                pe.wait_ge(ev_done[s], i + n // 2)
                for g, (c, w) in enumerate(GROUPS):
                    if g == len(GROUPS) - 1:
                        pe.wait_ge(tcopy_done, turned)
                    for k in range(KD):
                        for part, (wt, ht) in enumerate(((w_hi, hT_hi), (w_hi, hT_lo), (w_lo, hT_hi))):
                            last = pe.matmul(mm[:, s, g, 0:w], wt[s][:, k, :], ht[:, k, c:c + w],
                                             start=(k == 0 and part == 0), stop=(k == KD - 1 and part == 2))
                last.then_inc(mm_done[s], 1)

            def step(n, i, j):
                s, kind = n % 2, KINDS[n]
                if n + 1 < NBLK:
                    product(n + 1, i, turned_before(n) + (i * 2 if kind in TURNED and not isinstance(i, int) else 0))
                if kind in TURNED:
                    if kind in CONV:
                        pe.wait_ge(silu_done[s], i + (before(n, CONV) + 1))
                    else:
                        pe.wait_ge(ev_done[s], i + (n // 2 + 1))
                    pe.wait_ge(tcopy_done, i * 2 + turned_before(n))
                    for b in range(NQB):
                        pe.transpose(T[:, b, :], fT[:, s, b * P:(b + 1) * P], ident[:, :])
                    pe.transpose(Ts[s], fT[:, s, SEQ:TOK], ident[:, :]).then_inc(t_done[s], 1)

            product(0, 0)
            steps(pe, step)
def stage_ssd(nc, sem, io, consts, Xt, Bt, BT, CT, dt_raw, mixT, place):
    ident = consts["ident"]
    GW = DA // NGROUP
    C_ALL = NB * NH
    PC = NQB * NH

    def sb(name, shape):
        return place("sd_" + name, shape)

    ones, mask, mask_s, ones_s, in_seq = (sb("ones", [P, P]), sb("mask", [P, P]), sb("mask_s", [NS, NS]),
                                          sb("ones_s", [NS, NS]), sb("in_seq", [NS, DB]))
    tri, tri_s = sb("tri", [P, P]), sb("tri_s", [NS, NS])
    bias, a_log, skip, norm_w = sb("bias", [P, NH]), sb("a_log", [P, NH]), sb("skip", [P, NH]), sb("norm_w", [P, DA])
    d, ab, ex, dt, adt, ea = (sb(n, [P, C_ALL]) for n in ("d", "ab", "ex", "dt", "adt", "ea"))
    acs, rest, decay, eacs, etot = (sb(n, [P, C_ALL]) for n in ("acs", "rest", "decay", "eacs", "etot"))
    adt_b, etot_s = sb("adt_b", [NS, DB, NH]), sb("etot_s", [P, DB * NH])
    mhalf = sb("mhalf", [P, NGROUP])
    state = sb("state", [P, DA])
    state_s = sb("state_s", [P, DB, DA])
    E = sb("E", [P, 2, NH, P])
    xdt, xdd, xsk, zt, Y = (sb(n, [P, 2, DA]) for n in ("xdt", "xdd", "xsk", "zt", "Y"))
    off, junk, off_junk = sb("off", [P, DA]), sb("junk", [P, GW]), sb("junk2", [P, GW])
    BTs, CTs, Bts = (sb(n, [P, 2, NGROUP, P]) for n in ("BTs", "CTs", "Bts"))
    adts = sb("adts", [P, 2, NH])
    Cz = sb("Cz", [P, NGROUP, DB * (NS + DT)])
    Bz = sb("Bz", [NS, DB, GW])
    ssq, ms, rs = sb("ssq", [P, 2, NGROUP]), sb("ms", [P, 2, NGROUP]), sb("rs", [P, 2, NGROUP])

    names = ("loaded zeroed pad_set pre adt_ready sums_done acs_ready decay_ready cz_ready bz_ready staged x_ready gr_done z_done "
             "e_done m_done y_mm o_mm s_mm off_done st_scaled st_done y1_done xsk_done y2_done y3_done ssq_done "
             "ms_done rs_done yn_done yw_done t_mm ty_done st_out").split()
    S = {n: sem("sd_" + n) for n in names}
    z_loaded = [sem(f"sd_z_loaded{s}") for s in range(2)]
    heads = lambda ap: ap.rearrange("p (h f) -> p h f", f=HD)

    def chunk_cols(t, c):
        return t[:, c * NH:(c + 1) * NH] if isinstance(c, int) else t[:, ds(c * NH, NH)]

    def per_head(ap, r):
        return ap[0:r].unsqueeze(2).to_broadcast([r, NH, HD])

    def wait(engine, name, value):
        if not isinstance(value, int) or value > 0:
            engine.wait_ge(S[name], value)

    def steps(front, back, turn):
        front(0, 0)
        front(1, 1)
        back(0, 0)

        def body(i):
            for u in range(2):
                front(i * 2 + (2 + u), u)
                back(i * 2 + (1 + u), 1 - u)
                turn(i * 2 + u, u)
        return body, lambda: (back(NQB - 1, 1), turn(NQB - 2, 0), turn(NQB - 1, 1))

    def run(engine, front, back, turn):
        body, end = steps(front, back, turn)
        with engine.Fori(0, NQB // 2 - 1) as i:
            body(i)
        end()
        front(NQB, 0)
        back(NQB, 0)
        turn(NQB, 0)

    nothing = lambda *a: None
    is_sample = lambda c: isinstance(c, int) and c == NQB

    with ExitStack() as ctx:
        G = [ctx.enter_context(nc.psum_tensor(f"sd_G{s}", [P, NGROUP, P], F32)) for s in range(2)]
        R = ctx.enter_context(nc.psum_tensor("sd_R", [P, NH, P], F32))
        pY = ctx.enter_context(nc.psum_tensor("sd_pY", [P, DA], F32))
        pO = ctx.enter_context(nc.psum_tensor("sd_pO", [P, DA], F32))
        pS = ctx.enter_context(nc.psum_tensor("sd_pS", [P, DA], F32))
        pT = ctx.enter_context(nc.psum_tensor("sd_pT", [P, NPAIR, P], F32))
        block = ctx.enter_context(nc.Block())

        @block.sync
        def _(sp):
            loads = [(ones, consts["ones_d"]), (mask, consts["mask_d"]), (mask_s, consts["mask_s_d"]),
                     (ones_s, consts["ones_s_d"]), (in_seq, consts["in_seq_d"]), (tri, consts["tri_d"]),
                     (tri_s, consts["tri_s_d"])]
            for t, src in loads:
                sp.dma_start(t[:, :], src).then_inc(S["loaded"], 16)
            for t, name in ((bias, "dt_bias"), (a_log, "a_log"), (skip, "d_skip"), (norm_w, "ssd_norm_w")):
                sp.dma_start(t[:, :], io[name].partition_broadcast(P)).then_inc(S["loaded"], 16)
            sp.dma_start(state_s[:, :, :], io["state_ssmT"]).then_inc(S["loaded"], 16)

            def front(c, s):
                wait(sp, "y3_done", c - 1)
                rows = NS if is_sample(c) else P
                sp.dma_start(zt[0:rows, s, :], io["z_act"][ds(c * P, rows), :]).then_inc(z_loaded[s], 16)

            run(sp, front, nothing, nothing)
            wait(sp, "st_done", NQB)
            sp.dma_start(io["new_ssm_promptT"], state[:, :]).then_inc(S["st_out"], 16)
            wait(sp, "st_done", NQB + DB)
            sp.dma_start(io["new_ssm_sampleT"], state_s[:, :, :]).then_inc(S["st_out"], 16)
            wait(sp, "st_out", 32)

        @block.gpsimd
        def _(pool):
            pool.memset(mhalf[:, :], -0.5).then_inc(S["pad_set"], 1)
            pool.memset(state[:, :], 0.0).then_inc(S["zeroed"], 1)
            pool.memset(Cz[:, :, :], 0.0).then_inc(S["pad_set"], 1)
            wait(pool, "pad_set", 3)
            for g in range(NGROUP):
                last = pool.tensor_copy(Cz[:, g, :].rearrange("p (b t) -> p b t", t=NS + DT)[:, :, 0:DT],
                                        CT[:, g, SEQ:TOK].rearrange("p (b t) -> p b t", t=DT))
            last.then_inc(S["cz_ready"], 1)
            wait(pool, "loaded", 192)

            def front(c, s):
                if is_sample(c):
                    return
                wait(pool, "s_mm", c - 1)
                wait(pool, "adt_ready", 1)
                pool.tensor_copy(BTs[:, s, :, :], BT[:, :, ds(c * P, P)])
                pool.tensor_copy(CTs[:, s, :, :], CT[:, :, ds(c * P, P)])
                pool.tensor_copy(Bts[:, s, :, :], Bt[:, ds(c, 1), :].squeeze(1).rearrange("p (g n) -> p g n", n=P))
                pool.tensor_copy(adts[:, s, :], chunk_cols(adt, c)).then_inc(S["staged"], 1)

            def back(c, s):
                r = NS if is_sample(c) else P
                x = Xt[0:r, ds(c, 1), :].squeeze(1)
                wait(pool, "y2_done", c - 1)
                pool.tensor_tensor(heads(xsk[0:r, s, :]), heads(x), per_head(skip, r), ALU.mult).then_inc(S["xsk_done"], 1)

            def gate(c, s):
                r = NS if is_sample(c) else P
                wait(pool, "y1_done", c + 1)
                wait(pool, "xsk_done", c + 1)
                pool.tensor_tensor(Y[0:r, s, :], Y[0:r, s, :], xsk[0:r, s, :], ALU.add).then_inc(S["y2_done"], 1)
                wait(pool, "y2_done", c + 1)
                pool.wait_ge(z_loaded[s], 16 + 16 * (NQB // 2) if is_sample(c) else 16 * (c // 2 + 1) if isinstance(c, int)
                             else (c - s) * 8 + 16)
                pool.tensor_tensor(Y[0:r, s, :], Y[0:r, s, :], zt[0:r, s, :], ALU.mult).then_inc(S["y3_done"], 1)
                wait(pool, "pad_set", 3)
                wait(pool, "ssq_done", c + 1)
                pool.tensor_scalar(ms[0:r, s, :], ssq[0:r, s, :], 1.0 / GW, EPS, ALU.mult, ALU.add).then_inc(S["ms_done"], 1)
                wait(pool, "ms_done", c + 1)
                pool.tensor_tensor(rs[0:r, s, :], ms[0:r, s, :], mhalf[0:r, :], ALU.pow).then_inc(S["rs_done"], 1)
                wait(pool, "yn_done", c + 1)
                pool.tensor_tensor(Y[0:r, s, :], Y[0:r, s, :], norm_w[0:r, :], ALU.mult).then_inc(S["yw_done"], 1)

            run(pool, front, back, gate)

        @block.vector
        def _(dve):
            dve.memset(dt_raw[NS:P, NQB, :], 0.0).then_inc(S["pad_set"], 1)
            wait(dve, "loaded", 192)
            wait(dve, "pad_set", 3)
            by_chunk = lambda t: t[:, :].rearrange("p (c h) -> p c h", h=NH)
            over_chunks = lambda t: t[:, 0:NH].unsqueeze(1).to_broadcast([P, NB, NH])
            dve.tensor_tensor(by_chunk(d), dt_raw[:, :, :], over_chunks(bias), ALU.add).then_inc(S["pre"], 1)
            wait(dve, "pre", 5)
            dve.scalar_tensor_tensor(dt[:, :], d[:, :], 0.0, ex[:, :], ALU.max, ALU.add).then_inc(S["pre"], 1)
            wait(dve, "pre", 6)
            dve.scalar_tensor_tensor(by_chunk(adt), by_chunk(dt), -1.0, over_chunks(ea), ALU.mult,
                                     ALU.mult).then_inc(S["adt_ready"], 1)
            wait(dve, "adt_ready", 1)
            dve.tensor_tensor(adt_b[:, :, :], adt[0:NS, PC:].unsqueeze(1).to_broadcast([NS, DB, NH]),
                              in_seq[:, :].unsqueeze(2).to_broadcast([NS, DB, NH]), ALU.mult).then_inc(S["adt_ready"], 1)
            for b in range(DB):
                last = dve.tensor_scalar(Bz[:, b, :], Bt[0:NS, NQB, :], in_seq[:, b:b + 1], None, ALU.mult)
            last.then_inc(S["bz_ready"], 1)
            wait(dve, "sums_done", 1)
            dve.tensor_copy(acs[:, 0:PC], pY[:, 0:PC])
            dve.tensor_copy(acs[0:NS, PC:], pY[0:NS, PC:C_ALL]).then_inc(S["acs_ready"], 1)
            wait(dve, "acs_ready", 1)
            dve.tensor_tensor(rest[:, 0:PC], pO[:, 0:PC], acs[:, 0:PC], ALU.subtract)
            dve.tensor_tensor(rest[0:NS, PC:], pO[0:NS, PC:C_ALL], acs[0:NS, PC:], ALU.subtract).then_inc(S["acs_ready"], 1)

            def front(c, s):
                r = NS if is_sample(c) else P
                wait(dve, "decay_ready", 1)
                wait(dve, "s_mm", c - 1)
                x = Xt[0:r, ds(c, 1), :].squeeze(1)
                dve.tensor_tensor(heads(xdt[0:r, s, :]), heads(x), per_head(chunk_cols(dt, c), r),
                                  ALU.mult).then_inc(S["x_ready"], 1)
                dve.wait_ge(S["x_ready"], c * 2 + 1)
                dve.tensor_tensor(heads(xdd[0:r, s, :]), heads(xdt[0:r, s, :]), per_head(chunk_cols(decay, c), r),
                                  ALU.mult).then_inc(S["x_ready"], 1)
                wait(dve, "gr_done", c + 1)
                m = mask_s if is_sample(c) else mask
                for h in range(NH):
                    last = dve.scalar_tensor_tensor(E[0:r, s, h, 0:r], R[0:r, h, 0:r], chunk_cols(acs, c)[0:r, h:h + 1],
                                                    m[0:r, 0:r], ALU.subtract, ALU.add)
                last.then_inc(S["z_done"], 1)

            def back(c, s):
                r = NS if is_sample(c) else P
                wait(dve, "e_done", c + 1)
                for g in range(NGROUP):
                    e = E[0:r, s, g * HPG:(g + 1) * HPG, 0:r]
                    last = dve.tensor_tensor(e, e, G[s][0:r, g, 0:r].unsqueeze(1).to_broadcast([r, HPG, r]), ALU.mult)
                last.then_inc(S["m_done"], 1)
                wait(dve, "o_mm", c + 1)
                wait(dve, "y1_done", c)
                dve.tensor_tensor(heads(off[0:r, :]), heads(pO[0:r, :]), per_head(chunk_cols(eacs, c), r),
                                  ALU.mult).then_inc(S["off_done"], 1)
                if is_sample(c):
                    dve.tensor_tensor(state_s[:, :, :].rearrange("p b (h f) -> p (b h) f", f=HD),
                                      state_s[:, :, :].rearrange("p b (h f) -> p (b h) f", f=HD),
                                      etot_s[:, :].unsqueeze(2).to_broadcast([P, DB * NH, HD]),
                                      ALU.mult).then_inc(S["st_scaled"], 1)
                    wait(dve, "st_scaled", c + 1)
                    for b in range(DB):
                        wait(dve, "s_mm", c + 1 + b)
                        dve.tensor_tensor(state_s[:, b, :], state_s[:, b, :], pS[:, :], ALU.add).then_inc(S["st_done"], 1)
                else:
                    wait(dve, "zeroed", 1)
                    wait(dve, "st_done", c)
                    dve.tensor_tensor(heads(state[:, :]), heads(state[:, :]), per_head(chunk_cols(etot, c), P),
                                      ALU.mult).then_inc(S["st_scaled"], 1)
                    wait(dve, "st_scaled", c + 1)
                    wait(dve, "s_mm", c + 1)
                    dve.tensor_tensor(state[:, :], state[:, :], pS[:, :], ALU.add).then_inc(S["st_done"], 1)
                wait(dve, "off_done", c + 1)
                wait(dve, "t_mm", c - 1)
                dve.tensor_tensor(Y[0:r, s, :], off[0:r, :], pY[0:r, :], ALU.add).then_inc(S["y1_done"], 1)

            run(dve, front, back, nothing)

        @block.scalar
        def _(act):
            wait(act, "pre", 1)
            act.activation(ab[:, :], d[:, :], ACT.Abs).then_inc(S["pre"], 1)
            wait(act, "pre", 2)
            act.activation(ab[:, :], ab[:, :], ACT.Exp, scale=-1.0).then_inc(S["pre"], 1)
            wait(act, "loaded", 192)
            act.activation(ea[:, 0:NH], a_log[:, :], ACT.Exp).then_inc(S["pre"], 1)
            wait(act, "pre", 4)
            act.activation(ex[:, :], ab[:, :], ACT.Ln, bias=1.0).then_inc(S["pre"], 1)
            wait(act, "acs_ready", 2)
            act.activation(decay[:, 0:PC], rest[:, 0:PC], ACT.Exp)
            act.activation(decay[0:NS, PC:], rest[0:NS, PC:], ACT.Exp)
            act.activation(eacs[:, 0:PC], acs[:, 0:PC], ACT.Exp)
            act.activation(eacs[0:NS, PC:], acs[0:NS, PC:], ACT.Exp)
            act.activation(etot[:, 0:PC], pO[:, 0:PC], ACT.Exp)
            act.activation(etot_s[:, :], pS[:, 0:DB * NH], ACT.Exp).then_inc(S["decay_ready"], 1)

            def front(c, s):
                r = NS if is_sample(c) else P
                wait(act, "z_done", c + 1)
                act.activation(E[0:r, s, :, 0:r], E[0:r, s, :, 0:r], ACT.Exp).then_inc(S["e_done"], 1)

            def turn(c, s):
                r = NS if is_sample(c) else P
                wait(act, "y3_done", c + 1)
                for g in range(NGROUP):
                    wait(act, "ssq_done", c if g == 0 else c)
                    last = act.activation(junk[0:r, :] if g == 0 else off_junk[0:r, :], Y[0:r, s, g * GW:(g + 1) * GW],
                                          ACT.Square, accum_out=ssq[0:r, s, g:g + 1])
                last.then_inc(S["ssq_done"], 1)
                wait(act, "rs_done", c + 1)
                wait(act, "ssq_done", c + 1)
                for g in range(NGROUP):
                    y = Y[0:r, s, g * GW:(g + 1) * GW]
                    last = act.activation(y, y, ACT.Copy, scale=rs[0:r, s, g:g + 1])
                last.then_inc(S["yn_done"], 1)
                wait(act, "t_mm", c + 1)
                act.activation(mixT[:, NPAIR:2 * NPAIR, ds(c * P, r)], pT[:, :, 0:r], ACT.Copy).then_inc(S["ty_done"], 1)

            run(act, front, nothing, turn)

        @block.tensor
        def _(pe):
            wait(pe, "adt_ready", 2)
            wait(pe, "loaded", 192)
            pe.matmul(pY[:, 0:PC], tri[:, :], adt[:, 0:PC], start=True, stop=True)
            pe.matmul(pY[0:NS, PC:C_ALL], tri_s[:, :], adt[0:NS, PC:], start=True, stop=True)
            pe.matmul(pO[:, 0:PC], ones[:, :], adt[:, 0:PC], start=True, stop=True)
            pe.matmul(pO[0:NS, PC:C_ALL], ones_s[:, :], adt[0:NS, PC:], start=True, stop=True)
            pe.matmul(pS[:, 0:DB * NH], ones[0:NS, :], adt_b[:, :, :].rearrange("p b h -> p (b h)"), start=True,
                      stop=True).then_inc(S["sums_done"], 1)

            def front(c, s):
                wait(pe, "m_done", c - 1)
                if is_sample(c):
                    for g in range(NGROUP):
                        pe.matmul(G[s][0:NS, g, 0:NS], BT[:, g, SEQ:TOK], CT[:, g, SEQ:TOK], start=True, stop=True)
                    wait(pe, "z_done", c)
                    for h in range(NH):
                        last = pe.matmul(R[0:NS, h, 0:NS], adt[0:NS, PC + h:PC + h + 1].to_broadcast([NS, NS]), tri_s[:, :],
                                         start=True, stop=True)
                else:
                    wait(pe, "staged", c + 1)
                    for g in range(NGROUP):
                        pe.matmul(G[s][:, g, :], BTs[:, s, g, :], CTs[:, s, g, :], start=True, stop=True)
                    wait(pe, "z_done", c)
                    for h in range(NH):
                        last = pe.matmul(R[:, h, :], adts[:, s, h:h + 1].to_broadcast([P, P]), tri[:, :], start=True, stop=True)
                last.then_inc(S["gr_done"], 1)

            def back(c, s):
                r = NS if is_sample(c) else P
                wait(pe, "m_done", c + 1)
                wait(pe, "y1_done", c)
                wait(pe, "decay_ready", 1)
                for h in range(NH):
                    last = pe.matmul(pY[0:r, h * HD:(h + 1) * HD], E[0:r, s, h, 0:r], xdt[0:r, s, h * HD:(h + 1) * HD],
                                     start=True, stop=True)
                last.then_inc(S["y_mm"], 1)
                wait(pe, "off_done", c)
                wait(pe, "st_done", c)
                wait(pe, "zeroed", 1)
                if is_sample(c):
                    wait(pe, "cz_ready", 1)
                    wait(pe, "bz_ready", 1)
                    for g in range(NGROUP):
                        for b in range(DB):
                            last = pe.matmul(pO[0:NS, g * GW:(g + 1) * GW], Cz[:, g, b * NS:(b + 1) * NS],
                                             state_s[:, b, g * GW:(g + 1) * GW], start=(b == 0), stop=(b == DB - 1))
                    last.then_inc(S["o_mm"], 1)
                    for b in range(DB):
                        wait(pe, "st_done", c + b)
                        for g in range(NGROUP):
                            last = pe.matmul(pS[:, g * GW:(g + 1) * GW], Bz[:, b, g * P:(g + 1) * P],
                                             xdd[0:NS, s, g * GW:(g + 1) * GW], start=True, stop=True)
                        last.then_inc(S["s_mm"], 1)
                else:
                    for g in range(NGROUP):
                        last = pe.matmul(pO[:, g * GW:(g + 1) * GW], CTs[:, s, g, :], state[:, g * GW:(g + 1) * GW],
                                         start=True, stop=True)
                    last.then_inc(S["o_mm"], 1)
                    for g in range(NGROUP):
                        last = pe.matmul(pS[:, g * GW:(g + 1) * GW], Bts[:, s, g, :], xdd[:, s, g * GW:(g + 1) * GW],
                                         start=True, stop=True)
                    last.then_inc(S["s_mm"], 1)

            def turn(c, s):
                r = NS if is_sample(c) else P
                wait(pe, "yw_done", c + 1)
                wait(pe, "ty_done", c)
                for j in range(NPAIR):
                    last = pe.transpose(pT[:, j, 0:r], Y[0:r, s, j * P:(j + 1) * P], ident[0:r, 0:r])
                last.then_inc(S["t_mm"], 1)

            run(pe, front, back, turn)


def shape_constants():
    k = np.arange(P)
    tok = np.arange(NS)
    same = (tok[:, None] // DT) == (tok[None, :] // DT)
    causal_s = same & (tok[:, None] <= tok[None, :])
    f = np.float32
    return {
        "c_ident": np.eye(P, dtype=f),
        "c_tri": (k[:, None] <= k[None, :]).astype(f),
        "c_tri_s": causal_s.astype(f),
        "c_ones": np.ones((P, P), f),
        "c_mask": np.where(k[:, None] <= k[None, :], 0, NEG).astype(f),
        "c_mask_s": np.where(causal_s, 0, NEG).astype(f),
        "c_ones_s": same.astype(f),
        "c_in_seq": ((tok[:, None] // DT) == np.arange(DB)[None, :]).astype(f),
    }
def alibi(h, dist):
    slope = np.float32(2.0 ** (-8.0 * (h + 1) / NH))
    count = sum(((dist >= 0) & (dist <= w) & (dist % r == 0)).astype(np.float64) for w, r in BRANCHES)
    return np.where(count > 0, -slope * dist + np.log(np.maximum(count, 1)), NEG).astype(np.float32)


def attention_constants():
    p = np.arange(P)[:, None]
    wide = SEQ - P + p - np.arange(SEQ)[None, :]
    table = np.stack([alibi(h, wide) for h in range(NH)])
    t = np.arange(DT)[:, None]
    past = np.concatenate([alibi(h, PAST + t - np.arange(PAST)[None, :]) for h in range(NH)])
    new = np.full((NH * DT, (2 * DB - 1) * DT), NEG, np.float32)
    own = np.concatenate([alibi(h, t - np.arange(DT)[None, :]) for h in range(NH)])
    new[:, (DB - 1) * DT:DB * DT] = own
    return {"c_alibi": table, "c_alibi_past": past, "c_alibi_new": new}


def load_keys(sp, io, Kc, loaded, b, s):
    sp.dma_start(Kc[:, s, :, :], io["cache_kT"][ds(b, 1)].squeeze(0)).then_inc(loaded[s], 16)


def load_values(sp, io, Vc, loaded, b, s):
    sp.dma_start(Vc[:, s, :, :], io["cache_v"][ds(b, 1)].squeeze(0).rearrange("(n p) f -> p n f", p=P)).then_inc(loaded[s], 16)


def stage_prompt_attention(nc, sem, io, ident, qT, kT, mixT, place, prefetch):
    qz = [place(f"pa_qz{u}", [P, SEQ]) for u in range(2)]
    table = place("pa_table", [P, 2, SEQ])
    V = [place(f"pa_V{u}", [P, NQB, P]) for u in range(2)]
    NZ = 4
    Z = place("pa_Z", [P, NZ, SEQ])
    PT = [place(f"pa_PT{s}", [P, NQB, P]) for s in range(2)]
    nmax, total, inv = (place("pa_" + n, [P, NZ, 1]) for n in ("nmax", "total", "inv"))
    S = {n: sem("pa_" + n) for n in ("zeroed", "qk", "z", "max", "exp", "inv", "norm", "turn", "pt", "pv")}
    out_done = [sem(f"pa_out{s}") for s in range(2)]
    staged = [sem(f"pa_staged{u}") for u in range(2)]
    loaded = [sem(f"pa_loaded{u}") for u in range(2)]
    ITEMS = 2 * NQB
    head_of = lambda m: m // NQB % 2
    block_of = lambda m: m % NQB
    pair_of = lambda i, m: i + m // ITEMS
    keys = lambda m: (block_of(m) + 1) * P
    groups = lambda m: -(-(block_of(m) + 1) // 4)
    groups_to = lambda m: sum(groups(k) for k in range(m))
    G_ALL = groups_to(ITEMS)

    def pipeline(engine, lead, first, second, third):
        def step(i, m, last):
            if not last or m + lead < ITEMS:
                first(i, m + lead)
            second(i, m)
            if not isinstance(i, int) or i * ITEMS + m:
                third(i, m - 1)

        for m in range(lead):
            first(0, m)
        for m in range(NZ):
            step(0, m, False)
        with engine.Fori(0, NPAIR - 1) as i:
            for m in range(NZ, ITEMS + NZ):
                step(i, m, False)
        for m in range(NZ, ITEMS):
            step(NPAIR - 1, m, True)
        third(NPAIR - 1, ITEMS - 1)

    with ExitStack() as ctx:
        pS = [ctx.enter_context(nc.psum_tensor(f"pa_S{s}", [P, SEQ], F32)) for s in range(2)]
        pT = [ctx.enter_context(nc.psum_tensor(f"pa_T{s}", [P, 4, P], F32)) for s in range(2)]
        pO = [ctx.enter_context(nc.psum_tensor(f"pa_O{s}", [P, P], F32)) for s in range(2)]
        block = ctx.enter_context(nc.Block())

        @block.sync
        def _(sp):
            def load(i, u):
                sp.dma_start(table[:, u, :], io["c_alibi"][ds(i * 2 + u, 1)].squeeze(0)).then_inc(loaded[u], 16)
                sp.dma_start(V[u][:, :, :], io["new_v"][0:SEQ, ds(i * P, P)].rearrange("(b p) f -> p b f", p=P))\
                    .then_inc(loaded[u], 16)

            load(0, 0)
            load(0, 1)
            with sp.Fori(0, NPAIR - 1) as i:
                for u in range(2):
                    sp.wait_ge(S["z"], i * ITEMS + (u + 1) * NQB)
                    sp.wait_ge(S["pv"], i * ITEMS + (u + 1) * NQB)
                    load(i + 1, u)
            prefetch(sp)

        @block.gpsimd
        def _(pool):
            for u in range(2):
                pool.memset(qz[u][(1 - u) * HD:(2 - u) * HD, :], 0.0).then_inc(S["zeroed"], 1)
                pool.wait_ge(S["zeroed"], u + 1)
            def stage(i, u):
                pool.wait_ge(staged[1 - u], i + u)
                pool.tensor_copy(qz[u][u * HD:(u + 1) * HD, :],
                                 qT[u * HD:(u + 1) * HD, ds(i, 1), 0:SEQ].squeeze(1)).then_inc(staged[u], 1)

            stage(0, 0)
            stage(0, 1)
            with pool.Fori(0, NPAIR - 1) as i:
                for u in range(2):
                    pool.wait_ge(S["qk"], i * ITEMS + (u + 1) * NQB)
                    stage(i + 1, u)

        @block.vector
        def _(dve):
            def scores(i, m):
                n, u, at = keys(m), head_of(m), i * ITEMS + (m + 1)
                if block_of(m) == 0:
                    dve.wait_ge(loaded[u], pair_of(i, m) * 32 + 32)
                dve.wait_ge(S["qk"], at)
                if m >= NZ:
                    dve.wait_ge(S["turn"], i * G_ALL + groups_to(m - NZ + 1))
                z = Z[:, m % NZ, 0:n]
                dve.scalar_tensor_tensor(z, pS[m % 2][:, 0:n], HD ** -0.5, table[:, u, SEQ - n:SEQ], ALU.mult,
                                         ALU.add).then_inc(S["z"], 1)
                dve.wait_ge(S["z"], at)
                dve.reduce_max(nmax[:, m % NZ, :], z, AX.X, negate=True).then_inc(S["max"], 1)

            def norm(i, m):
                n, at = keys(m), i * ITEMS + (m + 1)
                dve.wait_ge(S["exp"], at)
                dve.reciprocal(inv[:, m % NZ, :], total[:, m % NZ, :]).then_inc(S["inv"], 1)
                dve.wait_ge(S["inv"], at)
                dve.tensor_scalar(Z[:, m % NZ, 0:n], Z[:, m % NZ, 0:n], inv[:, m % NZ, :], None, ALU.mult).then_inc(S["norm"], 1)

            pipeline(dve, 1, scores, norm, lambda i, m: None)

        @block.scalar
        def _(act):
            def exps(i, m):
                z = Z[:, m % NZ, 0:keys(m)]
                act.wait_ge(S["max"], i * ITEMS + (m + 1))
                act.activation(z, z, ACT.Exp, bias=nmax[:, m % NZ, :], accum_out=total[:, m % NZ, :]).then_inc(S["exp"], 1)

            def read_turned(i, m):
                if m >= 2:
                    act.wait_ge(S["pv"], i * ITEMS + (m - 1))
                for g in range(groups(m)):
                    t = groups_to(m) + g
                    k = min(4, block_of(m) + 1 - 4 * g)
                    act.wait_ge(S["turn"], i * G_ALL + (t + 1))
                    act.activation(PT[m % 2][:, 4 * g:4 * g + k, :], pT[t % 2][:, 0:k, :], ACT.Copy).then_inc(S["pt"], 1)

            def out(i, m):
                u, b = head_of(m), block_of(m)
                act.wait_ge(S["pv"], i * ITEMS + (m + 1))
                act.activation(mixT[u * HD:(u + 1) * HD, ds(pair_of(i, m), 1), b * P:(b + 1) * P].squeeze(1),
                               pO[m % 2][u * HD:(u + 1) * HD, :], ACT.Copy).then_inc(out_done[m % 2], 1)

            pipeline(act, 1, exps, read_turned, out)

        @block.tensor
        def _(pe):
            def qk(i, m):
                u, b, n = head_of(m), block_of(m), keys(m)
                if b == 0:
                    pe.wait_ge(staged[u], pair_of(i, m) + 1)
                if m >= 2:
                    pe.wait_ge(S["z"], i * ITEMS + (m - 1))
                for c in range(0, n, 512):
                    w = min(512, n - c)
                    last = pe.matmul(pS[m % 2][:, c:c + w], qz[u][:, b * P:(b + 1) * P],
                                     kT[:, ds(pair_of(i, m), 1), c:c + w].squeeze(1), start=True, stop=True)
                last.then_inc(S["qk"], 1)

            def turn(i, m):
                pe.wait_ge(S["norm"], i * ITEMS + (m + 1))
                for g in range(groups(m)):
                    t = groups_to(m) + g
                    if t >= 2:
                        pe.wait_ge(S["pt"], i * G_ALL + (t - 1))
                    for k in range(min(4, block_of(m) + 1 - 4 * g)):
                        kb = 4 * g + k
                        last = pe.transpose(pT[t % 2][:, k, :], Z[:, m % NZ, kb * P:(kb + 1) * P], ident[:, :])
                    last.then_inc(S["turn"], 1)

            def pv(i, m):
                u, nk = head_of(m), block_of(m) + 1
                if block_of(m) == 0:
                    pe.wait_ge(loaded[u], pair_of(i, m) * 32 + 32)
                pe.wait_ge(S["pt"], i * G_ALL + groups_to(m + 1))
                pe.wait_ge(out_done[m % 2], i * (ITEMS // 2) + m // 2)
                for kb in range(nk):
                    last = pe.matmul(pO[m % 2][:, :], V[u][:, kb, :], PT[m % 2][:, kb, :], start=(kb == 0), stop=(kb == nk - 1))
                last.then_inc(S["pv"], 1)

            pe.wait_ge(S["zeroed"], 2)
            pipeline(pe, 2, qk, turn, pv)


def stage_sample_attention(nc, sem, io, ident, qT, kT, mixT, Kc, Vc, keys_loaded, values_loaded, place):
    R = NH * DT
    past, new = place("sa_past", [R, PAST]), place("sa_new", [R, (2 * DB - 1) * DT])
    Vn = place("sa_Vn", [NS, DA])
    Q = [place(f"sa_Q{s}", [P, NPAIR * (R + 2 * DT)]) for s in range(2)]
    Z = place("sa_Z", [R, 2, PAST + NS])
    PT = [place(f"sa_PT{s}", [P, NQB + 1, R]) for s in range(2)]
    nmax, total, inv = (place("sa_" + n, [R, 2, 1]) for n in ("nmax", "total", "inv"))
    tables_loaded = sem("sa_tables_loaded")
    two = lambda n: [sem(f"sa_{n}{s}") for s in range(2)]
    zeroed, q_ready, qk, z, mx, ex, iv, norm, turn, pt, pv, out = (
        two(n) for n in ("zeroed", "q_ready", "qk", "z", "max", "exp", "inv", "norm", "turn", "pt", "pv", "out"))

    def over_sequences(engine, front, back):
        front(0, 0, 0)
        with engine.Fori(0, DB // 2 - 1) as i:
            front(i * 2 + 1, 1, i)
            back(i * 2, 0, i)
            front(i * 2 + 2, 0, i + 1)
            back(i * 2 + 1, 1, i)
        last = DB // 2 - 1
        front(DB - 1, 1, last)
        back(DB - 2, 0, last)
        back(DB - 1, 1, last)

    with ExitStack() as ctx:
        pS = ctx.enter_context(nc.psum_tensor("sa_S", [R, 3, 512], F32))
        pT = ctx.enter_context(nc.psum_tensor("sa_T", [P, 2, 512], F32))
        pO = ctx.enter_context(nc.psum_tensor("sa_O", [P, NPAIR, 2 * DT], F32))
        block = ctx.enter_context(nc.Block())

        @block.sync
        def _(sp):
            sp.dma_start(past[:, :], io["c_alibi_past"]).then_inc(tables_loaded, 16)
            sp.dma_start(new[:, :], io["c_alibi_new"]).then_inc(tables_loaded, 16)
            sp.dma_start(Vn[:, :], io["new_v"][SEQ:TOK, :]).then_inc(tables_loaded, 16)
            with sp.Fori(0, DB // 2 - 1) as i:
                for s in range(2):
                    sp.wait_ge(qk[s], i + 1)
                    load_keys(sp, io, Kc, keys_loaded, i * 2 + (2 + s), s)
                    sp.wait_ge(pv[s], i + 1)
                    load_values(sp, io, Vc, values_loaded, i * 2 + (2 + s), s)

        @block.gpsimd
        def _(pool):
            for s in range(2):
                pool.memset(Q[s][:, :], 0.0).then_inc(zeroed[s], 1)

            def front(b, s, i):
                pool.wait_ge(zeroed[0], 1)
                pool.wait_ge(zeroed[1], 1)
                pool.wait_ge(qk[s], i)
                pool.wait_ge(q_ready[1 - s], (i + s) * 2)
                for u in range(2):
                    pool.wait_ge(q_ready[s], i * 2 + u)
                    pool.tensor_copy(Q[s][u * HD:(u + 1) * HD, :].rearrange("p (j x) -> p j x", j=NPAIR)[:, :, u * DT:(u + 1) * DT],
                                     qT[u * HD:(u + 1) * HD, :, ds(b * DT + SEQ, DT)]).then_inc(q_ready[s], 1)

            over_sequences(pool, front, lambda *a: None)

        @block.vector
        def _(dve):
            dve.wait_ge(tables_loaded, 48)

            def front(b, s, i):
                dve.wait_ge(qk[s], i + 1)
                dve.wait_ge(turn[s], i)
                dve.scalar_tensor_tensor(Z[:, s, 0:PAST], pS[:, 0:2, :].rearrange("p a b -> p (a b)"), HD ** -0.5, past[:, :],
                                         ALU.mult, ALU.add)
                dve.scalar_tensor_tensor(Z[:, s, PAST:], pS[:, 2, 0:NS], HD ** -0.5, new[:, ds(b * -DT + (DB - 1) * DT, NS)],
                                         ALU.mult, ALU.add).then_inc(z[s], 1)
                dve.wait_ge(z[s], i + 1)
                dve.reduce_max(nmax[:, s, :], Z[:, s, :], AX.X, negate=True).then_inc(mx[s], 1)

            def back(b, s, i):
                dve.wait_ge(ex[s], i + 1)
                dve.reciprocal(inv[:, s, :], total[:, s, :]).then_inc(iv[s], 1)
                dve.wait_ge(iv[s], i + 1)
                dve.tensor_scalar(Z[:, s, :], Z[:, s, :], inv[:, s, :], None, ALU.mult).then_inc(norm[s], 1)
                dve.wait_ge(pv[s], i + 1)
                for u in range(2):
                    last = dve.tensor_copy(mixT[u * HD:(u + 1) * HD, 0:NPAIR, ds(b * DT + SEQ, DT)],
                                           pO[u * HD:(u + 1) * HD, :, u * DT:(u + 1) * DT])
                last.then_inc(out[s], 1)

            over_sequences(dve, front, back)

        @block.scalar
        def _(act):
            def front(b, s, i):
                act.wait_ge(mx[s], i + 1)
                act.activation(Z[:, s, :], Z[:, s, :], ACT.Exp, bias=nmax[:, s, :], accum_out=total[:, s, :]).then_inc(ex[s], 1)

            def back(b, s, i):
                act.wait_ge(turn[s], i + 1)
                act.wait_ge(pv[s], i)
                act.activation(PT[s][:, 0:NQB, :].rearrange("p n r -> p (n r)"), pT[:, 0, :], ACT.Copy)
                act.activation(PT[s][0:NS, NQB, :], pT[0:NS, 1, 0:R], ACT.Copy).then_inc(pt[s], 1)

            over_sequences(act, front, back)

        @block.tensor
        def _(pe):
            pe.wait_ge(tables_loaded, 48)

            def front(b, s, i):
                pe.wait_ge(keys_loaded[s], i * 16 + 16)
                pe.wait_ge(q_ready[s], i * 2 + 2)
                pe.wait_ge(z[1 - s], i + s)
                for c in range(3):
                    for j in range(NPAIR):
                        keys = Kc[:, s, j, c * 512:(c + 1) * 512] if c < 2 else kT[:, j, SEQ:TOK]
                        last = pe.matmul(pS[:, c, 0:512 if c < 2 else NS], Q[s][:, j * R:(j + 1) * R], keys,
                                         start=(j == 0), stop=(j == NPAIR - 1))
                last.then_inc(qk[s], 1)

            def back(b, s, i):
                pe.wait_ge(tables_loaded, 48)
                pe.wait_ge(norm[s], i + 1)
                pe.wait_ge(pt[1 - s], i + s)
                for n in range(NQB):
                    pe.transpose(pT[:, 0, n * R:(n + 1) * R], Z[:, s, n * P:(n + 1) * P], ident[0:R, 0:R])
                pe.transpose(pT[0:NS, 1, 0:R], Z[:, s, PAST:], ident[0:R, 0:R]).then_inc(turn[s], 1)
                pe.wait_ge(pt[s], i + 1)
                pe.wait_ge(out[1 - s], i + s)
                pe.wait_ge(values_loaded[s], i * 16 + 16)
                for j in range(NPAIR):
                    cols = slice(j * 2 * DT, (j + 1) * 2 * DT)
                    for n in range(NQB):
                        pe.matmul(pO[:, j, :], Vc[:, s, n, j * P:(j + 1) * P], PT[s][:, n, cols], start=(n == 0), stop=False)
                    last = pe.matmul(pO[:, j, :], Vn[:, j * P:(j + 1) * P], PT[s][0:NS, NQB, cols], start=False, stop=True)
                last.then_inc(pv[s], 1)

            over_sequences(pe, front, back)
class LayerNorm:

    def __init__(self, sem, place, tag):
        self.G, self.B = place(tag + "_g", [P, D]), place(tag + "_b", [P, D])
        self.bn, self.mv = place(tag + "_bn", [P, 2, 2, 6]), place(tag + "_mv", [P, 2, 2])
        self.veps, self.rstd, self.nmr = (place(f"{tag}_{n}", [P, 2, 1]) for n in ("veps", "rstd", "nmr"))
        self.mhalf, self.eps, self.taken = (place(f"{tag}_{n}", [P, 1]) for n in ("mhalf", "eps", "taken"))
        self.loaded, self.const_set = sem(tag + "_loaded"), sem(tag + "_const_set")
        two = lambda n: [sem(f"{tag}_{n}{s}") for s in range(2)]
        self.bn_done, self.mv_done, self.veps_done, self.rstd_done, self.nmr_done, self.xn_done, self.gain_done, self.done = (
            two(n) for n in ("bn_done", "mv_done", "veps_done", "rstd_done", "nmr_done", "xn_done", "gain_done", "done"))

    def load(self, sp, g, b):
        sp.dma_start(self.G[:, :], g.partition_broadcast(P)).then_inc(self.loaded, 16)
        sp.dma_start(self.B[:, :], b.partition_broadcast(P)).then_inc(self.loaded, 16)

    def constants(self, pool):
        pool.memset(self.mhalf[:, :], -0.5).then_inc(self.const_set, 1)
        pool.memset(self.eps[:, :], EPS).then_inc(self.const_set, 1)
        pool.wait_ge(self.const_set, 2)
        pool.wait_ge(self.loaded, 32)

    def statistics(self, dve, x, s, i, r):
        half = D // 2
        dve.bn_stats(self.bn[0:r, s, 0, :], x[:, 0:half])
        dve.bn_stats(self.bn[0:r, s, 1, :], x[:, half:D]).then_inc(self.bn_done[s], 1)
        take_statistics(dve, self.taken[0:r, :], self.bn[0:r, s, 1, 0:1], self.bn_done[s], i + 1)
        dve.bn_aggr(self.mv[0:r, s, :], self.bn[0:r, s, :, :]).then_inc(self.mv_done[s], 1)

    def inverse_root(self, pool, s, i, r):
        pool.wait_ge(self.mv_done[s], i + 1)
        pool.tensor_tensor(self.veps[0:r, s, :], self.mv[0:r, s, 1:2], self.eps[0:r, :], ALU.add).then_inc(self.veps_done[s], 1)
        pool.wait_ge(self.veps_done[s], i + 1)
        pool.tensor_tensor(self.rstd[0:r, s, :], self.veps[0:r, s, :], self.mhalf[0:r, :], ALU.pow).then_inc(self.rstd_done[s], 1)

    def shift(self, dve, s, i, r):
        dve.wait_ge(self.rstd_done[s], i + 1)
        dve.tensor_scalar(self.nmr[0:r, s, :], self.mv[0:r, s, 0:1], self.rstd[0:r, s, :], -1.0, ALU.mult,
                          ALU.mult).then_inc(self.nmr_done[s], 1)

    def normalise(self, act, out, x, s, i, r):
        act.wait_ge(self.nmr_done[s], i + 1)
        act.activation(out, x, ACT.Identity, bias=self.nmr[0:r, s, :], scale=self.rstd[0:r, s, :]).then_inc(self.xn_done[s], 1)

    def gain(self, pool, x, s, i, r):
        pool.wait_ge(self.xn_done[s], i + 1)
        pool.tensor_tensor(x, x, self.G[0:r, :], ALU.mult).then_inc(self.gain_done[s], 1)

    def bias(self, dve, x, s, i, r):
        dve.wait_ge(self.gain_done[s], i + 1)
        dve.tensor_tensor(x, x, self.B[0:r, :], ALU.add).then_inc(self.done[s], 1)


class ResidentWeight:

    def __init__(self, sem, place, tag, dram, width):
        self.dram, self.chunks, self.width = dram, dram.shape[0] // P, width
        self.raw = place(tag + "_raw", [P, 2, width])
        self.hi = place(tag + "_hi", [P, self.chunks, width], F32R)
        self.lo = place(tag + "_lo", [P, self.chunks, width], F32R)
        self.loaded = [sem(f"{tag}_loaded{s}") for s in range(2)]
        self.hi_done, self.lo_done = sem(tag + "_hi_done"), sem(tag + "_lo_done")

    def load(self, sp):
        for k in range(self.chunks):
            if k >= 2:
                sp.wait_ge(self.lo_done, k - 1)
            sp.dma_start(self.raw[:, k % 2, :], self.dram[k * P:(k + 1) * P, :]).then_inc(self.loaded[k % 2], 16)

    def split_hi(self, act):
        for k in range(self.chunks):
            act.wait_ge(self.loaded[k % 2], 16 * (k // 2 + 1))
            act.activation(self.hi[:, k, :], self.raw[:, k % 2, :], ACT.Copy).then_inc(self.hi_done, 1)

    def split_lo(self, dve):
        for k in range(self.chunks):
            dve.wait_ge(self.hi_done, k + 1)
            dve.tensor_tensor(self.lo[:, k, :], self.raw[:, k % 2, :], self.hi[:, k, :].bitcast(F32),
                              ALU.subtract).then_inc(self.lo_done, 1)


def over_blocks(engine, front, back):
    half = NQB // 2
    front(0, 0, P, 0)
    with engine.Fori(0, half - 1) as i:
        front(1, i, P, i * 2 + 1)
        back(0, i, P, i * 2)
        front(0, i + 1, P, i * 2 + 2)
        back(1, i, P, i * 2 + 1)
    front(1, half - 1, P, NQB - 1)
    back(0, half - 1, P, NQB - 2)
    front(0, half, NS, NQB)
    back(1, half - 1, P, NQB - 1)
    back(0, half, NS, NQB)


def split_product(pe, out, weights_first, n_k):
    for k in range(n_k):
        a_hi, a_lo, b_hi, b_lo = weights_first(k)
        for part, (a, b) in enumerate(((a_hi, b_hi), (a_hi, b_lo), (a_lo, b_hi))):
            last = pe.matmul(out, a, b, start=(k == 0 and part == 0), stop=(k == n_k - 1 and part == 2))
    return last


def stage_output(nc, sem, io, mixT, R, place):
    w = ResidentWeight(sem, place, "op_w", io["w_out"], D)
    ln = LayerNorm(sem, place, "op_ln")
    h0 = place("op_h0", [P, 2, D])
    m_hi = [place(f"op_m_hi{s}", [P, KD, P], F32R) for s in range(2)]
    m_lo = [place(f"op_m_lo{s}", [P, KD, P], F32R) for s in range(2)]
    two = lambda n: [sem(f"op_{n}{s}") for s in range(2)]
    h0_loaded, hi_done, lo_done, mm_done, x_done = (two(n) for n in ("h0_loaded", "hi_done", "lo_done", "mm_done", "x_done"))
    with ExitStack() as ctx:
        pM = [ctx.enter_context(nc.psum_tensor(f"op_M{s}", [P, 2, 512], F32)) for s in range(2)]
        block = ctx.enter_context(nc.Block())
        row = lambda n, r: R[0:r, ds(n, 1), :].squeeze(1)

        @block.sync
        def _(sp):
            w.load(sp)
            ln.load(sp, io["ln1_g"], io["ln1_b"])

            def front(s, i, r, n):
                sp.wait_ge(x_done[s], i)
                sp.dma_start(h0[0:r, s, :], io["h0"][ds(n * P, r), :]).then_inc(h0_loaded[s], 16)

            over_blocks(sp, front, lambda *a: None)

        @block.gpsimd
        def _(pool):
            ln.constants(pool)

            def back(s, i, r, n):
                ln.inverse_root(pool, s, i, r)
                ln.gain(pool, row(n, r), s, i, r)

            over_blocks(pool, lambda *a: None, back)

        @block.scalar
        def _(act):
            def front(s, i, r, n):
                act.wait_ge(mm_done[s], i)
                act.activation(m_hi[s][:, :, 0:r], mixT[:, :, ds(n * P, r)], ACT.Copy).then_inc(hi_done[s], 1)

            w.split_hi(act)
            over_blocks(act, front, lambda s, i, r, n: ln.normalise(act, row(n, r), row(n, r), s, i, r))

        @block.vector
        def _(dve):
            def front(s, i, r, n):
                dve.wait_ge(hi_done[s], i + 1)
                dve.tensor_tensor(m_lo[s][:, :, 0:r], mixT[:, :, ds(n * P, r)], m_hi[s][:, :, 0:r].bitcast(F32),
                                  ALU.subtract).then_inc(lo_done[s], 1)

            def back(s, i, r, n):
                dve.wait_ge(mm_done[s], i + 1)
                dve.wait_ge(h0_loaded[s], i * 16 + 16)
                dve.scalar_tensor_tensor(row(n, r), h0[0:r, s, :], ALPHA, pM[s][0:r, :, :].rearrange("p a b -> p (a b)"),
                                         ALU.mult, ALU.add).then_inc(x_done[s], 1)
                dve.wait_ge(ln.loaded, 32)
                dve.wait_ge(x_done[s], i + 1)
                ln.statistics(dve, row(n, r), s, i, r)
                ln.shift(dve, s, i, r)
                ln.bias(dve, row(n, r), s, i, r)

            w.split_lo(dve)
            over_blocks(dve, front, back)

        @block.tensor
        def _(pe):
            def back(s, i, r, n):
                pe.wait_ge(lo_done[s], i + 1)
                pe.wait_ge(x_done[s], i)
                for half in range(2):
                    c = slice(half * 512, (half + 1) * 512)
                    last = split_product(pe, pM[s][0:r, half, :], lambda k: (
                        m_hi[s][:, k, 0:r], m_lo[s][:, k, 0:r], w.hi[:, k, c], w.lo[:, k, c]), KD)
                last.then_inc(mm_done[s], 1)

            pe.wait_ge(w.lo_done, KD)
            over_blocks(pe, lambda *a: None, back)


def stage_mlp(nc, sem, io, ident, R, place):
    FB = 4
    NC = DFF // (FB * P)
    UNITS = NB * 2
    hT_hi, hT_lo = place("ml_hT_hi", [P, KD, TOK], F32R), place("ml_hT_lo", [P, KD, TOK], F32R)
    u_hi = [place(f"ml_u_hi{f}", [P, TOK], F32R) for f in range(FB)]
    u_lo = [place(f"ml_u_lo{f}", [P, TOK], F32R) for f in range(FB)]
    relu, u = place("ml_relu", [P, TOK]), place("ml_u", [P, TOK])
    up_raw, down_raw = place("ml_up_raw", [P, KD, P]), place("ml_down_raw", [P, D])
    up_hi = [place(f"ml_up_hi{s}", [P, KD, P], F32R) for s in range(2)]
    up_lo = [place(f"ml_up_lo{s}", [P, KD, P], F32R) for s in range(2)]
    down_hi, down_lo = place("ml_down_hi", [P, FB, D], F32R), place("ml_down_lo", [P, FB, D], F32R)
    one = lambda *names: [sem("ml_" + n) for n in names]
    many = lambda n, k: [sem(f"ml_{n}{s}") for s in range(k)]
    up_loaded, up_hi_done, up_lo_done, down_loaded, down_hi_done, down_lo_done, down_used = one(
        "up_loaded", "up_hi_done", "up_lo_done", "down_loaded", "down_hi_done", "down_lo_done", "down_used")
    t_done, thi_done, tlo_done, scaled = one("t_done", "thi_done", "tlo_done", "scaled")
    up_mm, dn_mm, added = many("up_mm", 2), many("dn_mm", 2), many("added", 2)
    relu_done = [many(f"relu{s}_", 3) for s in range(2)]
    mul_done, sq_done, ulo_done = many("mul", 3), many("sq", 3), many("ulo", 3)

    def rows(n):
        return NS if n == NB - 1 else P

    with ExitStack() as ctx:
        pU = [ctx.enter_context(nc.psum_tensor(f"ml_U{s}", [P, 3, 512], F32)) for s in range(2)]
        pD = [ctx.enter_context(nc.psum_tensor(f"ml_D{s}", [P, 512], F32)) for s in range(2)]
        block = ctx.enter_context(nc.Block())

        def chunks(engine, chunk):
            with engine.Fori(0, NC - 1) as c:
                chunk(c, False)
            chunk(NC - 1, True)

        @block.sync
        def _(sp):
            def load_up(c, f):
                sp.wait_ge(up_lo_done, c * FB + f)
                sp.dma_start(up_raw[:, :, :], w_raw_view(io["w_up"], c * (FB * P) + f * P, P)).then_inc(up_loaded, 16)

            def chunk(c, last):
                for f in range(FB):
                    if not (last and f >= 2):
                        load_up(c, f + 2)
                    sp.wait_ge(down_lo_done, c * FB + f)
                    sp.dma_start(down_raw[:, :], io["w_down"][ds(c * (FB * P) + f * P, P), :]).then_inc(down_loaded, 16)

            load_up(0, 0)
            load_up(0, 1)
            chunks(sp, chunk)

        @block.gpsimd
        def _(pool):
            def chunk(c, last):
                for f in range(FB):
                    for g, (col, w) in enumerate(GROUPS):
                        pool.wait_ge(relu_done[f % 2][g], c * 2 + (f // 2 + 1))
                        pool.wait_ge(ulo_done[g], c * FB + f)
                        x = relu[:, col:col + w]
                        pool.tensor_tensor(u[:, col:col + w], x, x, ALU.mult).then_inc(mul_done[g], 1)

            chunks(pool, chunk)

        @block.scalar
        def _(act):
            def split_up(c, f):
                act.wait_ge(up_loaded, c * (16 * FB) + 16 * (f + 1))
                act.wait_ge(up_mm[f % 2], c * 6 + 3 * (f // 2))
                act.activation(up_hi[f % 2][:, :, :], up_raw[:, :, :], ACT.Copy).then_inc(up_hi_done, 1)

            def chunk(c, last):
                for f in range(FB):
                    s = f % 2
                    for g, (col, w) in enumerate(GROUPS):
                        act.wait_ge(up_mm[s], c * 6 + (3 * (f // 2) + g + 1))
                        act.wait_ge(mul_done[g], c * FB + f)
                        act.activation(relu[:, col:col + w], pU[s][:, g, 0:w], ACT.Relu).then_inc(relu_done[s][g], 1)
                        act.wait_ge(relu_done[s][g], c * 2 + (f // 2 + 1))
                        act.wait_ge(down_used, c)
                        act.activation(u_hi[f][:, col:col + w], relu[:, col:col + w], ACT.Square).then_inc(sq_done[g], 1)
                    if not (last and f >= 2):
                        split_up(c, f + 2)
                    act.wait_ge(down_loaded, c * (16 * FB) + 16 * (f + 1))
                    act.activation(down_hi[:, f, :], down_raw[:, :], ACT.Copy).then_inc(down_hi_done, 1)

            split_up(0, 0)
            split_up(0, 1)
            for n in range(NB):
                r = rows(n)
                act.wait_ge(t_done, n + 1)
                act.activation(hT_hi[:, :, n * P:n * P + r], pU[n % 2][:, 0:2, :].rearrange("p a (b c) -> p (a b) c", c=P)[:, :, 0:r],
                               ACT.Copy).then_inc(thi_done, 1)
                act.activation(R[0:r, n, :], R[0:r, n, :], ACT.Copy, scale=ALPHA).then_inc(scaled, 1)
            chunks(act, chunk)

        @block.vector
        def _(dve):
            def split_up(c, f):
                dve.wait_ge(up_hi_done, c * FB + (f + 1))
                dve.tensor_tensor(up_lo[f % 2][:, :, :], up_raw[:, :, :], up_hi[f % 2][:, :, :].bitcast(F32),
                                  ALU.subtract).then_inc(up_lo_done, 1)

            def chunk(c, last):
                for f in range(FB):
                    for g, (col, w) in enumerate(GROUPS):
                        dve.wait_ge(mul_done[g], c * FB + (f + 1))
                        dve.wait_ge(sq_done[g], c * FB + (f + 1))
                        dve.tensor_tensor(u_lo[f][:, col:col + w], u[:, col:col + w], u_hi[f][:, col:col + w].bitcast(F32),
                                          ALU.subtract).then_inc(ulo_done[g], 1)
                    if not (last and f >= 2):
                        split_up(c, f + 2)
                    dve.wait_ge(down_hi_done, c * FB + (f + 1))
                    dve.tensor_tensor(down_lo[:, f, :], down_raw[:, :], down_hi[:, f, :].bitcast(F32),
                                      ALU.subtract).then_inc(down_lo_done, 1)
                for v in range(UNITS):
                    n, half, s = v // 2, v % 2, v % 2
                    r = rows(n)
                    dve.wait_ge(dn_mm[s], c * NB + (v // 2 + 1))
                    dve.wait_ge(added[s], c * NB + v // 2)
                    acc = R[0:r, n, half * 512:(half + 1) * 512]
                    dve.tensor_tensor(acc, acc, pD[s][0:r, :], ALU.add).then_inc(added[s], 1)

            split_up(0, 0)
            split_up(0, 1)
            for n in range(NB):
                r = rows(n)
                dve.wait_ge(thi_done, n + 1)
                dve.tensor_tensor(hT_lo[:, :, n * P:n * P + r], pU[n % 2][:, 0:2, :].rearrange("p a (b c) -> p (a b) c", c=P)[:, :, 0:r],
                                  hT_hi[:, :, n * P:n * P + r].bitcast(F32), ALU.subtract).then_inc(tlo_done, 1)
            dve.wait_ge(scaled, NB)
            chunks(dve, chunk)

        @block.tensor
        def _(pe):
            for n in range(NB):
                r = rows(n)
                if n >= 2:
                    pe.wait_ge(tlo_done, n - 1)
                for k in range(KD):
                    last = pe.transpose(pU[n % 2][:, k // 4, (k % 4) * P:(k % 4) * P + r], R[0:r, n, k * P:(k + 1) * P], ident[0:r, 0:r])
                last.then_inc(t_done, 1)
            pe.wait_ge(tlo_done, NB)

            def down(c, v, f):
                n, half, s = v // 2, v % 2, v % 2
                r = rows(n)
                cols, out = slice(half * 512, (half + 1) * 512), pD[s][0:r, :]
                a_hi, a_lo = u_hi[f][:, n * P:n * P + r], u_lo[f][:, n * P:n * P + r]
                for part, (a, b) in enumerate(((a_hi, down_hi), (a_hi, down_lo), (a_lo, down_hi))):
                    last = pe.matmul(out, a, b[:, f, cols], start=(f == 0 and part == 0), stop=(f == FB - 1 and part == 2))
                return last

            def chunk(c, last):
                for f in range(FB):
                    s = f % 2
                    pe.wait_ge(up_lo_done, c * FB + (f + 1))
                    for g, (col, w) in enumerate(GROUPS):
                        pe.wait_ge(relu_done[s][g], c * 2 + f // 2)
                        split_product(pe, pU[s][:, g, 0:w], lambda k: (
                            up_hi[s][:, k, :], up_lo[s][:, k, :], hT_hi[:, k, col:col + w], hT_lo[:, k, col:col + w]),
                            KD).then_inc(up_mm[s], 1)
                order = [(v, f) for f in range(FB - 1) for v in range(2)] + [(v, FB - 1) for v in range(2)]
                order += [(v, f) for v in range(2, UNITS) for f in range(FB)]
                for at, (v, f) in enumerate(order):
                    if f == 0:
                        pe.wait_ge(added[v % 2], c * NB + v // 2)
                    if v == 0:
                        pe.wait_ge(down_lo_done, c * FB + (f + 1))
                        for g in range(3):
                            pe.wait_ge(ulo_done[g], c * FB + (f + 1))
                    last_mm = down(c, v, f)
                    if f == FB - 1:
                        last_mm.then_inc(dn_mm[v % 2], 1)
                        if v == UNITS - 1:
                            pe.wait_ge(dn_mm[v % 2], c * NB + NB)
                            pe.sem_inc(down_used, 1)

            chunks(pe, chunk)


def stage_gate(nc, sem, io, ident, R, place):
    wg = ResidentWeight(sem, place, "gt_wg", io["w_gate"], D)
    wp = ResidentWeight(sem, place, "gt_wp", io["w_ple"], D)
    ln2, ln3 = LayerNorm(sem, place, "gt_ln2"), LayerNorm(sem, place, "gt_ln3")
    pe_raw = place("gt_pe", [P, 2, KPLE, P])
    h_hi = [place(f"gt_h_hi{s}", [P, KD, P], F32R) for s in range(2)]
    h_lo = [place(f"gt_h_lo{s}", [P, KD, P], F32R) for s in range(2)]
    p_hi = [place(f"gt_p_hi{s}", [P, KPLE, P], F32R) for s in range(2)]
    p_lo = [place(f"gt_p_lo{s}", [P, KPLE, P], F32R) for s in range(2)]
    gate, H = place("gt_gate", [P, 2, D]), place("gt_h", [P, 2, D])
    names = "pe_loaded turned hi lo phi plo gate_mm ple_mm sg gated x stored".split()
    S = {n: [sem(f"gt_{n}{s}") for s in range(2)] for n in names}
    with ExitStack() as ctx:
        pT = ctx.enter_context(nc.psum_tensor("gt_T", [P, KD, P], F32))
        pG = ctx.enter_context(nc.psum_tensor("gt_G", [P, 2, 512], F32))
        pP = ctx.enter_context(nc.psum_tensor("gt_P", [P, 2, 512], F32))
        block = ctx.enter_context(nc.Block())
        row = lambda n, r: R[0:r, ds(n, 1), :].squeeze(1)
        flat = lambda t, r: t[0:r, :, :].rearrange("p a b -> p (a b)")

        @block.sync
        def _(sp):
            ln2.load(sp, io["ln2_g"], io["ln2_b"])
            wg.load(sp)
            wp.load(sp)
            ln3.load(sp, io["ln3_g"], io["ln3_b"])

            def front(s, i, r, n):
                sp.wait_ge(S["plo"][s], i)
                sp.dma_start(pe_raw[:, s, :, 0:r], io["pT"][:, ds(n * P, r)].rearrange("(k p) t -> p k t", p=P))\
                    .then_inc(S["pe_loaded"][s], 16)

            def back(s, i, r, n):
                sp.wait_ge(ln3.done[s], i + 1)
                sp.dma_start(io["y"][ds(n * P, r), :], gate[0:r, s, :]).then_inc(S["stored"][s], 16)

            over_blocks(sp, front, back)
            sp.wait_ge(S["stored"][0], 16 * (NQB // 2 + 1))
            sp.wait_ge(S["stored"][1], 16 * (NQB // 2))

        @block.gpsimd
        def _(pool):
            ln2.constants(pool)
            ln3.constants(pool)

            def front(s, i, r, n):
                ln2.inverse_root(pool, s, i, r)
                ln2.gain(pool, H[0:r, s, :], s, i, r)

            def back(s, i, r, n):
                ln3.inverse_root(pool, s, i, r)
                ln3.gain(pool, gate[0:r, s, :], s, i, r)

            over_blocks(pool, front, back)

        @block.scalar
        def _(act):
            def front(s, i, r, n):
                act.wait_ge(S["x"][s], i)
                ln2.normalise(act, H[0:r, s, :], row(n, r), s, i, r)
                act.wait_ge(S["pe_loaded"][s], i * 16 + 16)
                act.wait_ge(S["ple_mm"][s], i)
                act.activation(p_hi[s][:, :, 0:r], pe_raw[:, s, :, 0:r], ACT.Copy).then_inc(S["phi"][s], 1)
                act.wait_ge(S["turned"][s], i + 1)
                act.activation(h_hi[s][:, :, 0:r], pT[:, :, 0:r], ACT.Copy).then_inc(S["hi"][s], 1)

            def back(s, i, r, n):
                act.wait_ge(S["gate_mm"][s], i + 1)
                act.wait_ge(S["stored"][s], i * 16)
                act.activation(gate[0:r, s, :], flat(pG, r), ACT.Sigmoid).then_inc(S["sg"][s], 1)
                ln3.normalise(act, gate[0:r, s, :], gate[0:r, s, :], s, i, r)

            wg.split_hi(act)
            wp.split_hi(act)
            over_blocks(act, front, back)

        @block.vector
        def _(dve):
            def front(s, i, r, n):
                ln2.statistics(dve, row(n, r), s, i, r)
                ln2.shift(dve, s, i, r)
                ln2.bias(dve, H[0:r, s, :], s, i, r)
                dve.wait_ge(S["phi"][s], i + 1)
                dve.tensor_tensor(p_lo[s][:, :, 0:r], pe_raw[:, s, :, 0:r], p_hi[s][:, :, 0:r].bitcast(F32),
                                  ALU.subtract).then_inc(S["plo"][s], 1)
                dve.wait_ge(S["hi"][s], i + 1)
                dve.tensor_tensor(h_lo[s][:, :, 0:r], pT[:, :, 0:r], h_hi[s][:, :, 0:r].bitcast(F32),
                                  ALU.subtract).then_inc(S["lo"][s], 1)

            def back(s, i, r, n):
                dve.wait_ge(S["sg"][s], i + 1)
                dve.wait_ge(S["ple_mm"][s], i + 1)
                x = gate[0:r, s, :]
                dve.tensor_tensor(x, x, flat(pP, r), ALU.mult).then_inc(S["gated"][s], 1)
                dve.wait_ge(S["gated"][s], i + 1)
                dve.scalar_tensor_tensor(x, H[0:r, s, :], ALPHA, x, ALU.mult, ALU.add).then_inc(S["x"][s], 1)
                dve.wait_ge(ln3.loaded, 32)
                dve.wait_ge(S["x"][s], i + 1)
                ln3.statistics(dve, x, s, i, r)
                ln3.shift(dve, s, i, r)
                ln3.bias(dve, x, s, i, r)

            wg.split_lo(dve)
            wp.split_lo(dve)
            over_blocks(dve, front, back)

        @block.tensor
        def _(pe):
            pe.wait_ge(wg.lo_done, KD)
            pe.wait_ge(wp.lo_done, KPLE)

            def front(s, i, r, n):
                pe.wait_ge(ln2.done[s], i + 1)
                pe.wait_ge(S["lo"][1 - s], i + s)
                for k in range(KD):
                    last = pe.transpose(pT[:, k, 0:r], H[0:r, s, k * P:(k + 1) * P], ident[0:r, 0:r])
                last.then_inc(S["turned"][s], 1)

            def back(s, i, r, n):
                pe.wait_ge(S["lo"][s], i + 1)
                pe.wait_ge(S["sg"][1 - s], i + s)
                pe.wait_ge(S["gated"][1 - s], i + s)
                for half in range(2):
                    c = slice(half * 512, (half + 1) * 512)
                    last = split_product(pe, pG[0:r, half, :], lambda k: (
                        h_hi[s][:, k, 0:r], h_lo[s][:, k, 0:r], wg.hi[:, k, c], wg.lo[:, k, c]), KD)
                last.then_inc(S["gate_mm"][s], 1)
                for half in range(2):
                    c = slice(half * 512, (half + 1) * 512)
                    last = split_product(pe, pP[0:r, half, :], lambda k: (
                        p_hi[s][:, k, 0:r], p_lo[s][:, k, 0:r], wp.hi[:, k, c], wp.lo[:, k, c]), KPLE)
                last.then_inc(S["ple_mm"][s], 1)

            over_blocks(pe, front, back)
OUTPUTS = {"y": (TOK, D), "new_k": (TOK, DA), "new_v": (TOK, DA), "new_convT": (P, NXBC, (CW - 1) * (1 + DB)),
           "new_ssm_promptT": (NSTATE, DA), "new_ssm_sampleT": (NSTATE, DB, DA)}


def build(nc, io):
    io = dict(io)
    io["h0"] = nc.dram_tensor("h0_scratch", [TOK, D], F32, kind="Internal").ap()
    io["z_act"] = nc.dram_tensor("z_act_scratch", [TOK, DA], F32, kind="Internal").ap()
    with ExitStack() as ctx:
        held, in_use = [ExitStack()], []

        def sem(name):
            in_use.append(held[0].enter_context(nc.semaphore(name)))
            return in_use[-1]

        def clear_semaphores():
            with nc.Block() as block:
                @block.sync
                def _(sp):
                    for s in in_use:
                        sp.sem_clear(s)
            held[0].close()
            held[0] = ExitStack()
            in_use.clear()

        ctx.callback(lambda: held[0].close())

        const = Place(nc, SBUF_START)
        ident = const("ident", [P, P])
        base = const.offset
        qk = Place(nc, base)
        qT, kT = qk("qT", [P, NPAIR, TOK]), qk("kT", [P, NPAIR, TOK])
        hT_hi, hT_lo = qk("hT_hi", [P, KD, TOK], F32R), qk("hT_lo", [P, KD, TOK], F32R)
        xbc_start = qk.offset
        Xt, Bt = qk("Xt", [P, NB, DA]), qk("Bt", [P, NB, NGROUP * NSTATE])
        BT, CT = qk("BT", [P, NGROUP, TOK]), qk("CT", [P, NGROUP, TOK])
        dt_raw = qk("dt_raw", [P, NB, NH])
        after_xbc = qk.offset
        late = Place(nc, base)
        R, mixT = late("R", [P, NB, D]), late("mixT", [P, KD, TOK])
        after_mix = late.offset

        consts_loaded = sem("consts_loaded")
        with nc.Block() as block:
            @block.sync
            def _(sp):
                sp.dma_start(ident[:, :], io["c_ident"]).then_inc(consts_loaded, 16)
                sp.wait_ge(consts_loaded, 16)

        consts = {"ident": ident, **{k[2:] + "_d": io[k] for k in (
            "c_tri", "c_tri_s", "c_ones", "c_mask", "c_mask_s", "c_ones_s", "c_in_seq")}}
        stage_input_norm(nc, sem, io, ident, hT_hi, hT_lo, Place(nc, xbc_start))
        stage_projection(nc, sem, io, ident, hT_hi, hT_lo, qT, kT, Xt, Bt, BT, CT, dt_raw, Place(nc, after_xbc))
        stage_ssd(nc, sem, io, consts, Xt, Bt, BT, CT, dt_raw, mixT, Place(nc, after_mix, xbc_start, after_xbc))
        clear_semaphores()
        attention = Place(nc, after_mix)
        Kc, Vc = attention("Kc", [P, 2, NPAIR, PAST]), attention("Vc", [P, 2, NQB, DA])
        keys_loaded, values_loaded = ([sem(f"cache_{n}_loaded{s}") for s in range(2)] for n in ("keys", "values"))
        after_cache = attention.offset

        def prefetch(sp):
            for b in range(2):
                load_keys(sp, io, Kc, keys_loaded, b, b)
                load_values(sp, io, Vc, values_loaded, b, b)

        stage_prompt_attention(nc, sem, io, ident, qT, kT, mixT, attention, prefetch)
        stage_sample_attention(nc, sem, io, ident, qT, kT, mixT, Kc, Vc, keys_loaded, values_loaded, Place(nc, after_cache))
        stage_output(nc, sem, io, mixT, R, Place(nc, after_mix))
        clear_semaphores()
        after_R = base + 4 * NB * D
        stage_mlp(nc, sem, io, ident, R, Place(nc, after_R))
        stage_gate(nc, sem, io, ident, R, Place(nc, after_R))


def kernel(**inputs):
    import concourse.bacc as bacc
    from concourse.bass_utils import run_bass_kernel_spmd

    x = {k: np.asarray(v) for k, v in inputs.items()}

    def features_first(a):
        a = a.reshape(a.shape[:-1] + (-1, P))
        return np.moveaxis(a, (-1, -2), (0, 1))

    arrays = {
        "x_prompt": x["x_prompt"][0], "x_sample": x["x_sample"].reshape(NS, D),
        "cache_kT": x["cache_k"][0].reshape(DB, PAST, NPAIR, P).transpose(0, 3, 2, 1),
        "cache_v": x["cache_v"][0].reshape(DB, PAST, DA),
        "state_convT": features_first(x["state_conv"][0].reshape(DB * (CW - 1), CD)),
        "state_ssmT": x["state_ssm"][0].reshape(DB, DA, NSTATE).transpose(2, 0, 1),
        "pT": np.concatenate([x["p_prompt"][0, 0], x["p_sample"][0].reshape(NS, DPLE)]).T,
        "conv_wT": np.moveaxis(features_first(x["conv_w"][0]), 2, -1), "conv_bT": features_first(x["conv_b"][0]),
        **{k: x[k] for k in ("ln_in_g", "ln_in_b")},
        **{k: x[k][0] for k in ("w_in", "dt_bias", "a_log", "d_skip", "ssd_norm_w", "w_out", "ln1_g", "ln1_b", "w_up",
                                "w_down", "ln2_g", "ln2_b", "w_gate", "w_ple", "ln3_g", "ln3_b")},
        **shape_constants(), **attention_constants(),
    }
    arrays = {k: np.ascontiguousarray(v) for k, v in arrays.items()}
    nc = bacc.Bacc("TRN2", target_bir_lowering=False, num_devices=1)
    io = {k: nc.dram_tensor("in_" + k, v.shape, mybir.dt.from_np(v.dtype), kind="ExternalInput").ap() for k, v in arrays.items()}
    io.update({k: nc.dram_tensor("out_" + k, shape, F32, kind="ExternalOutput").ap() for k, shape in OUTPUTS.items()})
    build(nc, io)
    result = run_bass_kernel_spmd(nc, [{"in_" + k: v for k, v in arrays.items()}], core_ids=[0]).results[0]
    y, k, v, conv, ssm_p, ssm_s = (np.asarray(result["out_" + n]) for n in OUTPUTS)
    conv = conv.transpose(2, 1, 0).reshape(-1, CD)
    return (y[:SEQ].reshape(1, SEQ, D), y[SEQ:].reshape(DB, DT, D),
            k[:SEQ].reshape(1, 1, SEQ, NH, HD), v[:SEQ].reshape(1, 1, SEQ, NH, HD),
            k[SEQ:].reshape(1, DB, DT, NH, HD), v[SEQ:].reshape(1, DB, DT, NH, HD),
            conv[:CW - 1].reshape(1, 1, CW - 1, CD), conv[CW - 1:].reshape(1, DB, CW - 1, CD),
            ssm_p.T.reshape(1, 1, NH, HD, NSTATE), ssm_s.transpose(1, 2, 0).reshape(1, DB, NH, HD, NSTATE))
```

```python
from contextlib import ExitStack

import concourse.bass as bass
import numpy as np
from concourse import mybir

F32 = mybir.dt.float32
F32R = mybir.dt.float32r
ALU = mybir.AluOpType
ACT = mybir.ActivationFunctionType
AX = mybir.AxisListType
ds = bass.ds

P = 128
D = 1024
KD = D // P
SEQ = 1024
NQB = SEQ // P
DB, DT = 8, 8
NS = DB * DT
TOK = SEQ + NS
NB = NQB + 1
PAST = 1024
HD = 64
NH = 8
DA = NH * HD
NPAIR = DA // P
NSTATE = 128
NGROUP = 2
HPG = NH // NGROUP
CW = 4
CD = DA + 2 * NGROUP * NSTATE
NXBC = CD // P
DIN = 3 * DA + DA + CD + NH
DFF = 4 * D
DPLE = 256
KPLE = DPLE // P
EPS = 1e-5
ALPHA = 2.0 ** 0.25
BRANCHES = ((128, 1), (512, 4), (2048, 16))
NEG = -1e30

GROUPS = [(0, 364), (364, 364), (728, 360)]

SBUF_START = 16512


class Place:

    def __init__(self, nc, offset, limit=None, then=None):
        self.nc, self.offset, self.limit, self.then = nc, offset, limit, then

    def __call__(self, name, shape, dtype=F32):
        size = 4 * int(np.prod(shape[1:]))
        if self.limit is not None and self.offset + size > self.limit:
            self.offset, self.limit = self.then, None
        t = self.nc.alloc_sbuf_tensor_at(name, list(shape), dtype, offset=self.offset)
        self.offset += -(-size // 32) * 32
        return t


def nothing(*step):
    pass


def take_statistics(dve, out, last_count, done, value):
    dve.wait_ge(done, value)
    dve.tensor_copy(out, last_count)


def w_raw_view(w, col, n):
    return w[:, ds(col, n)].rearrange("(k p) n -> p k n", p=P)


class LayerNorm:

    def __init__(self, sem, place, tag):
        self.G, self.B = place(tag + "_g", [P, D]), place(tag + "_b", [P, D])
        self.bn, self.mv = place(tag + "_bn", [P, 2, 2, 6]), place(tag + "_mv", [P, 2, 2])
        self.veps, self.rstd, self.nmr = (place(f"{tag}_{n}", [P, 2, 1]) for n in ("veps", "rstd", "nmr"))
        self.mhalf, self.eps, self.taken = (place(f"{tag}_{n}", [P, 1]) for n in ("mhalf", "eps", "taken"))
        self.loaded, self.const_set = sem(tag + "_loaded"), sem(tag + "_const_set")
        two = lambda n: [sem(f"{tag}_{n}{s}") for s in range(2)]
        self.bn_done, self.mv_done, self.veps_done, self.rstd_done, self.nmr_done, self.xn_done, self.gain_done, self.done = (
            two(n) for n in ("bn_done", "mv_done", "veps_done", "rstd_done", "nmr_done", "xn_done", "gain_done", "done"))

    def load(self, sp, g, b):
        sp.dma_start(self.G[:, :], g.partition_broadcast(P)).then_inc(self.loaded, 16)
        sp.dma_start(self.B[:, :], b.partition_broadcast(P)).then_inc(self.loaded, 16)

    def constants(self, pool):
        pool.memset(self.mhalf[:, :], -0.5).then_inc(self.const_set, 1)
        pool.memset(self.eps[:, :], EPS).then_inc(self.const_set, 1)
        pool.wait_ge(self.const_set, 2)
        pool.wait_ge(self.loaded, 32)

    def statistics(self, dve, x, s, i, r):
        half = D // 2
        dve.bn_stats(self.bn[0:r, s, 0, :], x[:, 0:half])
        dve.bn_stats(self.bn[0:r, s, 1, :], x[:, half:D]).then_inc(self.bn_done[s], 1)
        take_statistics(dve, self.taken[0:r, :], self.bn[0:r, s, 1, 0:1], self.bn_done[s], i + 1)
        dve.bn_aggr(self.mv[0:r, s, :], self.bn[0:r, s, :, :]).then_inc(self.mv_done[s], 1)

    def inverse_root(self, pool, s, i, r):
        pool.wait_ge(self.mv_done[s], i + 1)
        pool.tensor_tensor(self.veps[0:r, s, :], self.mv[0:r, s, 1:2], self.eps[0:r, :], ALU.add).then_inc(self.veps_done[s], 1)
        pool.wait_ge(self.veps_done[s], i + 1)
        pool.tensor_tensor(self.rstd[0:r, s, :], self.veps[0:r, s, :], self.mhalf[0:r, :], ALU.pow).then_inc(self.rstd_done[s], 1)

    def shift(self, dve, s, i, r):
        dve.wait_ge(self.rstd_done[s], i + 1)
        dve.tensor_scalar(self.nmr[0:r, s, :], self.mv[0:r, s, 0:1], self.rstd[0:r, s, :], -1.0, ALU.mult,
                          ALU.mult).then_inc(self.nmr_done[s], 1)

    def normalise(self, act, out, x, s, i, r):
        act.wait_ge(self.nmr_done[s], i + 1)
        act.activation(out, x, ACT.Identity, bias=self.nmr[0:r, s, :], scale=self.rstd[0:r, s, :]).then_inc(self.xn_done[s], 1)

    def gain(self, pool, x, s, i, r):
        pool.wait_ge(self.xn_done[s], i + 1)
        pool.tensor_tensor(x, x, self.G[0:r, :], ALU.mult).then_inc(self.gain_done[s], 1)

    def bias(self, dve, x, s, i, r):
        dve.wait_ge(self.gain_done[s], i + 1)
        dve.tensor_tensor(x, x, self.B[0:r, :], ALU.add).then_inc(self.done[s], 1)


def over_blocks(engine, *parts):
    def step(n, i=None):
        for lead, f in parts:
            m = n + lead
            if i is not None:
                f(m % 2, i + m // 2, P, i * 2 + m)
            elif 0 <= m < NB:
                f(m % 2, m // 2, NS if m == NB - 1 else P, m)

    leads = [lead for lead, _ in parts]
    at = 2 - min(leads)
    rounds = (NB - 1 - max(leads) - at) // 2
    for n in range(-max(leads), at):
        step(n)
    if rounds > 1:
        with engine.Fori(0, rounds) as i:
            step(at, i)
            step(at + 1, i)
        at += 2 * rounds
    for n in range(at, NB - min(leads)):
        step(n)


def stage_input_norm(nc, sem, io, ident, hT_hi, hT_lo, weights, place):
    X, H = place("in_x", [P, 2, D]), place("in_h", [P, 2, D])
    ln = LayerNorm(sem, place, "in_ln")
    names = "x_loaded stored t_done hi_done lo_done".split()
    S = {n: [sem(f"in_{n}{s}") for s in range(2)] for n in names}
    with ExitStack() as ctx:
        T = ctx.enter_context(nc.psum_tensor("in_T", [P, 2, KD, P], F32))
        block = ctx.enter_context(nc.Block())

        @block.sync
        def _(sp):
            def load(s, i, r, n):
                sp.wait_ge(ln.xn_done[s], i)
                src = io["x_sample"] if r == NS else io["x_prompt"][ds(n * P, P), :]
                sp.dma_start(X[0:r, s, :], src).then_inc(S["x_loaded"][s], 16)
                if isinstance(n, int) and n == 1:
                    ln.load(sp, io["ln_in_g"], io["ln_in_b"])
                    for m in range(2):
                        weights.load(sp, m)

            def store(s, i, r, n):
                sp.wait_ge(ln.done[s], i + 1)
                sp.dma_start(io["h0"][ds(n * P, r), :], H[0:r, s, :]).then_inc(S["stored"][s], 16)

            over_blocks(sp, (2, load), (0, store))
            sp.wait_ge(S["stored"][0], 16 * (NQB // 2 + 1))
            sp.wait_ge(S["stored"][1], 16 * (NQB // 2))

        @block.gpsimd
        def _(pool):
            ln.constants(pool)

            def norm(s, i, r, n):
                ln.inverse_root(pool, s, i, r)
                ln.gain(pool, H[0:r, s, :], s, i, r)

            over_blocks(pool, (0, norm))

        @block.vector
        def _(dve):
            def statistics(s, i, r, n):
                dve.wait_ge(S["x_loaded"][s], i * 16 + 16)
                ln.statistics(dve, X[0:r, s, :], s, i, r)

            def lo(s, i, r, n):
                dve.wait_ge(S["hi_done"][s], i + 1)
                dve.tensor_tensor(hT_lo[:, :, ds(n * P, r)], T[:, s, :, 0:r], hT_hi[:, :, ds(n * P, r)].bitcast(F32),
                                  ALU.subtract).then_inc(S["lo_done"][s], 1)

            over_blocks(dve, (2, statistics), (0, lo), (2, lambda s, i, r, n: ln.shift(dve, s, i, r)),
                        (1, lambda s, i, r, n: ln.bias(dve, H[0:r, s, :], s, i, r)))
            for m in range(2):
                weights.split_lo(dve, m)

        @block.scalar
        def _(act):
            def normalise(s, i, r, n):
                act.wait_ge(S["t_done"][s], i)
                act.wait_ge(S["stored"][s], i * 16)
                ln.normalise(act, H[0:r, s, :], X[0:r, s, :], s, i, r)

            def hi(s, i, r, n):
                act.wait_ge(S["t_done"][s], i + 1)
                act.activation(hT_hi[:, :, ds(n * P, r)], T[:, s, :, 0:r], ACT.Copy).then_inc(S["hi_done"][s], 1)

            over_blocks(act, (2, normalise), (1, hi))
            for m in range(2):
                weights.split_hi(act, m)

        @block.tensor
        def _(pe):
            def turn(s, i, r, n):
                pe.wait_ge(ln.done[s], i + 1)
                pe.wait_ge(S["lo_done"][s], i)
                for k in range(KD):
                    last = pe.transpose(T[:, s, k, 0:r], H[0:r, s, k * P:(k + 1) * P], ident[0:r, 0:r])
                last.then_inc(S["t_done"][s], 1)

            over_blocks(pe, (0, turn))


class ProjectionWeights:

    def __init__(self, sem, place, w_in):
        self.w_in = w_in
        self.raw = place("pj_raw", [P, 2, KD, P])
        self.hi = [place(f"pj_w_hi{s}", [P, KD, P], F32R) for s in range(2)]
        self.lo = [place(f"pj_w_lo{s}", [P, KD, P], F32R) for s in range(2)]
        self.loaded, self.hi_done, self.lo_done, self.used = (
            [sem(f"pj_w_{n}{s}") for s in range(2)] for n in ("loaded", "hi_done", "lo_done", "used"))

    def load(self, sp, m, i=0):
        s = m % 2
        sp.wait_ge(self.lo_done[s], i + m // 2)
        col = DIN - P if m == 0 else i * (2 * P) + (m - 1) * P
        sp.dma_start(self.raw[:, s, :, :], w_raw_view(self.w_in, col, P)).then_inc(self.loaded[s], 16)

    def split_hi(self, act, m, i=0):
        s = m % 2
        act.wait_ge(self.loaded[s], i * 16 + 16 * (m // 2 + 1))
        act.wait_ge(self.used[s], i + m // 2)
        act.activation(self.hi[s][:, :, :], self.raw[:, s, :, :], ACT.Copy).then_inc(self.hi_done[s], 1)

    def split_lo(self, dve, m, i=0):
        s = m % 2
        dve.wait_ge(self.hi_done[s], i + (m // 2 + 1))
        dve.tensor_tensor(self.lo[s][:, :, :], self.raw[:, s, :, :], self.hi[s][:, :, :].bitcast(F32),
                          ALU.subtract).then_inc(self.lo_done[s], 1)


def stage_projection(nc, sem, io, ident, hT_hi, hT_lo, weights, qT, kT, Xt, Bt, BT, CT, dt_raw, place):
    KINDS = ["dt"] + ["q"] * 4 + ["k"] * 4 + ["v"] * 4 + ["z"] * 4 + ["x"] * 4 + ["B"] * 2 + ["C"] * 2
    NBLK = len(KINDS)
    TURNED = ("dt", "k", "v", "z", "x", "B")
    STORED = ("k", "v", "z")
    CONV = ("x", "B", "C")
    COPIED = ("k", "B")
    LAST = CW - 1
    TAIL = LAST * (1 + DB)

    def before(n, kinds):
        return 1 + sum(KINDS[m] in kinds for m in range(n % 2, n, 2))

    def turned_before(n):
        return sum(KINDS[m] in TURNED for m in range(n))

    w_hi, w_lo, lo_done, mm_done = weights.hi, weights.lo, weights.lo_done, weights.used
    fT = place("pj_fT", [P, 2, TOK])
    SX = LAST + SEQ
    cv = place("pj_cv", [P, 2, SX + DB * (LAST + DT)])
    cc = place("pj_cc", [P, 2, TOK])
    stage = place("pj_stage", [P, 2, NB, P])
    conv_w = place("pj_conv_w", [P, NXBC, CW])
    conv_b = place("pj_conv_b", [P, NXBC])
    stateT = place("pj_stateT", [P, NXBC, DB * LAST])
    tail = place("pj_tail", [P, NXBC, TAIL])

    small_loaded, tail_stored, tcopy_done = sem("pj_small_loaded"), sem("pj_tail_stored"), sem("pj_tcopy_done")
    pad_set, v_chain = sem("pj_pad_set"), sem("pj_v_chain")
    two = lambda name: [sem(f"pj_{name}{s}") for s in range(2)]
    ev_done, t_done, stored, kept, conv_done, silu_done = two("ev_done"), two("t_done"), two("stored"), two("kept"), two("conv_done"), two("silu_done")
    tail_done, fill_done, tap = two("tail_done"), two("fill_done"), two("tap")

    def sample_view(ap, width):
        return ap.rearrange("p (b t) -> p b t", t=width)

    with ExitStack() as ctx:
        mm = ctx.enter_context(nc.psum_tensor("pj_mm", [P, 2, 3, 512], F32))
        T = ctx.enter_context(nc.psum_tensor("pj_T", [P, NQB, P], F32))
        Ts = [mm[0:NS, s, 2, 384:384 + P] for s in range(2)]
        block = ctx.enter_context(nc.Block())

        def steps(engine, step):
            n = 0
            while n < NBLK:
                if KINDS[n:n + 4] == [KINDS[n]] * 4:
                    with engine.Fori(0, 2) as i:
                        for u in range(2):
                            step(n + u, i, i * 2 + u)
                    n += 4
                else:
                    step(n, 0, n - KINDS.index(KINDS[n]))
                    n += 1

        @block.sync
        def _(sp):
            for s in range(2):
                for counted in (t_done, kept, conv_done, silu_done, tail_done, fill_done):
                    sp.sem_inc(counted[s], 1)
                sp.sem_inc(stored[s], 32)
            sp.dma_start(conv_w[:, :, :], io["conv_wT"]).then_inc(small_loaded, 16)
            sp.dma_start(conv_b[:, :], io["conv_bT"]).then_inc(small_loaded, 16)
            sp.dma_start(stateT[:, :, :], io["state_convT"]).then_inc(small_loaded, 16)
            weights.load(sp, 2)

            def step(n, i, j):
                if n + 3 < NBLK:
                    weights.load(sp, n + 3, i)
                if KINDS[n] in STORED:
                    s = n % 2
                    to = io[{"k": "new_k", "v": "new_v", "z": "z_act"}[KINDS[n]]]
                    sp.wait_ge(tcopy_done, i * 2 + (turned_before(n) + 1))
                    sp.dma_start(to[0:SEQ, ds(j * P, P)].rearrange("(b p) f -> p b f", p=P),
                                 stage[:, s, 0:NQB, :]).then_inc(stored[s], 16)
                    sp.dma_start(to[SEQ:TOK, ds(j * P, P)], stage[0:NS, s, NQB, :]).then_inc(stored[s], 16)

            steps(sp, step)
            for s in range(2):
                sp.wait_ge(tail_done[s], NXBC // 2 + 1)
            sp.dma_start(io["new_convT"], tail[:, :, :]).then_inc(tail_stored, 16)
            sp.wait_ge(tail_stored, 16)
            for s in range(2):
                sp.wait_ge(stored[s], 32 * (len([k for k in KINDS if k in STORED]) // 2 + 1))

        @block.scalar
        def _(act):
            def step(n, i, j):
                s, kind = n % 2, KINDS[n]
                if n + 2 < NBLK:
                    weights.split_hi(act, n + 2, i)
                act.wait_ge(mm_done[s], i + (n // 2 + 1))
                fT_free = kind in TURNED
                if kind in CONV:
                    act.wait_ge(conv_done[s], i + before(n, CONV))
                    act.wait_ge(tail_done[s], i + before(n, CONV))
                elif fT_free:
                    act.wait_ge(t_done[s], i + before(n, TURNED))
                    act.wait_ge(kept[s], i + before(n, COPIED) if kind == "k" else before(n, COPIED))
                for g, (c, w) in enumerate(GROUPS):
                    w_prompt = min(w, SEQ - c)
                    if kind in CONV:
                        last = act.activation(cv[:, s, LAST + c:LAST + c + w_prompt], mm[:, s, g, 0:w_prompt], ACT.Copy)
                        if w_prompt < w:
                            last = act.activation(sample_view(cv[:, s, SX:], LAST + DT)[:, :, LAST:],
                                                  sample_view(mm[:, s, g, w_prompt:w], DT), ACT.Copy)
                    else:
                        to = qT[:, ds(j, 1), c:c + w].squeeze(1) if kind == "q" else fT[:, s, c:c + w]
                        last = act.activation(to, mm[:, s, g, 0:w], ACT.Copy)
                last.then_inc(ev_done[s], 1)
                if kind == "z":
                    act.wait_ge(t_done[s], i + (before(n, TURNED) + 1))
                    act.wait_ge(stored[s], i * 32 + 32 * before(n, STORED))
                    act.activation(stage[:, s, 0:NQB, :], T[:, :, :], ACT.Silu)
                    act.activation(stage[0:NS, s, NQB, :], Ts[s], ACT.Silu).then_inc(tcopy_done, 1)
                if kind in CONV:
                    act.wait_ge(conv_done[s], i + (before(n, CONV) + 1))
                    if kind != "C":
                        act.wait_ge(t_done[s], i + before(n, TURNED))
                        act.wait_ge(kept[s], before(n, COPIED))
                    to = CT[:, j, :] if kind == "C" else fT[:, s, :]
                    act.activation(to, cc[:, s, :], ACT.Silu).then_inc(silu_done[s], 1)

            steps(act, step)

        @block.gpsimd
        def _(pool):
            for s in range(2):
                pool.memset(cv[:, s, 0:LAST], 0.0).then_inc(pad_set, 1)
            pool.wait_ge(small_loaded, 48)

            def step(n, i, j):
                s, kind = n % 2, KINDS[n]
                if kind in CONV:
                    jx = n + 2 * 0 - KINDS.index("x")
                    jx = j if kind == "x" else jx
                    pool.wait_ge(conv_done[s], i + before(n, CONV))
                    pool.tensor_copy(sample_view(cv[:, s, SX:], LAST + DT)[:, :, 0:LAST],
                                     sample_view(stateT[:, ds(jx, 1), :].squeeze(1), LAST)).then_inc(fill_done[s], 1)
                    pool.wait_ge(ev_done[s], i + (n // 2 + 1))
                    pool.tensor_copy(tail[:, ds(jx, 1), 0:LAST].squeeze(1), cv[:, s, SEQ:SEQ + LAST])
                    pool.tensor_copy(sample_view(tail[:, ds(jx, 1), LAST:].squeeze(1), LAST),
                                     sample_view(cv[:, s, SX:], LAST + DT)[:, :, DT:]).then_inc(tail_done[s], 1)
                if kind == "k":
                    pool.wait_ge(ev_done[s], i + (n // 2 + 1))
                    pool.tensor_copy(kT[:, ds(j, 1), :].squeeze(1), fT[:, s, :]).then_inc(kept[s], 1)
                if kind == "B":
                    pool.wait_ge(silu_done[s], before(n, CONV) + 1)
                    pool.tensor_copy(BT[:, j, :], fT[:, s, :]).then_inc(kept[s], 1)

            steps(pool, step)

        @block.vector
        def _(dve):
            def step(n, i, j):
                s, kind = n % 2, KINDS[n]
                if n + 2 < NBLK:
                    weights.split_lo(dve, n + 2, i)
                if kind in CONV:
                    jx = j if kind == "x" else n - KINDS.index("x")
                    dve.wait_ge(ev_done[s], i + (n // 2 + 1))
                    dve.wait_ge(fill_done[s], i + (before(n, CONV) + 1))
                    dve.wait_ge(silu_done[s], i + before(n, CONV))
                    base = i * LAST + LAST * (before(n, CONV) - 1)
                    for t in range(CW):
                        cw = conv_w[:, ds(jx, 1), t:t + 1].squeeze(1)
                        src = cv[:, s, t:t + SEQ]
                        src_s = sample_view(cv[:, s, SX:], LAST + DT)[:, :, t:t + DT]
                        out, out_s = cc[:, s, 0:SEQ], sample_view(cc[:, s, SEQ:], DT)
                        if t == 0:
                            cb = conv_b[:, ds(jx, 1)]
                            dve.tensor_scalar(out, src, cw, cb, ALU.mult, ALU.add)
                            dve.tensor_scalar(out_s, src_s, cw, cb, ALU.mult, ALU.add).then_inc(tap[s], 1)
                        else:
                            dve.wait_ge(tap[s], base + t)
                            dve.scalar_tensor_tensor(out, src, cw, out, ALU.mult, ALU.add)
                            last = dve.scalar_tensor_tensor(out_s, src_s, cw, out_s, ALU.mult, ALU.add)
                            last.then_inc(tap[s] if t < CW - 1 else conv_done[s], 1)
                if kind in TURNED and kind != "z":
                    dve.wait_ge(t_done[s], i + (before(n, TURNED) + 1))
                    if kind in STORED:
                        dve.wait_ge(stored[s], i * 32 + 32 * before(n, STORED))
                        to, to_s = stage[:, s, 0:NQB, :], stage[0:NS, s, NQB, :]
                    elif kind == "x":
                        to = Xt[:, 0:NQB, ds(j * P, P)]
                        to_s = Xt[0:NS, NQB, ds(j * P, P)]
                    elif kind == "B":
                        to, to_s = Bt[:, 0:NQB, j * P:(j + 1) * P], Bt[0:NS, NQB, j * P:(j + 1) * P]
                    else:
                        to, to_s = dt_raw[:, 0:NQB, :], dt_raw[0:NS, NQB, :]
                    c = P - NH if kind == "dt" else 0
                    dve.tensor_copy(to, T[:, :, c:])
                    dve.tensor_copy(to_s, Ts[s][:, c:]).then_inc(tcopy_done, 1)

            dve.wait_ge(small_loaded, 48)
            dve.wait_ge(pad_set, 2)
            steps(dve, step)

        @block.tensor
        def _(pe):
            def product(n, i, turned=0):
                s = n % 2
                pe.wait_ge(lo_done[s], i + (n // 2 + 1))
                pe.wait_ge(ev_done[s], i + n // 2)
                for g, (c, w) in enumerate(GROUPS):
                    if g == len(GROUPS) - 1:
                        pe.wait_ge(tcopy_done, turned)
                    for k in range(KD):
                        for part, (wt, ht) in enumerate(((w_hi, hT_hi), (w_hi, hT_lo), (w_lo, hT_hi))):
                            last = pe.matmul(mm[:, s, g, 0:w], wt[s][:, k, :], ht[:, k, c:c + w],
                                             start=(k == 0 and part == 0), stop=(k == KD - 1 and part == 2))
                last.then_inc(mm_done[s], 1)

            def step(n, i, j):
                s, kind = n % 2, KINDS[n]
                if n + 1 < NBLK:
                    product(n + 1, i, turned_before(n) + (i * 2 if kind in TURNED and not isinstance(i, int) else 0))
                if kind in TURNED:
                    if kind in CONV:
                        pe.wait_ge(silu_done[s], i + (before(n, CONV) + 1))
                    else:
                        pe.wait_ge(ev_done[s], i + (n // 2 + 1))
                    pe.wait_ge(tcopy_done, i * 2 + turned_before(n))
                    for b in range(NQB):
                        pe.transpose(T[:, b, :], fT[:, s, b * P:(b + 1) * P], ident[:, :])
                    pe.transpose(Ts[s], fT[:, s, SEQ:TOK], ident[:, :]).then_inc(t_done[s], 1)

            product(0, 0)
            steps(pe, step)
def stage_ssd(nc, sem, io, consts, Xt, Bt, BT, CT, dt_raw, mixT, place):
    ident = consts["ident"]
    GW = DA // NGROUP
    C_ALL = NB * NH
    PC = NQB * NH

    def sb(name, shape):
        return place("sd_" + name, shape)

    ones, mask, mask_s, ones_s, in_seq = (sb("ones", [P, P]), sb("mask", [P, P]), sb("mask_s", [NS, NS]),
                                          sb("ones_s", [NS, NS]), sb("in_seq", [NS, DB]))
    tri, tri_s = sb("tri", [P, P]), sb("tri_s", [NS, NS])
    bias, a_log, skip, norm_w = sb("bias", [P, NH]), sb("a_log", [P, NH]), sb("skip", [P, NH]), sb("norm_w", [P, DA])
    d, ab, ex, dt, adt, ea = (sb(n, [P, C_ALL]) for n in ("d", "ab", "ex", "dt", "adt", "ea"))
    acs, rest, decay, eacs, etot = (sb(n, [P, C_ALL]) for n in ("acs", "rest", "decay", "eacs", "etot"))
    adt_b, etot_s = sb("adt_b", [NS, DB, NH]), sb("etot_s", [P, DB * NH])
    mhalf = sb("mhalf", [P, NGROUP])
    state = sb("state", [P, DA])
    state_s = sb("state_s", [P, DB, DA])
    E = sb("E", [P, 2, NH, P])
    xdt, xdd, xsk, zt, Y = (sb(n, [P, 2, DA]) for n in ("xdt", "xdd", "xsk", "zt", "Y"))
    off, junk, off_junk = sb("off", [P, DA]), sb("junk", [P, GW]), sb("junk2", [P, GW])
    BTs, CTs, Bts = (sb(n, [P, 2, NGROUP, P]) for n in ("BTs", "CTs", "Bts"))
    adts = sb("adts", [P, 2, NH])
    Cz = sb("Cz", [P, NGROUP, DB * (NS + DT)])
    Bz = sb("Bz", [NS, DB, GW])
    ssq, ms, rs = sb("ssq", [P, 2, NGROUP]), sb("ms", [P, 2, NGROUP]), sb("rs", [P, 2, NGROUP])

    names = ("loaded state_loaded zeroed pad_set pre adt_ready sums_done acs_ready decay_ready cz_ready bz_ready staged staged2 x_ready gr_done z_done "
             "e_done m_done y_mm o_mm s_mm off_done st_scaled st_done y1_done xsk_done y2_done y3_done ssq_done "
             "ms_done rs_done yn_done yw_done t_mm ty_done st_out").split()
    S = {n: sem("sd_" + n) for n in names}
    z_loaded = [sem(f"sd_z_loaded{s}") for s in range(2)]
    heads = lambda ap: ap.rearrange("p (h f) -> p h f", f=HD)

    def chunk_cols(t, c):
        return t[:, c * NH:(c + 1) * NH] if isinstance(c, int) else t[:, ds(c * NH, NH)]

    def per_head(ap, r):
        return ap[0:r].unsqueeze(2).to_broadcast([r, NH, HD])

    def wait(engine, name, value):
        if not isinstance(value, int) or value > 0:
            engine.wait_ge(S[name], value)

    def steps(front, back, turn):
        front(0, 0)
        front(1, 1)
        back(0, 0)

        def body(i):
            for u in range(2):
                front(i * 2 + (2 + u), u)
                back(i * 2 + (1 + u), 1 - u)
                turn(i * 2 + u, u)
        return body, lambda: (back(NQB - 1, 1), turn(NQB - 2, 0), turn(NQB - 1, 1))

    def run(engine, front, back, turn, straight=False):
        body, end = steps(front, back, turn)
        body(0)
        if straight:
            for i in range(1, NQB // 2 - 1):
                body(i)
        else:
            with engine.Fori(1, NQB // 2 - 1) as i:
                body(i)
        end()
        front(NQB, 0)
        back(NQB, 0)
        turn(NQB, 0)

    nothing = lambda *a: None
    is_sample = lambda c: isinstance(c, int) and c == NQB

    with ExitStack() as ctx:
        G = [ctx.enter_context(nc.psum_tensor(f"sd_G{s}", [P, NGROUP, P], F32)) for s in range(2)]
        R = ctx.enter_context(nc.psum_tensor("sd_R", [P, NH, P], F32))
        pY = ctx.enter_context(nc.psum_tensor("sd_pY", [P, DA], F32))
        pO = ctx.enter_context(nc.psum_tensor("sd_pO", [P, DA], F32))
        pS = ctx.enter_context(nc.psum_tensor("sd_pS", [P, DA], F32))
        added = [pS[:, :]] + [R[:, 4 * k:4 * k + 4, :].rearrange("p a b -> p (a b)") for k in range(2)]
        pT = ctx.enter_context(nc.psum_tensor("sd_pT", [P, NPAIR, P], F32))
        block = ctx.enter_context(nc.Block())

        @block.sync
        def _(sp):
            loads = [(ones, consts["ones_d"]), (mask, consts["mask_d"]), (mask_s, consts["mask_s_d"]),
                     (ones_s, consts["ones_s_d"]), (in_seq, consts["in_seq_d"]), (tri, consts["tri_d"]),
                     (tri_s, consts["tri_s_d"])]
            for t, src in loads:
                sp.dma_start(t[:, :], src).then_inc(S["loaded"], 16)
            for t, name in ((bias, "dt_bias"), (a_log, "a_log"), (skip, "d_skip"), (norm_w, "ssd_norm_w")):
                sp.dma_start(t[:, :], io[name].partition_broadcast(P)).then_inc(S["loaded"], 16)
            sp.dma_start(state_s[:, :, :], io["state_ssmT"]).then_inc(S["state_loaded"], 16)

            def front(c, s):
                wait(sp, "y3_done", c - 1)
                rows = NS if is_sample(c) else P
                sp.dma_start(zt[0:rows, s, :], io["z_act"][ds(c * P, rows), :]).then_inc(z_loaded[s], 16)

            run(sp, front, nothing, nothing)
            wait(sp, "st_done", NQB)
            sp.dma_start(io["new_ssm_promptT"], state[:, :]).then_inc(S["st_out"], 16)
            wait(sp, "st_done", NQB + DB)
            sp.dma_start(io["new_ssm_sampleT"], state_s[:, :, :]).then_inc(S["st_out"], 16)
            wait(sp, "st_out", 32)

        @block.gpsimd
        def _(pool):
            pool.memset(mhalf[:, :], -0.5).then_inc(S["pad_set"], 1)
            pool.memset(state[:, :], 0.0).then_inc(S["zeroed"], 1)
            pool.memset(Cz[:, :, :], 0.0).then_inc(S["pad_set"], 1)
            wait(pool, "pad_set", 3)
            for g in range(NGROUP):
                last = pool.tensor_copy(Cz[:, g, :].rearrange("p (b t) -> p b t", t=NS + DT)[:, :, 0:DT],
                                        CT[:, g, SEQ:TOK].rearrange("p (b t) -> p b t", t=DT))
            last.then_inc(S["cz_ready"], 1)
            wait(pool, "loaded", 176)

            def stage_first(c, s):
                wait(pool, "gr_done", c - 1)
                pool.tensor_copy(BTs[:, s, :, :], BT[:, :, ds(c * P, P)])
                pool.tensor_copy(adts[:, s, :], chunk_cols(adt, c)).then_inc(S["staged"], 1)

            def stage_second(c, s):
                wait(pool, "s_mm", c - 1)
                pool.tensor_copy(CTs[:, s, :, :], CT[:, :, ds(c * P, P)])
                pool.tensor_copy(Bts[:, s, :, :], Bt[:, ds(c, 1), :].squeeze(1).rearrange("p (g n) -> p g n", n=P))\
                    .then_inc(S["staged2"], 1)

            def front(c, s):
                if is_sample(c):
                    return
                if c == 0:
                    wait(pool, "adt_ready", 1)
                    stage_first(0, 0)
                if c + 1 < NQB:
                    stage_first(c + 1, 1 - s)
                stage_second(c, s)

            def back(c, s):
                r = NS if is_sample(c) else P
                x = Xt[0:r, ds(c, 1), :].squeeze(1)
                wait(pool, "y2_done", c - 1)
                pool.tensor_tensor(heads(xsk[0:r, s, :]), heads(x), per_head(skip, r), ALU.mult).then_inc(S["xsk_done"], 1)

            def gate(c, s):
                r = NS if is_sample(c) else P
                wait(pool, "y1_done", c + 1)
                wait(pool, "xsk_done", c + 1)
                pool.tensor_tensor(Y[0:r, s, :], Y[0:r, s, :], xsk[0:r, s, :], ALU.add).then_inc(S["y2_done"], 1)
                wait(pool, "y2_done", c + 1)
                pool.wait_ge(z_loaded[s], 16 + 16 * (NQB // 2) if is_sample(c) else 16 * (c // 2 + 1) if isinstance(c, int)
                             else (c - s) * 8 + 16)
                pool.tensor_tensor(Y[0:r, s, :], Y[0:r, s, :], zt[0:r, s, :], ALU.mult).then_inc(S["y3_done"], 1)
                wait(pool, "pad_set", 3)
                wait(pool, "ssq_done", c + 1)
                pool.tensor_scalar(ms[0:r, s, :], ssq[0:r, s, :], 1.0 / GW, EPS, ALU.mult, ALU.add).then_inc(S["ms_done"], 1)
                wait(pool, "ms_done", c + 1)
                pool.tensor_tensor(rs[0:r, s, :], ms[0:r, s, :], mhalf[0:r, :], ALU.pow).then_inc(S["rs_done"], 1)
                wait(pool, "yn_done", c + 1)
                pool.tensor_tensor(Y[0:r, s, :], Y[0:r, s, :], norm_w[0:r, :], ALU.mult).then_inc(S["yw_done"], 1)

            run(pool, front, back, gate, straight=True)

        @block.vector
        def _(dve):
            dve.memset(dt_raw[NS:P, NQB, :], 0.0).then_inc(S["pad_set"], 1)
            wait(dve, "loaded", 176)
            wait(dve, "pad_set", 3)
            by_chunk = lambda t: t[:, :].rearrange("p (c h) -> p c h", h=NH)
            over_chunks = lambda t: t[:, 0:NH].unsqueeze(1).to_broadcast([P, NB, NH])
            dve.tensor_tensor(by_chunk(d), dt_raw[:, :, :], over_chunks(bias), ALU.add).then_inc(S["pre"], 1)
            wait(dve, "pre", 5)
            dve.scalar_tensor_tensor(dt[:, :], d[:, :], 0.0, ex[:, :], ALU.max, ALU.add).then_inc(S["pre"], 1)
            wait(dve, "pre", 6)
            dve.scalar_tensor_tensor(by_chunk(adt), by_chunk(dt), -1.0, over_chunks(ea), ALU.mult,
                                     ALU.mult).then_inc(S["adt_ready"], 1)
            wait(dve, "adt_ready", 1)
            dve.tensor_tensor(adt_b[:, :, :], adt[0:NS, PC:].unsqueeze(1).to_broadcast([NS, DB, NH]),
                              in_seq[:, :].unsqueeze(2).to_broadcast([NS, DB, NH]), ALU.mult).then_inc(S["adt_ready"], 1)
            for b in range(DB):
                last = dve.tensor_scalar(Bz[:, b, :], Bt[0:NS, NQB, :], in_seq[:, b:b + 1], None, ALU.mult)
            last.then_inc(S["bz_ready"], 1)
            wait(dve, "sums_done", 1)
            dve.tensor_copy(acs[:, 0:PC], pY[:, 0:PC])
            dve.tensor_copy(acs[0:NS, PC:], pY[0:NS, PC:C_ALL]).then_inc(S["acs_ready"], 1)
            wait(dve, "acs_ready", 1)
            dve.tensor_tensor(rest[:, 0:PC], pO[:, 0:PC], acs[:, 0:PC], ALU.subtract)
            dve.tensor_tensor(rest[0:NS, PC:], pO[0:NS, PC:C_ALL], acs[0:NS, PC:], ALU.subtract).then_inc(S["acs_ready"], 1)

            def front(c, s):
                r = NS if is_sample(c) else P
                wait(dve, "gr_done", c + 1)
                m = mask_s if is_sample(c) else mask
                for h in range(NH):
                    last = dve.scalar_tensor_tensor(E[0:r, s, h, 0:r], R[0:r, h, 0:r], chunk_cols(acs, c)[0:r, h:h + 1],
                                                    m[0:r, 0:r], ALU.subtract, ALU.add)
                last.then_inc(S["z_done"], 1)
                wait(dve, "decay_ready", 1)
                wait(dve, "s_mm", c - 1)
                x = Xt[0:r, ds(c, 1), :].squeeze(1)
                dve.tensor_tensor(heads(xdt[0:r, s, :]), heads(x), per_head(chunk_cols(dt, c), r),
                                  ALU.mult).then_inc(S["x_ready"], 1)
                dve.wait_ge(S["x_ready"], c * 2 + 1)
                dve.tensor_tensor(heads(xdd[0:r, s, :]), heads(xdt[0:r, s, :]), per_head(chunk_cols(decay, c), r),
                                  ALU.mult).then_inc(S["x_ready"], 1)
                wait(dve, "e_done", c + 1)
                for g in range(NGROUP):
                    e = E[0:r, s, g * HPG:(g + 1) * HPG, 0:r]
                    last = dve.tensor_tensor(e, e, G[s][0:r, g, 0:r].unsqueeze(1).to_broadcast([r, HPG, r]), ALU.mult)
                last.then_inc(S["m_done"], 1)

            def back(c, s):
                r = NS if is_sample(c) else P
                wait(dve, "o_mm", c + 1)
                wait(dve, "y1_done", c)
                dve.tensor_tensor(heads(off[0:r, :]), heads(pO[0:r, :]), per_head(chunk_cols(eacs, c), r),
                                  ALU.mult).then_inc(S["off_done"], 1)
                if is_sample(c):
                    wait(dve, "state_loaded", 16)
                    dve.tensor_tensor(state_s[:, :, :].rearrange("p b (h f) -> p (b h) f", f=HD),
                                      state_s[:, :, :].rearrange("p b (h f) -> p (b h) f", f=HD),
                                      etot_s[:, :].unsqueeze(2).to_broadcast([P, DB * NH, HD]),
                                      ALU.mult).then_inc(S["st_scaled"], 1)
                    wait(dve, "st_scaled", c + 1)
                    for b in range(DB):
                        wait(dve, "s_mm", c + 1 + b)
                        dve.tensor_tensor(state_s[:, b, :], state_s[:, b, :], added[b % 3], ALU.add).then_inc(S["st_done"], 1)
                else:
                    wait(dve, "zeroed", 1)
                    wait(dve, "st_done", c)
                    dve.tensor_tensor(heads(state[:, :]), heads(state[:, :]), per_head(chunk_cols(etot, c), P),
                                      ALU.mult).then_inc(S["st_scaled"], 1)
                    wait(dve, "st_scaled", c + 1)
                    wait(dve, "s_mm", c + 1)
                    dve.tensor_tensor(state[:, :], state[:, :], pS[:, :], ALU.add).then_inc(S["st_done"], 1)
                wait(dve, "off_done", c + 1)
                wait(dve, "t_mm", c - 1)
                dve.tensor_tensor(Y[0:r, s, :], off[0:r, :], pY[0:r, :], ALU.add).then_inc(S["y1_done"], 1)

            run(dve, front, back, nothing)

        @block.scalar
        def _(act):
            wait(act, "pre", 1)
            act.activation(ab[:, :], d[:, :], ACT.Abs).then_inc(S["pre"], 1)
            wait(act, "pre", 2)
            act.activation(ab[:, :], ab[:, :], ACT.Exp, scale=-1.0).then_inc(S["pre"], 1)
            wait(act, "loaded", 176)
            act.activation(ea[:, 0:NH], a_log[:, :], ACT.Exp).then_inc(S["pre"], 1)
            wait(act, "pre", 4)
            act.activation(ex[:, :], ab[:, :], ACT.Ln, bias=1.0).then_inc(S["pre"], 1)
            wait(act, "acs_ready", 2)
            act.activation(decay[:, 0:PC], rest[:, 0:PC], ACT.Exp)
            act.activation(decay[0:NS, PC:], rest[0:NS, PC:], ACT.Exp)
            act.activation(eacs[:, 0:PC], acs[:, 0:PC], ACT.Exp)
            act.activation(eacs[0:NS, PC:], acs[0:NS, PC:], ACT.Exp)
            act.activation(etot[:, 0:PC], pO[:, 0:PC], ACT.Exp)
            act.activation(etot_s[:, :], pS[:, 0:DB * NH], ACT.Exp).then_inc(S["decay_ready"], 1)

            def front(c, s):
                r = NS if is_sample(c) else P
                wait(act, "z_done", c + 1)
                act.activation(E[0:r, s, :, 0:r], E[0:r, s, :, 0:r], ACT.Exp).then_inc(S["e_done"], 1)

            def turn(c, s):
                r = NS if is_sample(c) else P
                wait(act, "y3_done", c + 1)
                for g in range(NGROUP):
                    wait(act, "ssq_done", c if g == 0 else c)
                    last = act.activation(junk[0:r, :] if g == 0 else off_junk[0:r, :], Y[0:r, s, g * GW:(g + 1) * GW],
                                          ACT.Square, accum_out=ssq[0:r, s, g:g + 1])
                last.then_inc(S["ssq_done"], 1)
                wait(act, "rs_done", c + 1)
                wait(act, "ssq_done", c + 1)
                for g in range(NGROUP):
                    y = Y[0:r, s, g * GW:(g + 1) * GW]
                    last = act.activation(y, y, ACT.Copy, scale=rs[0:r, s, g:g + 1])
                last.then_inc(S["yn_done"], 1)
                wait(act, "t_mm", c + 1)
                act.activation(mixT[:, NPAIR:2 * NPAIR, ds(c * P, r)], pT[:, :, 0:r], ACT.Copy).then_inc(S["ty_done"], 1)

            run(act, front, nothing, turn)

        @block.tensor
        def _(pe):
            wait(pe, "adt_ready", 2)
            wait(pe, "loaded", 176)
            pe.matmul(pY[:, 0:PC], tri[:, :], adt[:, 0:PC], start=True, stop=True)
            pe.matmul(pY[0:NS, PC:C_ALL], tri_s[:, :], adt[0:NS, PC:], start=True, stop=True)
            pe.matmul(pO[:, 0:PC], ones[:, :], adt[:, 0:PC], start=True, stop=True)
            pe.matmul(pO[0:NS, PC:C_ALL], ones_s[:, :], adt[0:NS, PC:], start=True, stop=True)
            pe.matmul(pS[:, 0:DB * NH], ones[0:NS, :], adt_b[:, :, :].rearrange("p b h -> p (b h)"), start=True,
                      stop=True).then_inc(S["sums_done"], 1)

            def front(c, s):
                wait(pe, "m_done", c - 1)
                if is_sample(c):
                    for g in range(NGROUP):
                        pe.matmul(G[s][0:NS, g, 0:NS], BT[:, g, SEQ:TOK], CT[:, g, SEQ:TOK], start=True, stop=True)
                    wait(pe, "z_done", c)
                    for h in range(NH):
                        last = pe.matmul(R[0:NS, h, 0:NS], adt[0:NS, PC + h:PC + h + 1].to_broadcast([NS, NS]), tri_s[:, :],
                                         start=True, stop=True)
                else:
                    wait(pe, "staged", c + 1)
                    for g in range(NGROUP):
                        pe.matmul(G[s][:, g, :], BTs[:, s, g, :], CT[:, g, ds(c * P, P)], start=True, stop=True)
                    wait(pe, "z_done", c)
                    for h in range(NH):
                        last = pe.matmul(R[:, h, :], adts[:, s, h:h + 1].to_broadcast([P, P]), tri[:, :], start=True, stop=True)
                last.then_inc(S["gr_done"], 1)

            def back(c, s):
                r = NS if is_sample(c) else P
                wait(pe, "m_done", c + 1)
                wait(pe, "y1_done", c)
                wait(pe, "decay_ready", 1)
                for h in range(NH):
                    last = pe.matmul(pY[0:r, h * HD:(h + 1) * HD], E[0:r, s, h, 0:r], xdt[0:r, s, h * HD:(h + 1) * HD],
                                     start=True, stop=True)
                last.then_inc(S["y_mm"], 1)
                wait(pe, "off_done", c)
                wait(pe, "st_done", c)
                wait(pe, "zeroed", 1)
                if is_sample(c):
                    wait(pe, "cz_ready", 1)
                    wait(pe, "bz_ready", 1)
                    wait(pe, "state_loaded", 16)
                    for g in range(NGROUP):
                        for b in range(DB):
                            last = pe.matmul(pO[0:NS, g * GW:(g + 1) * GW], Cz[:, g, b * NS:(b + 1) * NS],
                                             state_s[:, b, g * GW:(g + 1) * GW], start=(b == 0), stop=(b == DB - 1))
                    last.then_inc(S["o_mm"], 1)
                    for b in range(DB):
                        wait(pe, "st_done", c + b - 2)
                        for g in range(NGROUP):
                            last = pe.matmul(added[b % 3][:, g * GW:(g + 1) * GW], Bz[:, b, g * P:(g + 1) * P],
                                             xdd[0:NS, s, g * GW:(g + 1) * GW], start=True, stop=True)
                        last.then_inc(S["s_mm"], 1)
                else:
                    wait(pe, "staged2", c + 1)
                    for g in range(NGROUP):
                        last = pe.matmul(pO[:, g * GW:(g + 1) * GW], CTs[:, s, g, :], state[:, g * GW:(g + 1) * GW],
                                         start=True, stop=True)
                    last.then_inc(S["o_mm"], 1)
                    for g in range(NGROUP):
                        last = pe.matmul(pS[:, g * GW:(g + 1) * GW], Bts[:, s, g, :], xdd[:, s, g * GW:(g + 1) * GW],
                                         start=True, stop=True)
                    last.then_inc(S["s_mm"], 1)

            def turn(c, s):
                r = NS if is_sample(c) else P
                wait(pe, "yw_done", c + 1)
                wait(pe, "ty_done", c)
                for j in range(NPAIR):
                    last = pe.transpose(pT[:, j, 0:r], Y[0:r, s, j * P:(j + 1) * P], ident[0:r, 0:r])
                last.then_inc(S["t_mm"], 1)

            run(pe, front, back, turn)


def shape_constants():
    k = np.arange(P)
    tok = np.arange(NS)
    same = (tok[:, None] // DT) == (tok[None, :] // DT)
    causal_s = same & (tok[:, None] <= tok[None, :])
    f = np.float32
    return {
        "c_ident": np.eye(P, dtype=f),
        "c_tri": (k[:, None] <= k[None, :]).astype(f),
        "c_tri_s": causal_s.astype(f),
        "c_ones": np.ones((P, P), f),
        "c_mask": np.where(k[:, None] <= k[None, :], 0, NEG).astype(f),
        "c_mask_s": np.where(causal_s, 0, NEG).astype(f),
        "c_ones_s": same.astype(f),
        "c_in_seq": ((tok[:, None] // DT) == np.arange(DB)[None, :]).astype(f),
    }
def alibi(h, dist):
    slope = np.float32(2.0 ** (-8.0 * (h + 1) / NH))
    count = sum(((dist >= 0) & (dist <= w) & (dist % r == 0)).astype(np.float64) for w, r in BRANCHES)
    return np.where(count > 0, -slope * dist + np.log(np.maximum(count, 1)), NEG).astype(np.float32)


def attention_constants():
    p = np.arange(P)[:, None]
    wide = SEQ - P + p - np.arange(SEQ)[None, :]
    table = np.stack([alibi(h, wide) for h in range(NH)])
    t = np.arange(DT)[:, None]
    past = np.concatenate([alibi(h, PAST + t - np.arange(PAST)[None, :]) for h in range(NH)])
    new = np.full((NH * DT, (2 * DB - 1) * DT), NEG, np.float32)
    own = np.concatenate([alibi(h, t - np.arange(DT)[None, :]) for h in range(NH)])
    new[:, (DB - 1) * DT:DB * DT] = own
    return {"c_alibi": table, "c_alibi_past": past, "c_alibi_new": new}


def load_keys(sp, io, Kc, loaded, b, s):
    sp.dma_start(Kc[:, s, :, :], io["cache_kT"][ds(b, 1)].squeeze(0)).then_inc(loaded[s], 16)


def load_values(sp, io, Vc, loaded, b, s):
    sp.dma_start(Vc[:, s, :, :], io["cache_v"][ds(b, 1)].squeeze(0).rearrange("(n p) f -> p n f", p=P)).then_inc(loaded[s], 16)


def stage_prompt_attention(nc, sem, io, ident, qT, kT, mixT, place, prefetch):
    qz = [place(f"pa_qz{u}", [P, SEQ]) for u in range(2)]
    table = place("pa_table", [P, 2, SEQ])
    V = [place(f"pa_V{u}", [P, NQB, P]) for u in range(2)]
    NZ = 4
    Z = place("pa_Z", [P, NZ, SEQ])
    PT = [place(f"pa_PT{s}", [P, NQB, P]) for s in range(2)]
    nmax, total, inv = (place("pa_" + n, [P, NZ, 1]) for n in ("nmax", "total", "inv"))
    S = {n: sem("pa_" + n) for n in ("zeroed", "qk", "z", "max", "exp", "inv", "norm", "turn", "pt", "pv")}
    out_done = [sem(f"pa_out{s}") for s in range(2)]
    staged = [sem(f"pa_staged{u}") for u in range(2)]
    loaded = [sem(f"pa_loaded{u}") for u in range(2)]
    ITEMS = 2 * NQB
    head_of = lambda m: m // NQB % 2
    block_of = lambda m: m % NQB
    pair_of = lambda i, m: i + m // ITEMS
    keys = lambda m: (block_of(m) + 1) * P
    groups = lambda m: -(-(block_of(m) + 1) // 4)
    groups_to = lambda m: sum(groups(k) for k in range(m))
    G_ALL = groups_to(ITEMS)

    def pipeline(engine, lead, first, second, third):
        def step(i, m, last):
            if not last or m + lead < ITEMS:
                first(i, m + lead)
            second(i, m)
            if not isinstance(i, int) or i * ITEMS + m:
                third(i, m - 1)

        for m in range(lead):
            first(0, m)
        for m in range(NZ):
            step(0, m, False)
        with engine.Fori(0, NPAIR - 1) as i:
            for m in range(NZ, ITEMS + NZ):
                step(i, m, False)
        for m in range(NZ, ITEMS):
            step(NPAIR - 1, m, True)
        third(NPAIR - 1, ITEMS - 1)

    with ExitStack() as ctx:
        pS = [ctx.enter_context(nc.psum_tensor(f"pa_S{s}", [P, SEQ], F32)) for s in range(2)]
        pT = [ctx.enter_context(nc.psum_tensor(f"pa_T{s}", [P, 4, P], F32)) for s in range(2)]
        pO = [ctx.enter_context(nc.psum_tensor(f"pa_O{s}", [P, P], F32)) for s in range(2)]
        block = ctx.enter_context(nc.Block())

        @block.sync
        def _(sp):
            def load(i, u):
                sp.dma_start(table[:, u, :], io["c_alibi"][ds(i * 2 + u, 1)].squeeze(0)).then_inc(loaded[u], 16)
                sp.dma_start(V[u][:, :, :], io["new_v"][0:SEQ, ds(i * P, P)].rearrange("(b p) f -> p b f", p=P))\
                    .then_inc(loaded[u], 16)

            load(0, 0)
            load(0, 1)
            with sp.Fori(0, NPAIR - 1) as i:
                for u in range(2):
                    sp.wait_ge(S["z"], i * ITEMS + (u + 1) * NQB)
                    sp.wait_ge(S["pv"], i * ITEMS + (u + 1) * NQB)
                    load(i + 1, u)
            prefetch(sp)

        @block.gpsimd
        def _(pool):
            for u in range(2):
                pool.memset(qz[u][(1 - u) * HD:(2 - u) * HD, :], 0.0).then_inc(S["zeroed"], 1)
                pool.wait_ge(S["zeroed"], u + 1)
            def stage(i, u):
                pool.wait_ge(staged[1 - u], i + u)
                pool.tensor_copy(qz[u][u * HD:(u + 1) * HD, :],
                                 qT[u * HD:(u + 1) * HD, ds(i, 1), 0:SEQ].squeeze(1)).then_inc(staged[u], 1)

            stage(0, 0)
            stage(0, 1)
            with pool.Fori(0, NPAIR - 1) as i:
                for u in range(2):
                    pool.wait_ge(S["qk"], i * ITEMS + (u + 1) * NQB)
                    stage(i + 1, u)

        @block.vector
        def _(dve):
            def scores(i, m):
                n, u, at = keys(m), head_of(m), i * ITEMS + (m + 1)
                if block_of(m) == 0:
                    dve.wait_ge(loaded[u], pair_of(i, m) * 32 + 32)
                dve.wait_ge(S["qk"], at)
                if m >= NZ:
                    dve.wait_ge(S["turn"], i * G_ALL + groups_to(m - NZ + 1))
                z = Z[:, m % NZ, 0:n]
                dve.scalar_tensor_tensor(z, pS[m % 2][:, 0:n], HD ** -0.5, table[:, u, SEQ - n:SEQ], ALU.mult,
                                         ALU.add).then_inc(S["z"], 1)
                dve.wait_ge(S["z"], at)
                dve.reduce_max(nmax[:, m % NZ, :], z, AX.X, negate=True).then_inc(S["max"], 1)

            def norm(i, m):
                n, at = keys(m), i * ITEMS + (m + 1)
                dve.wait_ge(S["exp"], at)
                dve.reciprocal(inv[:, m % NZ, :], total[:, m % NZ, :]).then_inc(S["inv"], 1)
                dve.wait_ge(S["inv"], at)
                dve.tensor_scalar(Z[:, m % NZ, 0:n], Z[:, m % NZ, 0:n], inv[:, m % NZ, :], None, ALU.mult).then_inc(S["norm"], 1)

            pipeline(dve, 1, scores, norm, lambda i, m: None)

        @block.scalar
        def _(act):
            def exps(i, m):
                z = Z[:, m % NZ, 0:keys(m)]
                act.wait_ge(S["max"], i * ITEMS + (m + 1))
                act.activation(z, z, ACT.Exp, bias=nmax[:, m % NZ, :], accum_out=total[:, m % NZ, :]).then_inc(S["exp"], 1)

            def read_turned(i, m):
                if m >= 2:
                    act.wait_ge(S["pv"], i * ITEMS + (m - 1))
                for g in range(groups(m)):
                    t = groups_to(m) + g
                    k = min(4, block_of(m) + 1 - 4 * g)
                    act.wait_ge(S["turn"], i * G_ALL + (t + 1))
                    act.activation(PT[m % 2][:, 4 * g:4 * g + k, :], pT[t % 2][:, 0:k, :], ACT.Copy).then_inc(S["pt"], 1)

            def out(i, m):
                u, b = head_of(m), block_of(m)
                act.wait_ge(S["pv"], i * ITEMS + (m + 1))
                act.activation(mixT[u * HD:(u + 1) * HD, ds(pair_of(i, m), 1), b * P:(b + 1) * P].squeeze(1),
                               pO[m % 2][u * HD:(u + 1) * HD, :], ACT.Copy).then_inc(out_done[m % 2], 1)

            pipeline(act, 1, exps, read_turned, out)

        @block.tensor
        def _(pe):
            def qk(i, m):
                u, b, n = head_of(m), block_of(m), keys(m)
                if b == 0:
                    pe.wait_ge(staged[u], pair_of(i, m) + 1)
                if m >= 2:
                    pe.wait_ge(S["z"], i * ITEMS + (m - 1))
                for c in range(0, n, 512):
                    w = min(512, n - c)
                    last = pe.matmul(pS[m % 2][:, c:c + w], qz[u][:, b * P:(b + 1) * P],
                                     kT[:, ds(pair_of(i, m), 1), c:c + w].squeeze(1), start=True, stop=True)
                last.then_inc(S["qk"], 1)

            def turn(i, m):
                pe.wait_ge(S["norm"], i * ITEMS + (m + 1))
                for g in range(groups(m)):
                    t = groups_to(m) + g
                    if t >= 2:
                        pe.wait_ge(S["pt"], i * G_ALL + (t - 1))
                    for k in range(min(4, block_of(m) + 1 - 4 * g)):
                        kb = 4 * g + k
                        last = pe.transpose(pT[t % 2][:, k, :], Z[:, m % NZ, kb * P:(kb + 1) * P], ident[:, :])
                    last.then_inc(S["turn"], 1)

            def pv(i, m):
                u, nk = head_of(m), block_of(m) + 1
                if block_of(m) == 0:
                    pe.wait_ge(loaded[u], pair_of(i, m) * 32 + 32)
                pe.wait_ge(S["pt"], i * G_ALL + groups_to(m + 1))
                pe.wait_ge(out_done[m % 2], i * (ITEMS // 2) + m // 2)
                for kb in range(nk):
                    last = pe.matmul(pO[m % 2][:, :], V[u][:, kb, :], PT[m % 2][:, kb, :], start=(kb == 0), stop=(kb == nk - 1))
                last.then_inc(S["pv"], 1)

            pe.wait_ge(S["zeroed"], 2)
            pipeline(pe, 2, qk, turn, pv)


def stage_sample_attention(nc, sem, io, ident, qT, kT, mixT, Kc, Vc, keys_loaded, values_loaded, place, prefetch):
    R = NH * DT
    past, new = place("sa_past", [R, PAST]), place("sa_new", [R, (2 * DB - 1) * DT])
    Vn = place("sa_Vn", [NS, DA])
    Q = [place(f"sa_Q{s}", [P, NPAIR * (R + 2 * DT)]) for s in range(2)]
    Z = place("sa_Z", [R, 2, PAST + NS])
    PT = [place(f"sa_PT{s}", [P, NQB + 1, R]) for s in range(2)]
    O = place("sa_O", [R, DA])
    nmax, total, inv = (place("sa_" + n, [R, 2, 1]) for n in ("nmax", "total", "inv"))
    tables_loaded, turn_begun = sem("sa_tables_loaded"), sem("sa_turn_begun")
    two = lambda n: [sem(f"sa_{n}{s}") for s in range(2)]
    zeroed, q_ready, qk, z, mx, ex, iv, norm, turn, pt, pv, copied, o_turn, out = (
        two(n) for n in ("zeroed", "q_ready", "qk", "z", "max", "exp", "inv", "norm", "turn", "pt", "pv", "copied", "o_turn", "out"))

    def over_sequences(engine, first, second, third, fourth=nothing):
        def step(b, s, i):
            first(b + 1, 1 - s, i + s)
            second(b, s, i)
            third(b + 1, 1 - s, i + s)
            fourth(b, s, i)

        first(0, 0, 0)
        third(0, 0, 0)
        for s in range(2):
            step(s, s, 0)
        with engine.Fori(1, DB // 2 - 1) as i:
            for s in range(2):
                step(i * 2 + s, s, i)
        last = DB // 2 - 1
        step(DB - 2, 0, last)
        second(DB - 1, 1, last)
        fourth(DB - 1, 1, last)

    with ExitStack() as ctx:
        pS = ctx.enter_context(nc.psum_tensor("sa_S", [R, 3, 512], F32))
        pT = ctx.enter_context(nc.psum_tensor("sa_T", [P, 2, 512], F32))
        pO = ctx.enter_context(nc.psum_tensor("sa_pO", [R, DA], F32))
        pX = ctx.enter_context(nc.psum_tensor("sa_pX", [P, NPAIR * (R + 2 * DT)], F32))
        block = ctx.enter_context(nc.Block())

        @block.sync
        def _(sp):
            sp.dma_start(past[:, :], io["c_alibi_past"]).then_inc(tables_loaded, 16)
            sp.dma_start(new[:, :], io["c_alibi_new"]).then_inc(tables_loaded, 16)
            sp.dma_start(Vn[:, :], io["new_v"][SEQ:TOK, :]).then_inc(tables_loaded, 16)

            prefetch(sp)

            def keys(b, s, i):
                sp.wait_ge(qk[s], i)
                load_keys(sp, io, Kc, keys_loaded, b, s)

            def values(b, s, i):
                sp.wait_ge(pv[s], i)
                load_values(sp, io, Vc, values_loaded, b, s)

            keys(2, 0, 1)
            with sp.Fori(1, DB // 2 - 1) as i:
                keys(i * 2 + 1, 1, i)
                values(i * 2, 0, i)
                keys(i * 2 + 2, 0, i + 1)
                values(i * 2 + 1, 1, i)
            last = DB // 2 - 1
            keys(DB - 1, 1, last)
            values(DB - 2, 0, last)
            values(DB - 1, 1, last)

        @block.gpsimd
        def _(pool):
            for s in range(2):
                pool.memset(Q[s][:, :], 0.0).then_inc(zeroed[s], 1)

            pool.wait_ge(zeroed[0], 1)
            pool.wait_ge(zeroed[1], 1)

            def front(b, s, i):
                pool.wait_ge(qk[s], i)
                pool.wait_ge(q_ready[1 - s], (i + s) * 2)
                for u in range(2):
                    pool.wait_ge(q_ready[s], i * 2 + u)
                    pool.tensor_copy(Q[s][u * HD:(u + 1) * HD, :].rearrange("p (j x) -> p j x", j=NPAIR)[:, :, u * DT:(u + 1) * DT],
                                     qT[u * HD:(u + 1) * HD, :, ds(b * DT + SEQ, DT)]).then_inc(q_ready[s], 1)

            over_sequences(pool, front, nothing, nothing)

        @block.vector
        def _(dve):
            dve.wait_ge(tables_loaded, 48)

            def front(b, s, i):
                dve.wait_ge(qk[s], i + 1)
                dve.wait_ge(turn[s], i)
                dve.scalar_tensor_tensor(Z[:, s, 0:PAST], pS[:, 0:2, :].rearrange("p a b -> p (a b)"), HD ** -0.5, past[:, :],
                                         ALU.mult, ALU.add)
                dve.scalar_tensor_tensor(Z[:, s, PAST:], pS[:, 2, 0:NS], HD ** -0.5, new[:, ds(b * -DT + (DB - 1) * DT, NS)],
                                         ALU.mult, ALU.add).then_inc(z[s], 1)
                dve.wait_ge(z[s], i + 1)
                dve.reduce_max(nmax[:, s, :], Z[:, s, :], AX.X, negate=True).then_inc(mx[s], 1)

                dve.wait_ge(ex[s], i + 1)
                dve.reciprocal(inv[:, s, :], total[:, s, :]).then_inc(iv[s], 1)
                dve.wait_ge(iv[s], i + 1)
                dve.tensor_scalar(Z[:, s, :], Z[:, s, :], inv[:, s, :], None, ALU.mult).then_inc(norm[s], 1)

            def back(b, s, i):
                dve.wait_ge(o_turn[s], i + 1)
                for u in range(2):
                    last = dve.tensor_copy(mixT[u * HD:(u + 1) * HD, 0:NPAIR, ds(b * DT + SEQ, DT)],
                                           pX[u * HD:(u + 1) * HD, :].rearrange("p (j x) -> p j x", j=NPAIR)[:, :, u * DT:(u + 1) * DT])
                last.then_inc(out[s], 1)

            over_sequences(dve, front, back, nothing)

        @block.scalar
        def _(act):
            def front(b, s, i):
                act.wait_ge(mx[s], i + 1)
                act.activation(Z[:, s, :], Z[:, s, :], ACT.Exp, bias=nmax[:, s, :], accum_out=total[:, s, :]).then_inc(ex[s], 1)


            def copy_out(b, s, i):
                act.wait_ge(pv[s], i + 1)
                act.wait_ge(o_turn[1 - s], i + s)
                act.activation(O[:, :], pO[:, :], ACT.Copy).then_inc(copied[s], 1)

            def read_turned(b, s, i):
                act.wait_ge(turn[s], i + 1)
                act.wait_ge(pv[s], i)
                act.activation(PT[s][:, 0:NQB, :].rearrange("p n r -> p (n r)"), pT[:, 0, :], ACT.Copy)
                act.activation(PT[s][0:NS, NQB, :], pT[0:NS, 1, 0:R], ACT.Copy).then_inc(pt[s], 1)

            over_sequences(act, front, copy_out, read_turned)

        @block.tensor
        def _(pe):
            pe.wait_ge(tables_loaded, 48)

            def front(b, s, i):
                pe.wait_ge(keys_loaded[s], i * 16 + 16)
                pe.wait_ge(q_ready[s], i * 2 + 2)
                pe.wait_ge(z[1 - s], i + s)
                for c in range(3):
                    for j in range(NPAIR):
                        keys = Kc[:, s, j, c * 512:(c + 1) * 512] if c < 2 else kT[:, j, SEQ:TOK]
                        last = pe.matmul(pS[:, c, 0:512 if c < 2 else NS], Q[s][:, j * R:(j + 1) * R], keys,
                                         start=(j == 0), stop=(j == NPAIR - 1))
                last.then_inc(qk[s], 1)

            def turned(b, s, i):
                pe.wait_ge(norm[s], i + 1)
                pe.wait_ge(pt[1 - s], i + s)
                pe.sem_inc(turn_begun, 1)
                pe.wait_ge(turn_begun, 1)
                for n in range(NQB):
                    pe.transpose(pT[:, 0, n * R:(n + 1) * R], Z[:, s, n * P:(n + 1) * P], ident[0:R, 0:R])
                pe.transpose(pT[0:NS, 1, 0:R], Z[:, s, PAST:], ident[0:R, 0:R]).then_inc(turn[s], 1)

            def back(b, s, i):
                pe.wait_ge(pt[s], i + 1)
                pe.wait_ge(copied[1 - s], i + s)
                pe.wait_ge(values_loaded[s], i * 16 + 16)
                for n in range(NQB):
                    pe.matmul(pO[:, :], PT[s][:, n, :], Vc[:, s, n, :], start=(n == 0), stop=False)
                pe.matmul(pO[:, :], PT[s][0:NS, NQB, :], Vn[:, :], start=False, stop=True).then_inc(pv[s], 1)

            def turn_out(b, s, i):
                pe.wait_ge(copied[s], i + 1)
                pe.wait_ge(out[1 - s], i + s)
                pe.sem_inc(turn_begun, 1)
                pe.wait_ge(turn_begun, 1)
                for j in range(NPAIR):
                    last = pe.transpose(pX[:, j * R:(j + 1) * R], O[:, j * P:(j + 1) * P], ident[0:R, 0:R])
                last.then_inc(o_turn[s], 1)

            over_sequences(pe, front, back, turned, turn_out)
class ResidentWeight:

    def __init__(self, sem, place, place_raw, tag, dram, width):
        self.dram, self.chunks = dram, dram.shape[0] // P
        self.raw = place_raw(tag + "_raw", [P, self.chunks, width])
        self.hi = place(tag + "_hi", [P, self.chunks, width], F32R)
        self.lo = place(tag + "_lo", [P, self.chunks, width], F32R)
        self.loaded, self.hi_done, self.lo_done = (sem(f"{tag}_{n}") for n in ("loaded", "hi_done", "lo_done"))

    def load(self, sp):
        for k in range(self.chunks):
            sp.dma_start(self.raw[:, k, :], self.dram[k * P:(k + 1) * P, :]).then_inc(self.loaded, 16)

    def split_hi(self, act):
        act.wait_ge(self.loaded, 16 * self.chunks)
        for k in range(self.chunks):
            act.activation(self.hi[:, k, :], self.raw[:, k, :], ACT.Copy).then_inc(self.hi_done, 1)

    def split_lo(self, dve):
        for k in range(self.chunks):
            dve.wait_ge(self.hi_done, k + 1)
            dve.tensor_tensor(self.lo[:, k, :], self.raw[:, k, :], self.hi[:, k, :].bitcast(F32),
                              ALU.subtract).then_inc(self.lo_done, 1)


def split_product(pe, out, weights_first, n_k, ready=nothing):
    for k in range(n_k):
        ready(k)
        a_hi, a_lo, b_hi, b_lo = weights_first(k)
        for part, (a, b) in enumerate(((a_hi, b_hi), (a_hi, b_lo), (a_lo, b_hi))):
            last = pe.matmul(out, a, b, start=(k == 0 and part == 0), stop=(k == n_k - 1 and part == 2))
    return last


def stage_output(nc, sem, io, mixT, R, w, place):
    ln = LayerNorm(sem, place, "op_ln")
    h0 = place("op_h0", [P, 2, D])
    m_hi = [place(f"op_m_hi{s}", [P, KD, P], F32R) for s in range(2)]
    m_lo = [place(f"op_m_lo{s}", [P, KD, P], F32R) for s in range(2)]
    two = lambda n: [sem(f"op_{n}{s}") for s in range(2)]
    h0_loaded, hi_done, lo_done, mm_done, x_done = (two(n) for n in ("h0_loaded", "hi_done", "lo_done", "mm_done", "x_done"))
    with ExitStack() as ctx:
        pM = [ctx.enter_context(nc.psum_tensor(f"op_M{s}", [P, 2, 512], F32)) for s in range(2)]
        block = ctx.enter_context(nc.Block())
        row = lambda n, r: R[0:r, ds(n, 1), :].squeeze(1)

        @block.sync
        def _(sp):
            ln.load(sp, io["ln1_g"], io["ln1_b"])

            def front(s, i, r, n):
                sp.wait_ge(x_done[s], i)
                sp.dma_start(h0[0:r, s, :], io["h0"][ds(n * P, r), :]).then_inc(h0_loaded[s], 16)

            over_blocks(sp, (1, front))

        @block.gpsimd
        def _(pool):
            ln.constants(pool)

            def back(s, i, r, n):
                ln.inverse_root(pool, s, i, r)
                ln.gain(pool, row(n, r), s, i, r)

            over_blocks(pool, (0, back))

        @block.scalar
        def _(act):
            def front(s, i, r, n):
                act.wait_ge(mm_done[s], i)
                act.activation(m_hi[s][:, :, 0:r], mixT[:, :, ds(n * P, r)], ACT.Copy).then_inc(hi_done[s], 1)

            w.split_hi(act)
            over_blocks(act, (1, front), (0, lambda s, i, r, n: ln.normalise(act, row(n, r), row(n, r), s, i, r)))

        @block.vector
        def _(dve):
            def front(s, i, r, n):
                dve.wait_ge(hi_done[s], i + 1)
                dve.tensor_tensor(m_lo[s][:, :, 0:r], mixT[:, :, ds(n * P, r)], m_hi[s][:, :, 0:r].bitcast(F32),
                                  ALU.subtract).then_inc(lo_done[s], 1)

            def back(s, i, r, n):
                dve.wait_ge(mm_done[s], i + 1)
                dve.wait_ge(h0_loaded[s], i * 16 + 16)
                dve.scalar_tensor_tensor(row(n, r), h0[0:r, s, :], ALPHA, pM[s][0:r, :, :].rearrange("p a b -> p (a b)"),
                                         ALU.mult, ALU.add).then_inc(x_done[s], 1)
                dve.wait_ge(ln.loaded, 32)
                dve.wait_ge(x_done[s], i + 1)
                ln.statistics(dve, row(n, r), s, i, r)
                ln.shift(dve, s, i, r)
                ln.bias(dve, row(n, r), s, i, r)

            w.split_lo(dve)
            over_blocks(dve, (1, front), (0, back))

        @block.tensor
        def _(pe):
            def back(s, i, r, n):
                pe.wait_ge(lo_done[s], i + 1)
                pe.wait_ge(x_done[s], i)
                first = isinstance(n, int) and n == 0

                def ready(k):
                    if first:
                        pe.wait_ge(w.lo_done, k + 1)

                for half in range(2):
                    c = slice(half * 512, (half + 1) * 512)
                    last = split_product(pe, pM[s][0:r, half, :], lambda k: (
                        m_hi[s][:, k, 0:r], m_lo[s][:, k, 0:r], w.hi[:, k, c], w.lo[:, k, c]), KD, ready)
                last.then_inc(mm_done[s], 1)

            over_blocks(pe, (0, back))


def stage_mlp(nc, sem, io, ident, R, place, prefetch):
    FB = 4
    NC = DFF // (FB * P)
    UNITS = NB * 2
    hT_hi, hT_lo = place("ml_hT_hi", [P, KD, TOK], F32R), place("ml_hT_lo", [P, KD, TOK], F32R)
    u_hi = [place(f"ml_u_hi{f}", [P, TOK], F32R) for f in range(FB)]
    u_lo = [place(f"ml_u_lo{f}", [P, TOK], F32R) for f in range(FB)]
    relu, u = place("ml_relu", [P, TOK]), place("ml_u", [P, TOK])
    up_raw, down_raw = place("ml_up_raw", [P, KD, P]), place("ml_down_raw", [P, D])
    up_hi = [place(f"ml_up_hi{s}", [P, KD, P], F32R) for s in range(2)]
    up_lo = [place(f"ml_up_lo{s}", [P, KD, P], F32R) for s in range(2)]
    down_hi, down_lo = place("ml_down_hi", [P, FB, D], F32R), place("ml_down_lo", [P, FB, D], F32R)
    one = lambda *names: [sem("ml_" + n) for n in names]
    many = lambda n, k: [sem(f"ml_{n}{s}") for s in range(k)]
    up_loaded, up_hi_done, up_lo_done, down_loaded, down_hi_done, down_lo_done, down_used = one(
        "up_loaded", "up_hi_done", "up_lo_done", "down_loaded", "down_hi_done", "down_lo_done", "down_used")
    t_done, thi_done, tlo_done, scaled = one("t_done", "thi_done", "tlo_done", "scaled")
    up_mm, dn_mm, added = many("up_mm", 2), many("dn_mm", 2), many("added", 2)
    relu_done = [many(f"relu{s}_", 3) for s in range(2)]
    mul_done, sq_done, ulo_done = many("mul", 3), many("sq", 3), many("ulo", 3)

    def rows(n):
        return NS if n == NB - 1 else P

    with ExitStack() as ctx:
        pU = [ctx.enter_context(nc.psum_tensor(f"ml_U{s}", [P, 3, 512], F32)) for s in range(2)]
        pD = [ctx.enter_context(nc.psum_tensor(f"ml_D{s}", [P, 512], F32)) for s in range(2)]
        block = ctx.enter_context(nc.Block())

        def chunks(engine, chunk):
            chunk(0, False)
            with engine.Fori(1, NC - 1) as c:
                chunk(c, False)
            chunk(NC - 1, True)

        @block.sync
        def _(sp):
            def load_up(c, f):
                sp.wait_ge(up_lo_done, c * FB + f)
                sp.dma_start(up_raw[:, :, :], w_raw_view(io["w_up"], c * (FB * P) + f * P, P)).then_inc(up_loaded, 16)

            def chunk(c, last):
                for f in range(FB):
                    if not (last and f >= 2):
                        load_up(c, f + 2)
                    sp.wait_ge(down_lo_done, c * FB + f)
                    sp.dma_start(down_raw[:, :], io["w_down"][ds(c * (FB * P) + f * P, P), :]).then_inc(down_loaded, 16)

            load_up(0, 0)
            load_up(0, 1)
            chunks(sp, chunk)
            sp.wait_ge(up_mm[0], 3 * FB // 2 * NC)
            sp.wait_ge(up_mm[1], 3 * FB // 2 * NC)
            prefetch(sp)

        @block.gpsimd
        def _(pool):
            def chunk(c, last):
                for f in range(FB):
                    for g, (col, w) in enumerate(GROUPS):
                        pool.wait_ge(relu_done[f % 2][g], c * 2 + (f // 2 + 1))
                        pool.wait_ge(ulo_done[g], c * FB + f)
                        x = relu[:, col:col + w]
                        pool.tensor_tensor(u[:, col:col + w], x, x, ALU.mult).then_inc(mul_done[g], 1)

            chunks(pool, chunk)

        @block.scalar
        def _(act):
            def split_up(c, f):
                act.wait_ge(up_loaded, c * (16 * FB) + 16 * (f + 1))
                act.wait_ge(up_mm[f % 2], c * 6 + 3 * (f // 2))
                act.activation(up_hi[f % 2][:, :, :], up_raw[:, :, :], ACT.Copy).then_inc(up_hi_done, 1)

            def chunk(c, last):
                for f in range(FB):
                    s = f % 2
                    for g, (col, w) in enumerate(GROUPS):
                        act.wait_ge(up_mm[s], c * 6 + (3 * (f // 2) + g + 1))
                        act.wait_ge(mul_done[g], c * FB + f)
                        act.activation(relu[:, col:col + w], pU[s][:, g, 0:w], ACT.Relu).then_inc(relu_done[s][g], 1)
                        act.wait_ge(relu_done[s][g], c * 2 + (f // 2 + 1))
                        act.wait_ge(down_used, c)
                        act.activation(u_hi[f][:, col:col + w], relu[:, col:col + w], ACT.Square).then_inc(sq_done[g], 1)
                    if not (last and f >= 2):
                        split_up(c, f + 2)
                    act.wait_ge(down_loaded, c * (16 * FB) + 16 * (f + 1))
                    act.activation(down_hi[:, f, :], down_raw[:, :], ACT.Copy).then_inc(down_hi_done, 1)

            split_up(0, 0)
            split_up(0, 1)
            for n in range(NB):
                r = rows(n)
                act.wait_ge(t_done, n + 1)
                act.activation(hT_hi[:, :, n * P:n * P + r], pU[n % 2][:, 0:2, :].rearrange("p a (b c) -> p (a b) c", c=P)[:, :, 0:r],
                               ACT.Copy).then_inc(thi_done, 1)
                act.activation(R[0:r, n, :], R[0:r, n, :], ACT.Copy, scale=ALPHA).then_inc(scaled, 1)
            chunks(act, chunk)

        @block.vector
        def _(dve):
            def split_up(c, f):
                dve.wait_ge(up_hi_done, c * FB + (f + 1))
                dve.tensor_tensor(up_lo[f % 2][:, :, :], up_raw[:, :, :], up_hi[f % 2][:, :, :].bitcast(F32),
                                  ALU.subtract).then_inc(up_lo_done, 1)

            def chunk(c, last):
                for f in range(FB):
                    for g, (col, w) in enumerate(GROUPS):
                        dve.wait_ge(mul_done[g], c * FB + (f + 1))
                        dve.wait_ge(sq_done[g], c * FB + (f + 1))
                        dve.tensor_tensor(u_lo[f][:, col:col + w], u[:, col:col + w], u_hi[f][:, col:col + w].bitcast(F32),
                                          ALU.subtract).then_inc(ulo_done[g], 1)
                    if not (last and f >= 2):
                        split_up(c, f + 2)
                    dve.wait_ge(down_hi_done, c * FB + (f + 1))
                    dve.tensor_tensor(down_lo[:, f, :], down_raw[:, :], down_hi[:, f, :].bitcast(F32),
                                      ALU.subtract).then_inc(down_lo_done, 1)
                for v in range(UNITS):
                    n, half, s = v // 2, v % 2, v % 2
                    r = rows(n)
                    dve.wait_ge(dn_mm[s], c * NB + (v // 2 + 1))
                    dve.wait_ge(added[s], c * NB + v // 2)
                    acc = R[0:r, n, half * 512:(half + 1) * 512]
                    dve.tensor_tensor(acc, acc, pD[s][0:r, :], ALU.add).then_inc(added[s], 1)

            split_up(0, 0)
            split_up(0, 1)
            for n in range(NB):
                r = rows(n)
                dve.wait_ge(thi_done, n + 1)
                dve.tensor_tensor(hT_lo[:, :, n * P:n * P + r], pU[n % 2][:, 0:2, :].rearrange("p a (b c) -> p (a b) c", c=P)[:, :, 0:r],
                                  hT_hi[:, :, n * P:n * P + r].bitcast(F32), ALU.subtract).then_inc(tlo_done, 1)
            dve.wait_ge(scaled, NB)
            chunks(dve, chunk)

        @block.tensor
        def _(pe):
            for n in range(NB):
                r = rows(n)
                if n >= 2:
                    pe.wait_ge(tlo_done, n - 1)
                for k in range(KD):
                    last = pe.transpose(pU[n % 2][:, k // 4, (k % 4) * P:(k % 4) * P + r], R[0:r, n, k * P:(k + 1) * P], ident[0:r, 0:r])
                last.then_inc(t_done, 1)
            pe.wait_ge(tlo_done, NB)

            def down(c, v, f):
                n, half, s = v // 2, v % 2, v % 2
                r = rows(n)
                cols, out = slice(half * 512, (half + 1) * 512), pD[s][0:r, :]
                a_hi, a_lo = u_hi[f][:, n * P:n * P + r], u_lo[f][:, n * P:n * P + r]
                for part, (a, b) in enumerate(((a_hi, down_hi), (a_hi, down_lo), (a_lo, down_hi))):
                    last = pe.matmul(out, a, b[:, f, cols], start=(f == 0 and part == 0), stop=(f == FB - 1 and part == 2))
                return last

            def chunk(c, last):
                for f in range(FB):
                    s = f % 2
                    pe.wait_ge(up_lo_done, c * FB + (f + 1))
                    for g, (col, w) in enumerate(GROUPS):
                        pe.wait_ge(relu_done[s][g], c * 2 + f // 2)
                        split_product(pe, pU[s][:, g, 0:w], lambda k: (
                            up_hi[s][:, k, :], up_lo[s][:, k, :], hT_hi[:, k, col:col + w], hT_lo[:, k, col:col + w]),
                            KD).then_inc(up_mm[s], 1)
                order = [(v, f) for f in range(FB - 1) for v in range(2)] + [(v, FB - 1) for v in range(2)]
                order += [(v, f) for v in range(2, UNITS) for f in range(FB)]
                for at, (v, f) in enumerate(order):
                    if f == 0:
                        pe.wait_ge(added[v % 2], c * NB + v // 2)
                    if v == 0:
                        pe.wait_ge(down_lo_done, c * FB + (f + 1))
                        for g in range(3):
                            pe.wait_ge(ulo_done[g], c * FB + (f + 1))
                    last_mm = down(c, v, f)
                    if f == FB - 1:
                        last_mm.then_inc(dn_mm[v % 2], 1)
                        if v == UNITS - 1:
                            pe.wait_ge(dn_mm[v % 2], c * NB + NB)
                            pe.sem_inc(down_used, 1)

            chunks(pe, chunk)


def stage_gate(nc, sem, io, ident, R, wg, wp, place):
    ln2, ln3 = LayerNorm(sem, place, "gt_ln2"), LayerNorm(sem, place, "gt_ln3")
    pe_raw = place("gt_pe", [P, 2, KPLE, P])
    h_hi = [place(f"gt_h_hi{s}", [P, KD, P], F32R) for s in range(2)]
    h_lo = [place(f"gt_h_lo{s}", [P, KD, P], F32R) for s in range(2)]
    p_hi = [place(f"gt_p_hi{s}", [P, KPLE, P], F32R) for s in range(2)]
    p_lo = [place(f"gt_p_lo{s}", [P, KPLE, P], F32R) for s in range(2)]
    H = place("gt_h", [P, 2, D])
    gate = wp.raw
    names = "pe_loaded staged turned hi lo phi plo gate_mm ple_mm sg gated x stored".split()
    S = {n: [sem(f"gt_{n}{s}") for s in range(2)] for n in names}
    with ExitStack() as ctx:
        pT = ctx.enter_context(nc.psum_tensor("gt_T", [P, KD, P], F32))
        pG = [ctx.enter_context(nc.psum_tensor(f"gt_G{s}", [P, 2, 512], F32)) for s in range(2)]
        pP = ctx.enter_context(nc.psum_tensor("gt_P", [P, 2, 512], F32))
        block = ctx.enter_context(nc.Block())
        row = lambda n, r: R[0:r, ds(n, 1), :].squeeze(1)
        flat = lambda t, r: t[0:r, :, :].rearrange("p a b -> p (a b)")

        @block.sync
        def _(sp):
            ln2.load(sp, io["ln2_g"], io["ln2_b"])
            ln3.load(sp, io["ln3_g"], io["ln3_b"])

            def load(s, i, r, n):
                sp.wait_ge(S["plo"][s], i)
                sp.dma_start(pe_raw[:, s, :, 0:r], io["pT"][:, ds(n * P, r)].rearrange("(k p) t -> p k t", p=P))\
                    .then_inc(S["pe_loaded"][s], 16)

            def store(s, i, r, n):
                sp.wait_ge(ln3.done[s], i + 1)
                sp.dma_start(io["y"][ds(n * P, r), :], gate[0:r, s, :]).then_inc(S["stored"][s], 16)

            over_blocks(sp, (2, load), (-1, store))
            sp.wait_ge(S["stored"][0], 16 * (NQB // 2 + 1))
            sp.wait_ge(S["stored"][1], 16 * (NQB // 2))

        @block.gpsimd
        def _(pool):
            ln2.constants(pool)
            ln3.constants(pool)
            over_blocks(pool, (-1, lambda s, i, r, n: ln3.inverse_root(pool, s, i, r)),
                        (2, lambda s, i, r, n: ln2.inverse_root(pool, s, i, r)),
                        (-1, lambda s, i, r, n: ln3.gain(pool, gate[0:r, s, :], s, i, r)),
                        (2, lambda s, i, r, n: ln2.gain(pool, row(n, r), s, i, r)))

        @block.scalar
        def _(act):
            def sigmoid(s, i, r, n):
                act.wait_ge(S["gate_mm"][s], i + 1)
                act.wait_ge(S["stored"][s], i * 16)
                if isinstance(n, int) and n < 2:
                    act.wait_ge(wp.lo_done, KPLE)
                act.activation(gate[0:r, s, :], flat(pG[s], r), ACT.Sigmoid).then_inc(S["sg"][s], 1)

            def split(s, i, r, n):
                act.wait_ge(S["turned"][s], i + 1)
                act.activation(h_hi[s][:, :, 0:r], pT[:, :, 0:r], ACT.Copy).then_inc(S["hi"][s], 1)
                act.wait_ge(S["pe_loaded"][s], i * 16 + 16)
                act.wait_ge(S["ple_mm"][s], i)
                act.activation(p_hi[s][:, :, 0:r], pe_raw[:, s, :, 0:r], ACT.Copy).then_inc(S["phi"][s], 1)

            def normalise2(s, i, r, n):
                ln2.normalise(act, row(n, r), row(n, r), s, i, r)
                if isinstance(n, int) and n == 0:
                    wg.split_hi(act)
                    wp.split_hi(act)

            def stage(s, i, r, n):
                act.wait_ge(ln2.done[s], i + 1)
                act.wait_ge(S["turned"][s], i)
                act.activation(H[0:r, s, :], row(n, r), ACT.Copy).then_inc(S["staged"][s], 1)

            over_blocks(act, (1, stage), (-1, sigmoid), (1, split),
                        (-1, lambda s, i, r, n: ln3.normalise(act, gate[0:r, s, :], gate[0:r, s, :], s, i, r)),
                        (2, normalise2))

        @block.vector
        def _(dve):
            def product(s, i, r, n):
                dve.wait_ge(S["sg"][s], i + 1)
                dve.wait_ge(S["ple_mm"][s], i + 1)
                x = gate[0:r, s, :]
                dve.tensor_tensor(x, x, flat(pP, r), ALU.mult).then_inc(S["gated"][s], 1)
                dve.wait_ge(S["gated"][s], i + 1)
                dve.scalar_tensor_tensor(x, row(n, r), ALPHA, x, ALU.mult, ALU.add).then_inc(S["x"][s], 1)
                dve.wait_ge(S["x"][s], i + 1)
                dve.wait_ge(ln3.loaded, 32)
                ln3.statistics(dve, x, s, i, r)

            def split(s, i, r, n):
                dve.wait_ge(S["hi"][s], i + 1)
                dve.tensor_tensor(h_lo[s][:, :, 0:r], pT[:, :, 0:r], h_hi[s][:, :, 0:r].bitcast(F32),
                                  ALU.subtract).then_inc(S["lo"][s], 1)
                dve.wait_ge(S["phi"][s], i + 1)
                dve.tensor_tensor(p_lo[s][:, :, 0:r], pe_raw[:, s, :, 0:r], p_hi[s][:, :, 0:r].bitcast(F32),
                                  ALU.subtract).then_inc(S["plo"][s], 1)

            def bias2(s, i, r, n):
                if isinstance(n, int) and n == 0:
                    wg.split_lo(dve)
                    wp.split_lo(dve)
                ln2.bias(dve, row(n, r), s, i, r)

            over_blocks(dve, (-1, product), (1, split), (2, lambda s, i, r, n: ln2.statistics(dve, row(n, r), s, i, r)),
                        (-1, lambda s, i, r, n: ln3.shift(dve, s, i, r)), (2, lambda s, i, r, n: ln2.shift(dve, s, i, r)),
                        (-1, lambda s, i, r, n: ln3.bias(dve, gate[0:r, s, :], s, i, r)), (2, bias2))

        @block.tensor
        def _(pe):
            def turn(s, i, r, n):
                pe.wait_ge(S["staged"][s], i + 1)
                if not (isinstance(n, int) and n == 0):
                    pe.wait_ge(S["lo"][1 - s], i + s)
                for k in range(KD):
                    last = pe.transpose(pT[:, k, 0:r], H[0:r, s, k * P:(k + 1) * P], ident[0:r, 0:r])
                last.then_inc(S["turned"][s], 1)

            def products(s, i, r, n):
                pe.wait_ge(S["lo"][s], i + 1)
                pe.wait_ge(S["sg"][s], i)
                first = isinstance(n, int) and n == 0

                def ready(k):
                    if first:
                        pe.wait_ge(wg.lo_done, k + 1)

                for half in range(2):
                    c = slice(half * 512, (half + 1) * 512)
                    last = split_product(pe, pG[s][0:r, half, :], lambda k: (
                        h_hi[s][:, k, 0:r], h_lo[s][:, k, 0:r], wg.hi[:, k, c], wg.lo[:, k, c]), KD, ready)
                last.then_inc(S["gate_mm"][s], 1)
                if first:
                    pe.wait_ge(wp.lo_done, KPLE)
                pe.wait_ge(S["plo"][s], i + 1)
                pe.wait_ge(S["gated"][1 - s], i + s)
                for half in range(2):
                    c = slice(half * 512, (half + 1) * 512)
                    last = split_product(pe, pP[0:r, half, :], lambda k: (
                        p_hi[s][:, k, 0:r], p_lo[s][:, k, 0:r], wp.hi[:, k, c], wp.lo[:, k, c]), KPLE)
                last.then_inc(S["ple_mm"][s], 1)

            over_blocks(pe, (1, turn), (0, products))
OUTPUTS = {"y": (TOK, D), "new_k": (TOK, DA), "new_v": (TOK, DA), "new_convT": (P, NXBC, (CW - 1) * (1 + DB)),
           "new_ssm_promptT": (NSTATE, DA), "new_ssm_sampleT": (NSTATE, DB, DA)}


SAMPLE_BYTES = 4 * (PAST + (2 * DB - 1) * DT + 2 * DA + 2 * NPAIR * (NH + 2) * DT + 2 * (PAST + NS) + 2 * (NQB + 1) * NH * DT + 64)


def build(nc, io):
    io = dict(io)
    io["h0"] = nc.dram_tensor("h0_scratch", [TOK, D], F32, kind="Internal").ap()
    io["z_act"] = nc.dram_tensor("z_act_scratch", [TOK, DA], F32, kind="Internal").ap()
    with ExitStack() as ctx:
        held, in_use = [ExitStack()], []

        def sem(name):
            in_use.append(held[0].enter_context(nc.semaphore(name)))
            return in_use[-1]

        def clear_semaphores():
            with nc.Block() as block:
                @block.sync
                def _(sp):
                    for s in in_use:
                        sp.sem_clear(s)
            held[0].close()
            held[0] = ExitStack()
            in_use.clear()

        ctx.callback(lambda: held[0].close())

        const = Place(nc, SBUF_START)
        ident = const("ident", [P, P])
        base = const.offset
        qk = Place(nc, base)
        qT, kT = qk("qT", [P, NPAIR, TOK]), qk("kT", [P, NPAIR, TOK])
        hT_hi, hT_lo = qk("hT_hi", [P, KD, TOK], F32R), qk("hT_lo", [P, KD, TOK], F32R)
        xbc_start = qk.offset
        Xt, Bt = qk("Xt", [P, NB, DA]), qk("Bt", [P, NB, NGROUP * NSTATE])
        BT, CT = qk("BT", [P, NGROUP, TOK]), qk("CT", [P, NGROUP, TOK])
        dt_raw = qk("dt_raw", [P, NB, NH])
        after_xbc = qk.offset
        late = Place(nc, base)
        R, mixT = late("R", [P, NB, D]), late("mixT", [P, KD, TOK])
        after_mix = late.offset

        consts_loaded = sem("consts_loaded")
        with nc.Block() as block:
            @block.sync
            def _(sp):
                sp.dma_start(ident[:, :], io["c_ident"]).then_inc(consts_loaded, 16)
                sp.wait_ge(consts_loaded, 16)

        consts = {"ident": ident, **{k[2:] + "_d": io[k] for k in (
            "c_tri", "c_tri_s", "c_ones", "c_mask", "c_mask_s", "c_ones_s", "c_in_seq")}}
        projection = Place(nc, after_xbc)
        weights = ProjectionWeights(sem, projection, io["w_in"])
        stage_input_norm(nc, sem, io, ident, hT_hi, hT_lo, weights, Place(nc, xbc_start, after_xbc, projection.offset))
        stage_projection(nc, sem, io, ident, hT_hi, hT_lo, weights, qT, kT, Xt, Bt, BT, CT, dt_raw, projection)
        stage_ssd(nc, sem, io, consts, Xt, Bt, BT, CT, dt_raw, mixT, Place(nc, after_mix, xbc_start, after_xbc))
        clear_semaphores()
        attention = Place(nc, after_mix)
        Kc, Vc = attention("Kc", [P, 2, NPAIR, PAST]), attention("Vc", [P, 2, NQB, DA])
        keys_loaded, values_loaded = ([sem(f"cache_{n}_loaded{s}") for s in range(2)] for n in ("keys", "values"))
        after_cache = attention.offset

        def prefetch(sp):
            for b in range(2):
                load_keys(sp, io, Kc, keys_loaded, b, b)
                load_values(sp, io, Vc, values_loaded, b, b)

        stage_prompt_attention(nc, sem, io, ident, qT, kT, mixT, attention, prefetch)
        sample = Place(nc, after_cache)
        for_raw = Place(nc, after_cache + SAMPLE_BYTES)
        w_out = ResidentWeight(sem, Place(nc, after_mix), for_raw, "op_w", io["w_out"], D)
        stage_sample_attention(nc, sem, io, ident, qT, kT, mixT, Kc, Vc, keys_loaded, values_loaded, sample, w_out.load)
        assert sample.offset <= after_cache + SAMPLE_BYTES
        stage_output(nc, sem, io, mixT, R, w_out, Place(nc, after_cache, after_cache + SAMPLE_BYTES, for_raw.offset))
        clear_semaphores()
        after_R = base + 4 * NB * D
        for_raw = Place(nc, after_R)
        gate = Place(nc, after_R + 4 * (KD + KPLE) * D)
        w_gate = ResidentWeight(sem, gate, for_raw, "gt_wg", io["w_gate"], D)
        w_ple = ResidentWeight(sem, gate, for_raw, "gt_wp", io["w_ple"], D)

        def prefetch_gate(sp):
            w_gate.load(sp)
            w_ple.load(sp)

        stage_mlp(nc, sem, io, ident, R, Place(nc, after_R), prefetch_gate)
        stage_gate(nc, sem, io, ident, R, w_gate, w_ple, gate)


def kernel(**inputs):
    import concourse.bacc as bacc
    from concourse.bass_utils import run_bass_kernel_spmd

    x = {k: np.asarray(v) for k, v in inputs.items()}

    def features_first(a):
        a = a.reshape(a.shape[:-1] + (-1, P))
        return np.moveaxis(a, (-1, -2), (0, 1))

    arrays = {
        "x_prompt": x["x_prompt"][0], "x_sample": x["x_sample"].reshape(NS, D),
        "cache_kT": x["cache_k"][0].reshape(DB, PAST, NPAIR, P).transpose(0, 3, 2, 1),
        "cache_v": x["cache_v"][0].reshape(DB, PAST, DA),
        "state_convT": features_first(x["state_conv"][0].reshape(DB * (CW - 1), CD)),
        "state_ssmT": x["state_ssm"][0].reshape(DB, DA, NSTATE).transpose(2, 0, 1),
        "pT": np.concatenate([x["p_prompt"][0, 0], x["p_sample"][0].reshape(NS, DPLE)]).T,
        "conv_wT": np.moveaxis(features_first(x["conv_w"][0]), 2, -1), "conv_bT": features_first(x["conv_b"][0]),
        **{k: x[k] for k in ("ln_in_g", "ln_in_b")},
        **{k: x[k][0] for k in ("w_in", "dt_bias", "a_log", "d_skip", "ssd_norm_w", "w_out", "ln1_g", "ln1_b", "w_up",
                                "w_down", "ln2_g", "ln2_b", "w_gate", "w_ple", "ln3_g", "ln3_b")},
        **shape_constants(), **attention_constants(),
    }
    arrays = {k: np.ascontiguousarray(v) for k, v in arrays.items()}
    nc = bacc.Bacc("TRN2", target_bir_lowering=False, num_devices=1)
    io = {k: nc.dram_tensor("in_" + k, v.shape, mybir.dt.from_np(v.dtype), kind="ExternalInput").ap() for k, v in arrays.items()}
    io.update({k: nc.dram_tensor("out_" + k, shape, F32, kind="ExternalOutput").ap() for k, shape in OUTPUTS.items()})
    build(nc, io)
    result = run_bass_kernel_spmd(nc, [{"in_" + k: v for k, v in arrays.items()}], core_ids=[0]).results[0]
    y, k, v, conv, ssm_p, ssm_s = (np.asarray(result["out_" + n]) for n in OUTPUTS)
    conv = conv.transpose(2, 1, 0).reshape(-1, CD)
    return (y[:SEQ].reshape(1, SEQ, D), y[SEQ:].reshape(DB, DT, D),
            k[:SEQ].reshape(1, 1, SEQ, NH, HD), v[:SEQ].reshape(1, 1, SEQ, NH, HD),
            k[SEQ:].reshape(1, DB, DT, NH, HD), v[SEQ:].reshape(1, DB, DT, NH, HD),
            conv[:CW - 1].reshape(1, 1, CW - 1, CD), conv[CW - 1:].reshape(1, DB, CW - 1, CD),
            ssm_p.T.reshape(1, 1, NH, HD, NSTATE), ssm_s.transpose(1, 2, 0).reshape(1, DB, NH, HD, NSTATE))
```

```python
from contextlib import ExitStack

import concourse.bass as bass
import numpy as np
from concourse import mybir

F32 = mybir.dt.float32
F32R = mybir.dt.float32r
ALU = mybir.AluOpType
ACT = mybir.ActivationFunctionType
AX = mybir.AxisListType
ds = bass.ds

P = 128
D = 1024
KD = D // P
SEQ = 1024
NQB = SEQ // P
DB, DT = 8, 8
NS = DB * DT
TOK = SEQ + NS
NB = NQB + 1
PAST = 1024
HD = 64
NH = 8
DA = NH * HD
NPAIR = DA // P
NSTATE = 128
NGROUP = 2
HPG = NH // NGROUP
CW = 4
CD = DA + 2 * NGROUP * NSTATE
NXBC = CD // P
DIN = 3 * DA + DA + CD + NH
DFF = 4 * D
DPLE = 256
KPLE = DPLE // P
EPS = 1e-5
ALPHA = 2.0 ** 0.25
BRANCHES = ((128, 1), (512, 4), (2048, 16))
NEG = -1e30

GROUPS = [(0, 364), (364, 364), (728, 360)]

SBUF_START = 16512


class Place:

    def __init__(self, nc, offset, limit=None, then=None):
        self.nc, self.offset, self.limit, self.then = nc, offset, limit, then

    def __call__(self, name, shape, dtype=F32):
        size = 4 * int(np.prod(shape[1:]))
        if self.limit is not None and self.offset + size > self.limit:
            self.offset, self.limit = self.then, None
        t = self.nc.alloc_sbuf_tensor_at(name, list(shape), dtype, offset=self.offset)
        self.offset += -(-size // 32) * 32
        return t


def nothing(*step):
    pass


def take_statistics(dve, out, last_count, done, value):
    dve.wait_ge(done, value)
    dve.tensor_copy(out, last_count)


def w_raw_view(w, col, n):
    return w[:, ds(col, n)].rearrange("(k p) n -> p k n", p=P)


class LayerNorm:

    def __init__(self, sem, place, tag):
        self.G, self.B = place(tag + "_g", [P, D]), place(tag + "_b", [P, D])
        self.bn, self.mv = place(tag + "_bn", [P, 2, 2, 6]), place(tag + "_mv", [P, 2, 2])
        self.veps, self.rstd, self.nmr = (place(f"{tag}_{n}", [P, 2, 1]) for n in ("veps", "rstd", "nmr"))
        self.mhalf, self.eps, self.taken = (place(f"{tag}_{n}", [P, 1]) for n in ("mhalf", "eps", "taken"))
        self.loaded, self.const_set = sem(tag + "_loaded"), sem(tag + "_const_set")
        two = lambda n: [sem(f"{tag}_{n}{s}") for s in range(2)]
        self.bn_done, self.mv_done, self.veps_done, self.rstd_done, self.nmr_done, self.xn_done, self.gain_done, self.done = (
            two(n) for n in ("bn_done", "mv_done", "veps_done", "rstd_done", "nmr_done", "xn_done", "gain_done", "done"))

    def load(self, sp, g, b):
        sp.dma_start(self.G[:, :], g.partition_broadcast(P)).then_inc(self.loaded, 16)
        sp.dma_start(self.B[:, :], b.partition_broadcast(P)).then_inc(self.loaded, 16)

    def constants(self, pool):
        pool.memset(self.mhalf[:, :], -0.5).then_inc(self.const_set, 1)
        pool.memset(self.eps[:, :], EPS).then_inc(self.const_set, 1)
        pool.wait_ge(self.const_set, 2)

    def statistics(self, dve, x, s, i, r):
        half = D // 2
        dve.bn_stats(self.bn[0:r, s, 0, :], x[:, 0:half])
        dve.bn_stats(self.bn[0:r, s, 1, :], x[:, half:D]).then_inc(self.bn_done[s], 1)
        take_statistics(dve, self.taken[0:r, :], self.bn[0:r, s, 1, 0:1], self.bn_done[s], i + 1)
        dve.bn_aggr(self.mv[0:r, s, :], self.bn[0:r, s, :, :]).then_inc(self.mv_done[s], 1)

    def inverse_root(self, pool, s, i, r):
        pool.wait_ge(self.mv_done[s], i + 1)
        pool.tensor_tensor(self.veps[0:r, s, :], self.mv[0:r, s, 1:2], self.eps[0:r, :], ALU.add).then_inc(self.veps_done[s], 1)
        pool.wait_ge(self.veps_done[s], i + 1)
        pool.tensor_tensor(self.rstd[0:r, s, :], self.veps[0:r, s, :], self.mhalf[0:r, :], ALU.pow).then_inc(self.rstd_done[s], 1)

    def shift(self, dve, s, i, r):
        dve.wait_ge(self.rstd_done[s], i + 1)
        dve.tensor_scalar(self.nmr[0:r, s, :], self.mv[0:r, s, 0:1], self.rstd[0:r, s, :], -1.0, ALU.mult,
                          ALU.mult).then_inc(self.nmr_done[s], 1)

    def normalise(self, act, out, x, s, i, r):
        act.wait_ge(self.nmr_done[s], i + 1)
        act.activation(out, x, ACT.Identity, bias=self.nmr[0:r, s, :], scale=self.rstd[0:r, s, :]).then_inc(self.xn_done[s], 1)

    def gain(self, pool, x, s, i, r):
        pool.wait_ge(self.loaded, 32)
        pool.wait_ge(self.xn_done[s], i + 1)
        pool.tensor_tensor(x, x, self.G[0:r, :], ALU.mult).then_inc(self.gain_done[s], 1)

    def bias(self, dve, x, s, i, r, out=None):
        dve.wait_ge(self.gain_done[s], i + 1)
        dve.tensor_tensor(x if out is None else out, x, self.B[0:r, :], ALU.add).then_inc(self.done[s], 1)


def over_blocks(engine, *parts):
    def step(n, i=None):
        for lead, f in parts:
            m = n + lead
            if i is not None:
                f(m % 2, i + m // 2, P, i * 2 + m)
            elif 0 <= m < NB:
                f(m % 2, m // 2, NS if m == NB - 1 else P, m)

    leads = [lead for lead, _ in parts]
    at = 2 - min(leads)
    rounds = (NB - 1 - max(leads) - at) // 2
    for n in range(-max(leads), at):
        step(n)
    if rounds > 1:
        with engine.Fori(0, rounds) as i:
            step(at, i)
            step(at + 1, i)
        at += 2 * rounds
    for n in range(at, NB - min(leads)):
        step(n)


def stage_input_norm(nc, sem, io, ident, hT_hi, hT_lo, weights, place):
    X, H = place("in_x", [P, 2, D]), place("in_h", [P, 2, D])
    ln = LayerNorm(sem, place, "in_ln")
    names = "x_loaded stored t_done hi_done lo_done".split()
    S = {n: [sem(f"in_{n}{s}") for s in range(2)] for n in names}
    with ExitStack() as ctx:
        T = ctx.enter_context(nc.psum_tensor("in_T", [P, 2, KD, P], F32))
        block = ctx.enter_context(nc.Block())

        @block.sync
        def _(sp):
            def load(s, i, r, n):
                sp.wait_ge(ln.xn_done[s], i)
                src = io["x_sample"] if r == NS else io["x_prompt"][ds(n * P, P), :]
                sp.dma_start(X[0:r, s, :], src).then_inc(S["x_loaded"][s], 16)
                if isinstance(n, int) and n == 1:
                    ln.load(sp, io["ln_in_g"], io["ln_in_b"])
                    for m in range(2):
                        weights.load(sp, m)

            def store(s, i, r, n):
                sp.wait_ge(ln.done[s], i + 1)
                sp.dma_start(io["h0"][ds(n * P, r), :], H[0:r, s, :]).then_inc(S["stored"][s], 16)

            over_blocks(sp, (2, load), (0, store))
            sp.wait_ge(S["stored"][0], 16 * (NQB // 2 + 1))
            sp.wait_ge(S["stored"][1], 16 * (NQB // 2))

        @block.gpsimd
        def _(pool):
            ln.constants(pool)

            def norm(s, i, r, n):
                ln.inverse_root(pool, s, i, r)
                ln.gain(pool, H[0:r, s, :], s, i, r)

            over_blocks(pool, (0, norm))

        @block.vector
        def _(dve):
            def statistics(s, i, r, n):
                dve.wait_ge(S["x_loaded"][s], i * 16 + 16)
                ln.statistics(dve, X[0:r, s, :], s, i, r)

            def lo(s, i, r, n):
                dve.wait_ge(S["hi_done"][s], i + 1)
                dve.tensor_tensor(hT_lo[:, :, ds(n * P, r)], T[:, s, :, 0:r], hT_hi[:, :, ds(n * P, r)].bitcast(F32),
                                  ALU.subtract).then_inc(S["lo_done"][s], 1)

            over_blocks(dve, (2, statistics),
                        (2, lambda s, i, r, n: ln.shift(dve, s, i, r)),
                        (1, lambda s, i, r, n: ln.bias(dve, H[0:r, s, :], s, i, r)),
                        (0, lo))
            for m in range(2):
                weights.split_lo(dve, m)

        @block.scalar
        def _(act):
            def normalise(s, i, r, n):
                act.wait_ge(S["t_done"][s], i)
                act.wait_ge(S["stored"][s], i * 16)
                ln.normalise(act, H[0:r, s, :], X[0:r, s, :], s, i, r)

            def hi(s, i, r, n):
                act.wait_ge(S["t_done"][s], i + 1)
                act.activation(hT_hi[:, :, ds(n * P, r)], T[:, s, :, 0:r], ACT.Copy).then_inc(S["hi_done"][s], 1)

            over_blocks(act, (2, normalise), (1, hi))
            for m in range(2):
                weights.split_hi(act, m)

        @block.tensor
        def _(pe):
            def turn(s, i, r, n):
                pe.wait_ge(ln.done[s], i + 1)
                pe.wait_ge(S["lo_done"][s], i)
                for k in range(KD):
                    last = pe.transpose(T[:, s, k, 0:r], H[0:r, s, k * P:(k + 1) * P], ident[0:r, 0:r])
                last.then_inc(S["t_done"][s], 1)

            over_blocks(pe, (0, turn))


KINDS = ["dt"] + ["k"] * 4 + ["v"] * 4 + ["z"] * 4 + ["x"] * 4 + ["B"] * 2 + ["C"] * 2 + ["q"] * 4
COLUMN = [DIN - P] + [P * (NPAIR + n) for n in range(len(KINDS) - 1 - NPAIR)] + [P * n for n in range(NPAIR)]


class ProjectionWeights:

    def __init__(self, sem, place, w_in):
        self.w_in = w_in
        self.raw = place("pj_raw", [P, 2, KD, P])
        self.hi = [place(f"pj_w_hi{s}", [P, KD, P], F32R) for s in range(2)]
        self.lo = [place(f"pj_w_lo{s}", [P, KD, P], F32R) for s in range(2)]
        self.loaded, self.hi_done, self.lo_done, self.used = (
            [sem(f"pj_w_{n}{s}") for s in range(2)] for n in ("loaded", "hi_done", "lo_done", "used"))

    def load(self, sp, m, i=0):
        s = m % 2
        sp.wait_ge(self.lo_done[s], i + m // 2)
        col = COLUMN[m] + i * (2 * P) if m else COLUMN[0]
        sp.dma_start(self.raw[:, s, :, :], w_raw_view(self.w_in, col, P)).then_inc(self.loaded[s], 16)

    def split_hi(self, act, m, i=0):
        s = m % 2
        act.wait_ge(self.loaded[s], i * 16 + 16 * (m // 2 + 1))
        act.wait_ge(self.used[s], i + m // 2)
        act.activation(self.hi[s][:, :, :], self.raw[:, s, :, :], ACT.Copy).then_inc(self.hi_done[s], 1)

    def split_lo(self, dve, m, i=0):
        s = m % 2
        dve.wait_ge(self.hi_done[s], i + (m // 2 + 1))
        dve.tensor_tensor(self.lo[s][:, :, :], self.raw[:, s, :, :], self.hi[s][:, :, :].bitcast(F32),
                          ALU.subtract).then_inc(self.lo_done[s], 1)


def stage_projection(nc, sem, io, ident, hT_hi, hT_lo, weights, qT, kT, Xt, Bt, BT, CT, dt_raw, place):
    NBLK = len(KINDS)
    TURNED = ("dt", "k", "v", "z", "x", "B")
    STORED = ("k", "v", "z")
    CONV = ("x", "B", "C")
    COPIED = ("k", "B")
    LAST = CW - 1
    TAIL = LAST * (1 + DB)

    def before(n, kinds):
        return 1 + sum(KINDS[m] in kinds for m in range(n % 2, n, 2))

    def turned_before(n):
        return sum(KINDS[m] in TURNED for m in range(n))

    w_hi, w_lo, lo_done, mm_done = weights.hi, weights.lo, weights.lo_done, weights.used
    fT = place("pj_fT", [P, 2, TOK])
    SX = LAST + SEQ
    cv = place("pj_cv", [P, 2, SX + DB * (LAST + DT)])
    cc = place("pj_cc", [P, 2, TOK])
    stage = place("pj_stage", [P, 2, NB, P])
    conv_w = place("pj_conv_w", [P, NXBC, CW])
    conv_b = place("pj_conv_b", [P, NXBC])
    stateT = place("pj_stateT", [P, NXBC, DB * LAST])
    tail = place("pj_tail", [P, NXBC, TAIL])

    small_loaded, tail_stored, tcopy_done = sem("pj_small_loaded"), sem("pj_tail_stored"), sem("pj_tcopy_done")
    pad_set, v_chain = sem("pj_pad_set"), sem("pj_v_chain")
    two = lambda name: [sem(f"pj_{name}{s}") for s in range(2)]
    ev_done, t_done, stored, kept, conv_done, silu_done = two("ev_done"), two("t_done"), two("stored"), two("kept"), two("conv_done"), two("silu_done")
    tail_done, fill_done, tap = two("tail_done"), two("fill_done"), two("tap")

    def sample_view(ap, width):
        return ap.rearrange("p (b t) -> p b t", t=width)

    with ExitStack() as ctx:
        mm = ctx.enter_context(nc.psum_tensor("pj_mm", [P, 2, 3, 512], F32))
        T = ctx.enter_context(nc.psum_tensor("pj_T", [P, NQB, P], F32))
        Ts = [mm[0:NS, s, 2, 384:384 + P] for s in range(2)]
        block = ctx.enter_context(nc.Block())

        def steps(engine, step):
            n = 0
            while n < NBLK:
                if KINDS[n:n + 4] == [KINDS[n]] * 4 and n + 4 < NBLK:
                    with engine.Fori(0, 2) as i:
                        for u in range(2):
                            step(n + u, i, i * 2 + u)
                    n += 4
                else:
                    step(n, 0, n - KINDS.index(KINDS[n]))
                    n += 1

        @block.sync
        def _(sp):
            for s in range(2):
                for counted in (t_done, kept, conv_done, silu_done, tail_done, fill_done):
                    sp.sem_inc(counted[s], 1)
                sp.sem_inc(stored[s], 32)
            sp.dma_start(conv_w[:, :, :], io["conv_wT"]).then_inc(small_loaded, 16)
            sp.dma_start(conv_b[:, :], io["conv_bT"]).then_inc(small_loaded, 16)
            sp.dma_start(stateT[:, :, :], io["state_convT"]).then_inc(small_loaded, 16)
            weights.load(sp, 2)

            def step(n, i, j):
                if n + 3 < NBLK:
                    weights.load(sp, n + 3, i)
                if KINDS[n] in STORED:
                    s = n % 2
                    to = io[{"k": "new_k", "v": "new_v", "z": "z_act"}[KINDS[n]]]
                    sp.wait_ge(tcopy_done, i * 2 + (turned_before(n) + 1))
                    sp.dma_start(to[0:SEQ, ds(j * P, P)].rearrange("(b p) f -> p b f", p=P),
                                 stage[:, s, 0:NQB, :]).then_inc(stored[s], 16)
                    sp.dma_start(to[SEQ:TOK, ds(j * P, P)], stage[0:NS, s, NQB, :]).then_inc(stored[s], 16)

            steps(sp, step)
            for s in range(2):
                sp.wait_ge(tail_done[s], NXBC // 2 + 1)
            sp.dma_start(io["new_convT"], tail[:, :, :]).then_inc(tail_stored, 16)
            sp.wait_ge(tail_stored, 16)
            for s in range(2):
                sp.wait_ge(stored[s], 32 * (len([k for k in KINDS if k in STORED]) // 2 + 1))

        @block.scalar
        def _(act):
            def step(n, i, j):
                s, kind = n % 2, KINDS[n]
                if n + 2 < NBLK:
                    weights.split_hi(act, n + 2, i)
                act.wait_ge(mm_done[s], i + (n // 2 + 1))
                fT_free = kind in TURNED
                if kind in CONV:
                    act.wait_ge(conv_done[s], i + before(n, CONV))
                    act.wait_ge(tail_done[s], i + before(n, CONV))
                elif fT_free:
                    act.wait_ge(t_done[s], i + before(n, TURNED))
                    act.wait_ge(kept[s], i + before(n, COPIED) if kind == "k" else before(n, COPIED))
                for g, (c, w) in enumerate(GROUPS):
                    w_prompt = min(w, SEQ - c)
                    if kind in CONV:
                        last = act.activation(cv[:, s, LAST + c:LAST + c + w_prompt], mm[:, s, g, 0:w_prompt], ACT.Copy)
                        if w_prompt < w:
                            last = act.activation(sample_view(cv[:, s, SX:], LAST + DT)[:, :, LAST:],
                                                  sample_view(mm[:, s, g, w_prompt:w], DT), ACT.Copy)
                    else:
                        to = qT[:, ds(j, 1), c:c + w].squeeze(1) if kind == "q" else fT[:, s, c:c + w]
                        last = act.activation(to, mm[:, s, g, 0:w], ACT.Copy)
                last.then_inc(ev_done[s], 1)
                if kind == "z":
                    act.wait_ge(t_done[s], i + (before(n, TURNED) + 1))
                    act.wait_ge(stored[s], i * 32 + 32 * before(n, STORED))
                    act.activation(stage[:, s, 0:NQB, :], T[:, :, :], ACT.Silu)
                    act.activation(stage[0:NS, s, NQB, :], Ts[s], ACT.Silu).then_inc(tcopy_done, 1)
                if kind in CONV:
                    act.wait_ge(conv_done[s], i + (before(n, CONV) + 1))
                    if kind != "C":
                        act.wait_ge(t_done[s], i + before(n, TURNED))
                        act.wait_ge(kept[s], before(n, COPIED))
                    to = CT[:, j, :] if kind == "C" else fT[:, s, :]
                    act.activation(to, cc[:, s, :], ACT.Silu).then_inc(silu_done[s], 1)

            steps(act, step)

        @block.gpsimd
        def _(pool):
            for s in range(2):
                pool.memset(cv[:, s, 0:LAST], 0.0).then_inc(pad_set, 1)
            pool.wait_ge(small_loaded, 48)

            def step(n, i, j):
                s, kind = n % 2, KINDS[n]
                if kind in CONV:
                    jx = n - KINDS.index("x")
                    jx = j if kind == "x" else jx
                    pool.wait_ge(conv_done[s], i + before(n, CONV))
                    pool.tensor_copy(sample_view(cv[:, s, SX:], LAST + DT)[:, :, 0:LAST],
                                     sample_view(stateT[:, ds(jx, 1), :].squeeze(1), LAST)).then_inc(fill_done[s], 1)
                    pool.wait_ge(ev_done[s], i + (n // 2 + 1))
                    pool.tensor_copy(tail[:, ds(jx, 1), 0:LAST].squeeze(1), cv[:, s, SEQ:SEQ + LAST])
                    pool.tensor_copy(sample_view(tail[:, ds(jx, 1), LAST:].squeeze(1), LAST),
                                     sample_view(cv[:, s, SX:], LAST + DT)[:, :, DT:]).then_inc(tail_done[s], 1)
                if kind == "k":
                    pool.wait_ge(ev_done[s], i + (n // 2 + 1))
                    pool.tensor_copy(kT[:, ds(j, 1), :].squeeze(1), fT[:, s, :]).then_inc(kept[s], 1)
                if kind == "B":
                    pool.wait_ge(silu_done[s], before(n, CONV) + 1)
                    pool.tensor_copy(BT[:, j, :], fT[:, s, :]).then_inc(kept[s], 1)

            steps(pool, step)

        @block.vector
        def _(dve):
            def step(n, i, j):
                s, kind = n % 2, KINDS[n]
                if n + 2 < NBLK:
                    weights.split_lo(dve, n + 2, i)
                if kind in CONV:
                    jx = j if kind == "x" else n - KINDS.index("x")
                    dve.wait_ge(ev_done[s], i + (n // 2 + 1))
                    dve.wait_ge(fill_done[s], i + (before(n, CONV) + 1))
                    dve.wait_ge(silu_done[s], i + before(n, CONV))
                    base = i * LAST + LAST * (before(n, CONV) - 1)
                    for t in range(CW):
                        cw = conv_w[:, ds(jx, 1), t:t + 1].squeeze(1)
                        src = cv[:, s, t:t + SEQ]
                        src_s = sample_view(cv[:, s, SX:], LAST + DT)[:, :, t:t + DT]
                        out, out_s = cc[:, s, 0:SEQ], sample_view(cc[:, s, SEQ:], DT)
                        if t == 0:
                            cb = conv_b[:, ds(jx, 1)]
                            dve.tensor_scalar(out, src, cw, cb, ALU.mult, ALU.add)
                            dve.tensor_scalar(out_s, src_s, cw, cb, ALU.mult, ALU.add).then_inc(tap[s], 1)
                        else:
                            dve.wait_ge(tap[s], base + t)
                            dve.scalar_tensor_tensor(out, src, cw, out, ALU.mult, ALU.add)
                            last = dve.scalar_tensor_tensor(out_s, src_s, cw, out_s, ALU.mult, ALU.add)
                            last.then_inc(tap[s] if t < CW - 1 else conv_done[s], 1)
                if kind in TURNED and kind != "z":
                    dve.wait_ge(t_done[s], i + (before(n, TURNED) + 1))
                    if kind in STORED:
                        dve.wait_ge(stored[s], i * 32 + 32 * before(n, STORED))
                        to, to_s = stage[:, s, 0:NQB, :], stage[0:NS, s, NQB, :]
                    elif kind == "x":
                        to = Xt[:, 0:NQB, ds(j * P, P)]
                        to_s = Xt[0:NS, NQB, ds(j * P, P)]
                    elif kind == "B":
                        to, to_s = Bt[:, 0:NQB, j * P:(j + 1) * P], Bt[0:NS, NQB, j * P:(j + 1) * P]
                    else:
                        to, to_s = dt_raw[:, 0:NQB, :], dt_raw[0:NS, NQB, :]
                    c = P - NH if kind == "dt" else 0
                    dve.tensor_copy(to, T[:, :, c:])
                    dve.tensor_copy(to_s, Ts[s][:, c:]).then_inc(tcopy_done, 1)

            dve.wait_ge(small_loaded, 48)
            dve.wait_ge(pad_set, 2)
            steps(dve, step)

        @block.tensor
        def _(pe):
            def product(n, i, turned=0):
                s = n % 2
                pe.wait_ge(lo_done[s], i + (n // 2 + 1))
                pe.wait_ge(ev_done[s], i + n // 2)
                for g, (c, w) in enumerate(GROUPS):
                    if g == len(GROUPS) - 1:
                        pe.wait_ge(tcopy_done, turned)
                    for k in range(KD):
                        for part, (wt, ht) in enumerate(((w_hi, hT_hi), (w_hi, hT_lo), (w_lo, hT_hi))):
                            last = pe.matmul(mm[:, s, g, 0:w], wt[s][:, k, :], ht[:, k, c:c + w],
                                             start=(k == 0 and part == 0), stop=(k == KD - 1 and part == 2))
                last.then_inc(mm_done[s], 1)

            def step(n, i, j):
                s, kind = n % 2, KINDS[n]
                if n + 1 < NBLK:
                    product(n + 1, i, turned_before(n) + (i * 2 if kind in TURNED and not isinstance(i, int) else 0))
                if kind in TURNED:
                    if kind in CONV:
                        pe.wait_ge(silu_done[s], i + (before(n, CONV) + 1))
                    else:
                        pe.wait_ge(ev_done[s], i + (n // 2 + 1))
                    pe.wait_ge(tcopy_done, i * 2 + turned_before(n))
                    for b in range(NQB):
                        pe.transpose(T[:, b, :], fT[:, s, b * P:(b + 1) * P], ident[:, :])
                    pe.transpose(Ts[s], fT[:, s, SEQ:TOK], ident[:, :]).then_inc(t_done[s], 1)

            product(0, 0)
            steps(pe, step)
SSD_TABLES = (("ones", P, P), ("mask", P, P), ("mask_s", NS, NS), ("ones_s", NS, NS), ("in_seq", NS, DB), ("tri", P, P),
              ("tri_s", NS, NS))


def stage_ssd(nc, sem, io, ident, Xt, Bt, BT, CT, dt_raw, mixT, place):
    GW = DA // NGROUP
    C_ALL = NB * NH
    PC = NQB * NH

    def sb(name, shape):
        return place("sd_" + name, shape)

    tables = sb("tables", [P, sum(w for _, _, w in SSD_TABLES)])
    view, at = {}, 0
    for name, rows, width in SSD_TABLES:
        view[name] = tables[0:rows, at:at + width]
        at += width
    ones, mask, mask_s, ones_s, in_seq, tri, tri_s = (view[n] for n in "ones mask mask_s ones_s in_seq tri tri_s".split())
    bias, a_log, skip, norm_w = sb("bias", [P, NH]), sb("a_log", [P, NH]), sb("skip", [P, NH]), sb("norm_w", [P, NPAIR])
    d, ab, ex, dt, adt, ea = (sb(n, [P, C_ALL]) for n in ("d", "ab", "ex", "dt", "adt", "ea"))
    acs, rest, decay, eacs, etot = (sb(n, [P, C_ALL]) for n in ("acs", "rest", "decay", "eacs", "etot"))
    adt_b, etot_s = sb("adt_b", [NS, DB, NH]), sb("etot_s", [P, DB * NH])
    mhalf = sb("mhalf", [P, NGROUP])
    state = sb("state", [P, DA])
    state_s = sb("state_s", [P, DB, DA])
    E = sb("E", [P, 2, NH, P])
    xdt, xdd, xsk, zt, Y = (sb(n, [P, 2, DA]) for n in ("xdt", "xdd", "xsk", "zt", "Y"))
    off, junk, off_junk = sb("off", [P, DA]), sb("junk", [P, GW]), sb("junk2", [P, GW])
    BTs, CTs, Bts = (sb(n, [P, 2, NGROUP, P]) for n in ("BTs", "CTs", "Bts"))
    adts = sb("adts", [P, 2, NH])
    Cz = sb("Cz", [P, NGROUP, DB * (NS + DT)])
    Bz = sb("Bz", [NS, DB, GW])
    ssq, ms, rs = sb("ssq", [P, 2, NGROUP]), sb("ms", [P, 2, NGROUP]), sb("rs", [P, 2, NGROUP])

    names = ("loaded state_loaded zeroed pad_set pre adt_ready sums_done acs_ready decay_ready cz_ready bz_ready staged staged2 x_ready gr_done z_done "
             "e_done m_done y_mm o_mm s_mm off_done st_scaled st_done y1_done xsk_done y2_done y3_done ssq_done "
             "ms_done rs_done yn_done t_mm ty_done st_out").split()
    S = {n: sem("sd_" + n) for n in names}
    z_loaded = [sem(f"sd_z_loaded{s}") for s in range(2)]
    heads = lambda ap: ap.rearrange("p (h f) -> p h f", f=HD)

    def chunk_cols(t, c):
        return t[:, c * NH:(c + 1) * NH] if isinstance(c, int) else t[:, ds(c * NH, NH)]

    def per_head(ap, r):
        return ap[0:r].unsqueeze(2).to_broadcast([r, NH, HD])

    def wait(engine, name, value):
        if not isinstance(value, int) or value > 0:
            engine.wait_ge(S[name], value)

    def run(engine, front, back, gate, turn, straight=False):
        def body(i):
            for u in range(2):
                front(i * 2 + (2 + u), u)
                back(i * 2 + (1 + u), 1 - u)
                if not (isinstance(i, int) and i * 2 + u == 0):
                    turn(i * 2 + u - 1, 1 - u)
                gate(i * 2 + u, u)

        front(0, 0)
        front(1, 1)
        back(0, 0)
        body(0)
        if straight:
            for i in range(1, NQB // 2 - 1):
                body(i)
        else:
            with engine.Fori(1, NQB // 2 - 1) as i:
                body(i)
        back(NQB - 1, 1)
        turn(NQB - 3, 1)
        gate(NQB - 2, 0)
        turn(NQB - 2, 0)
        gate(NQB - 1, 1)
        turn(NQB - 1, 1)
        front(NQB, 0)
        back(NQB, 0)
        gate(NQB, 0)
        turn(NQB, 0)

    nothing = lambda *a: None
    is_sample = lambda c: isinstance(c, int) and c == NQB

    with ExitStack() as ctx:
        G = [ctx.enter_context(nc.psum_tensor(f"sd_G{s}", [P, NGROUP, P], F32)) for s in range(2)]
        R = ctx.enter_context(nc.psum_tensor("sd_R", [P, NH, P], F32))
        pY = ctx.enter_context(nc.psum_tensor("sd_pY", [P, DA], F32))
        pO = ctx.enter_context(nc.psum_tensor("sd_pO", [P, DA], F32))
        pS = ctx.enter_context(nc.psum_tensor("sd_pS", [P, DA], F32))
        added = [pS[:, :]] + [R[:, 4 * k:4 * k + 4, :].rearrange("p a b -> p (a b)") for k in range(2)]
        pT = ctx.enter_context(nc.psum_tensor("sd_pT", [P, NPAIR, P], F32))
        block = ctx.enter_context(nc.Block())

        @block.sync
        def _(sp):
            sp.dma_start(tables[:, :], io["c_ssd"]).then_inc(S["loaded"], 16)
            for t, name in ((bias, "dt_bias"), (a_log, "a_log"), (skip, "d_skip")):
                sp.dma_start(t[:, :], io[name].partition_broadcast(P)).then_inc(S["loaded"], 16)
            sp.dma_start(norm_w[:, :], io["norm_wT"]).then_inc(S["loaded"], 16)
            sp.dma_start(state_s[:, :, :], io["state_ssmT"]).then_inc(S["state_loaded"], 16)

            def front(c, s):
                wait(sp, "y3_done", c - 1)
                rows = NS if is_sample(c) else P
                sp.dma_start(zt[0:rows, s, :], io["z_act"][ds(c * P, rows), :]).then_inc(z_loaded[s], 16)

            run(sp, front, nothing, nothing, nothing)
            wait(sp, "st_done", NQB)
            sp.dma_start(io["new_ssm_promptT"], state[:, :]).then_inc(S["st_out"], 16)
            wait(sp, "st_done", NQB + DB)
            sp.dma_start(io["new_ssm_sampleT"], state_s[:, :, :]).then_inc(S["st_out"], 16)
            wait(sp, "st_out", 32)

        @block.gpsimd
        def _(pool):
            pool.memset(mhalf[:, :], -0.5).then_inc(S["pad_set"], 1)
            pool.memset(state[:, :], 0.0).then_inc(S["zeroed"], 1)
            pool.memset(Cz[:, :, :], 0.0).then_inc(S["pad_set"], 1)
            wait(pool, "pad_set", 3)
            for g in range(NGROUP):
                last = pool.tensor_copy(Cz[:, g, :].rearrange("p (b t) -> p b t", t=NS + DT)[:, :, 0:DT],
                                        CT[:, g, SEQ:TOK].rearrange("p (b t) -> p b t", t=DT))
            last.then_inc(S["cz_ready"], 1)
            wait(pool, "loaded", 80)

            def back(c, s):
                r = NS if is_sample(c) else P
                x = Xt[0:r, ds(c, 1), :].squeeze(1)
                wait(pool, "y2_done", c - 1)
                pool.tensor_tensor(heads(xsk[0:r, s, :]), heads(x), per_head(skip, r), ALU.mult).then_inc(S["xsk_done"], 1)

            def gate(c, s):
                r = NS if is_sample(c) else P
                wait(pool, "y1_done", c + 1)
                wait(pool, "xsk_done", c + 1)
                pool.tensor_tensor(Y[0:r, s, :], Y[0:r, s, :], xsk[0:r, s, :], ALU.add).then_inc(S["y2_done"], 1)
                wait(pool, "y2_done", c + 1)
                pool.wait_ge(z_loaded[s], 16 + 16 * (NQB // 2) if is_sample(c) else 16 * (c // 2 + 1) if isinstance(c, int)
                             else (c - s) * 8 + 16)
                pool.tensor_tensor(Y[0:r, s, :], Y[0:r, s, :], zt[0:r, s, :], ALU.mult).then_inc(S["y3_done"], 1)
                wait(pool, "pad_set", 3)
                wait(pool, "ssq_done", c + 1)
                pool.tensor_scalar(ms[0:r, s, :], ssq[0:r, s, :], 1.0 / GW, EPS, ALU.mult, ALU.add).then_inc(S["ms_done"], 1)
                wait(pool, "ms_done", c + 1)
                pool.tensor_tensor(rs[0:r, s, :], ms[0:r, s, :], mhalf[0:r, :], ALU.pow).then_inc(S["rs_done"], 1)

            run(pool, nothing, back, gate, nothing)

        @block.vector
        def _(dve):
            dve.memset(dt_raw[NS:P, NQB, :], 0.0).then_inc(S["pad_set"], 1)
            wait(dve, "loaded", 80)
            wait(dve, "pad_set", 3)
            by_chunk = lambda t: t[:, :].rearrange("p (c h) -> p c h", h=NH)
            over_chunks = lambda t: t[:, 0:NH].unsqueeze(1).to_broadcast([P, NB, NH])
            dve.tensor_tensor(by_chunk(d), dt_raw[:, :, :], over_chunks(bias), ALU.add).then_inc(S["pre"], 1)
            wait(dve, "pre", 5)
            dve.scalar_tensor_tensor(dt[:, :], d[:, :], 0.0, ex[:, :], ALU.max, ALU.add).then_inc(S["pre"], 1)
            wait(dve, "pre", 6)
            dve.scalar_tensor_tensor(by_chunk(adt), by_chunk(dt), -1.0, over_chunks(ea), ALU.mult,
                                     ALU.mult).then_inc(S["adt_ready"], 1)
            wait(dve, "adt_ready", 1)
            dve.tensor_tensor(adt_b[:, :, :], adt[0:NS, PC:].unsqueeze(1).to_broadcast([NS, DB, NH]),
                              in_seq[:, :].unsqueeze(2).to_broadcast([NS, DB, NH]), ALU.mult).then_inc(S["adt_ready"], 1)
            for b in range(DB):
                last = dve.tensor_scalar(Bz[:, b, :], Bt[0:NS, NQB, :], in_seq[:, b:b + 1], None, ALU.mult)
            last.then_inc(S["bz_ready"], 1)
            wait(dve, "sums_done", 1)
            dve.tensor_copy(acs[:, 0:PC], pY[:, 0:PC])
            dve.tensor_copy(acs[0:NS, PC:], pY[0:NS, PC:C_ALL]).then_inc(S["acs_ready"], 1)
            wait(dve, "acs_ready", 1)
            dve.tensor_tensor(rest[:, 0:PC], pO[:, 0:PC], acs[:, 0:PC], ALU.subtract)
            dve.tensor_tensor(rest[0:NS, PC:], pO[0:NS, PC:C_ALL], acs[0:NS, PC:], ALU.subtract).then_inc(S["acs_ready"], 1)

            def front(c, s):
                r = NS if is_sample(c) else P
                wait(dve, "gr_done", c + 1)
                m = mask_s if is_sample(c) else mask
                for h in range(NH):
                    last = dve.scalar_tensor_tensor(E[0:r, s, h, 0:r], R[0:r, h, 0:r], chunk_cols(acs, c)[0:r, h:h + 1],
                                                    m[0:r, 0:r], ALU.subtract, ALU.add)
                last.then_inc(S["z_done"], 1)
                wait(dve, "decay_ready", 1)
                wait(dve, "s_mm", c - 1)
                x = Xt[0:r, ds(c, 1), :].squeeze(1)
                dve.tensor_tensor(heads(xdt[0:r, s, :]), heads(x), per_head(chunk_cols(dt, c), r),
                                  ALU.mult).then_inc(S["x_ready"], 1)
                dve.wait_ge(S["x_ready"], c * 2 + 1)
                dve.tensor_tensor(heads(xdd[0:r, s, :]), heads(xdt[0:r, s, :]), per_head(chunk_cols(decay, c), r),
                                  ALU.mult).then_inc(S["x_ready"], 1)
                wait(dve, "e_done", c + 1)
                for g in range(NGROUP):
                    e = E[0:r, s, g * HPG:(g + 1) * HPG, 0:r]
                    last = dve.tensor_tensor(e, e, G[s][0:r, g, 0:r].unsqueeze(1).to_broadcast([r, HPG, r]), ALU.mult)
                last.then_inc(S["m_done"], 1)

            def back(c, s):
                r = NS if is_sample(c) else P
                wait(dve, "o_mm", c + 1)
                wait(dve, "y1_done", c)
                dve.tensor_tensor(heads(off[0:r, :]), heads(pO[0:r, :]), per_head(chunk_cols(eacs, c), r),
                                  ALU.mult).then_inc(S["off_done"], 1)
                if is_sample(c):
                    wait(dve, "state_loaded", 16)
                    dve.tensor_tensor(state_s[:, :, :].rearrange("p b (h f) -> p (b h) f", f=HD),
                                      state_s[:, :, :].rearrange("p b (h f) -> p (b h) f", f=HD),
                                      etot_s[:, :].unsqueeze(2).to_broadcast([P, DB * NH, HD]),
                                      ALU.mult).then_inc(S["st_scaled"], 1)
                    wait(dve, "st_scaled", c + 1)
                    for b in range(DB):
                        wait(dve, "s_mm", c + 1 + b)
                        dve.tensor_tensor(state_s[:, b, :], state_s[:, b, :], added[b % 3], ALU.add).then_inc(S["st_done"], 1)
                else:
                    wait(dve, "zeroed", 1)
                    wait(dve, "st_done", c)
                    dve.tensor_tensor(heads(state[:, :]), heads(state[:, :]), per_head(chunk_cols(etot, c), P),
                                      ALU.mult).then_inc(S["st_scaled"], 1)
                    wait(dve, "st_scaled", c + 1)
                    wait(dve, "s_mm", c + 1)
                    dve.tensor_tensor(state[:, :], state[:, :], pS[:, :], ALU.add).then_inc(S["st_done"], 1)
                wait(dve, "off_done", c + 1)
                wait(dve, "t_mm", c - 1)
                dve.tensor_tensor(Y[0:r, s, :], off[0:r, :], pY[0:r, :], ALU.add).then_inc(S["y1_done"], 1)

            run(dve, front, back, nothing, nothing)

        @block.scalar
        def _(act):
            wait(act, "pre", 1)
            act.activation(ab[:, :], d[:, :], ACT.Abs).then_inc(S["pre"], 1)
            wait(act, "pre", 2)
            act.activation(ab[:, :], ab[:, :], ACT.Exp, scale=-1.0).then_inc(S["pre"], 1)
            wait(act, "loaded", 80)
            act.activation(ea[:, 0:NH], a_log[:, :], ACT.Exp).then_inc(S["pre"], 1)
            wait(act, "pre", 4)
            act.activation(ex[:, :], ab[:, :], ACT.Ln, bias=1.0).then_inc(S["pre"], 1)
            wait(act, "acs_ready", 2)
            act.activation(decay[:, 0:PC], rest[:, 0:PC], ACT.Exp)
            act.activation(decay[0:NS, PC:], rest[0:NS, PC:], ACT.Exp)
            act.activation(eacs[:, 0:PC], acs[:, 0:PC], ACT.Exp)
            act.activation(eacs[0:NS, PC:], acs[0:NS, PC:], ACT.Exp)
            act.activation(etot[:, 0:PC], pO[:, 0:PC], ACT.Exp)
            act.activation(etot_s[:, :], pS[:, 0:DB * NH], ACT.Exp).then_inc(S["decay_ready"], 1)

            def stage_first(c, s):
                wait(act, "gr_done", c - 1)
                act.activation(BTs[:, s, :, :], BT[:, :, ds(c * P, P)], ACT.Copy)
                act.activation(adts[:, s, :], chunk_cols(adt, c), ACT.Copy).then_inc(S["staged"], 1)

            def stage_second(c, s):
                wait(act, "s_mm", c - 1)
                act.activation(CTs[:, s, :, :], CT[:, :, ds(c * P, P)], ACT.Copy)
                act.activation(Bts[:, s, :, :], Bt[:, ds(c, 1), :].squeeze(1).rearrange("p (g n) -> p g n", n=P),
                               ACT.Copy).then_inc(S["staged2"], 1)

            def stage(c, s):
                if c + 2 < NQB:
                    stage_first(c + 2, s)
                if c + 1 < NQB:
                    stage_second(c + 1, 1 - s)

            def front(c, s):
                r = NS if is_sample(c) else P
                wait(act, "z_done", c + 1)
                act.activation(E[0:r, s, :, 0:r], E[0:r, s, :, 0:r], ACT.Exp).then_inc(S["e_done"], 1)

            def scale(c, s):
                r = NS if is_sample(c) else P
                wait(act, "y3_done", c + 1)
                for g in range(NGROUP):
                    wait(act, "ssq_done", c if g == 0 else c)
                    last = act.activation(junk[0:r, :] if g == 0 else off_junk[0:r, :], Y[0:r, s, g * GW:(g + 1) * GW],
                                          ACT.Square, accum_out=ssq[0:r, s, g:g + 1])
                last.then_inc(S["ssq_done"], 1)
                wait(act, "rs_done", c + 1)
                wait(act, "ssq_done", c + 1)
                for g in range(NGROUP):
                    y = Y[0:r, s, g * GW:(g + 1) * GW]
                    last = act.activation(y, y, ACT.Copy, scale=rs[0:r, s, g:g + 1])
                last.then_inc(S["yn_done"], 1)

            def turn(c, s):
                r = NS if is_sample(c) else P
                wait(act, "t_mm", c + 1)
                for j in range(NPAIR):
                    last = act.activation(mixT[:, NPAIR + j, ds(c * P, r)], pT[:, j, 0:r], ACT.Copy, scale=norm_w[:, j:j + 1])
                last.then_inc(S["ty_done"], 1)

            wait(act, "adt_ready", 1)
            stage_first(0, 0)
            stage_first(1, 1)
            stage_second(0, 0)
            run(act, front, stage, scale, turn, straight=True)

        @block.tensor
        def _(pe):
            wait(pe, "adt_ready", 2)
            wait(pe, "loaded", 80)
            pe.matmul(pY[:, 0:PC], tri[:, :], adt[:, 0:PC], start=True, stop=True)
            pe.matmul(pY[0:NS, PC:C_ALL], tri_s[:, :], adt[0:NS, PC:], start=True, stop=True)
            pe.matmul(pO[:, 0:PC], ones[:, :], adt[:, 0:PC], start=True, stop=True)
            pe.matmul(pO[0:NS, PC:C_ALL], ones_s[:, :], adt[0:NS, PC:], start=True, stop=True)
            pe.matmul(pS[:, 0:DB * NH], ones[0:NS, :], adt_b[:, :, :].rearrange("p b h -> p (b h)"), start=True,
                      stop=True).then_inc(S["sums_done"], 1)

            def front(c, s):
                wait(pe, "m_done", c - 1)
                if is_sample(c):
                    for g in range(NGROUP):
                        pe.matmul(G[s][0:NS, g, 0:NS], BT[:, g, SEQ:TOK], CT[:, g, SEQ:TOK], start=True, stop=True)
                    wait(pe, "z_done", c)
                    for h in range(NH):
                        last = pe.matmul(R[0:NS, h, 0:NS], adt[0:NS, PC + h:PC + h + 1].to_broadcast([NS, NS]), tri_s[:, :],
                                         start=True, stop=True)
                else:
                    wait(pe, "staged", c + 1)
                    for g in range(NGROUP):
                        pe.matmul(G[s][:, g, :], BTs[:, s, g, :], CT[:, g, ds(c * P, P)], start=True, stop=True)
                    wait(pe, "z_done", c)
                    for h in range(NH):
                        last = pe.matmul(R[:, h, :], adts[:, s, h:h + 1].to_broadcast([P, P]), tri[:, :], start=True, stop=True)
                last.then_inc(S["gr_done"], 1)

            def back(c, s):
                r = NS if is_sample(c) else P
                wait(pe, "m_done", c + 1)
                wait(pe, "y1_done", c)
                wait(pe, "decay_ready", 1)
                for h in range(NH):
                    last = pe.matmul(pY[0:r, h * HD:(h + 1) * HD], E[0:r, s, h, 0:r], xdt[0:r, s, h * HD:(h + 1) * HD],
                                     start=True, stop=True)
                last.then_inc(S["y_mm"], 1)
                wait(pe, "off_done", c)
                wait(pe, "st_done", c)
                wait(pe, "zeroed", 1)
                if is_sample(c):
                    wait(pe, "cz_ready", 1)
                    wait(pe, "bz_ready", 1)
                    wait(pe, "state_loaded", 16)
                    for g in range(NGROUP):
                        for b in range(DB):
                            last = pe.matmul(pO[0:NS, g * GW:(g + 1) * GW], Cz[:, g, b * NS:(b + 1) * NS],
                                             state_s[:, b, g * GW:(g + 1) * GW], start=(b == 0), stop=(b == DB - 1))
                    last.then_inc(S["o_mm"], 1)
                    for b in range(DB):
                        wait(pe, "st_done", c + b - 2)
                        for g in range(NGROUP):
                            last = pe.matmul(added[b % 3][:, g * GW:(g + 1) * GW], Bz[:, b, g * P:(g + 1) * P],
                                             xdd[0:NS, s, g * GW:(g + 1) * GW], start=True, stop=True)
                        last.then_inc(S["s_mm"], 1)
                else:
                    wait(pe, "staged2", c + 1)
                    for g in range(NGROUP):
                        last = pe.matmul(pO[:, g * GW:(g + 1) * GW], CTs[:, s, g, :], state[:, g * GW:(g + 1) * GW],
                                         start=True, stop=True)
                    last.then_inc(S["o_mm"], 1)
                    for g in range(NGROUP):
                        last = pe.matmul(pS[:, g * GW:(g + 1) * GW], Bts[:, s, g, :], xdd[:, s, g * GW:(g + 1) * GW],
                                         start=True, stop=True)
                    last.then_inc(S["s_mm"], 1)

            def turn(c, s):
                r = NS if is_sample(c) else P
                wait(pe, "yn_done", c + 1)
                wait(pe, "ty_done", c)
                for j in range(NPAIR):
                    last = pe.transpose(pT[:, j, 0:r], Y[0:r, s, j * P:(j + 1) * P], ident[0:r, 0:r])
                last.then_inc(S["t_mm"], 1)

            run(pe, front, back, nothing, turn)


def shape_constants():
    k = np.arange(P)
    tok = np.arange(NS)
    same = (tok[:, None] // DT) == (tok[None, :] // DT)
    causal_s = same & (tok[:, None] <= tok[None, :])
    tables = {
        "ones": np.ones((P, P)),
        "mask": np.where(k[:, None] <= k[None, :], 0, NEG),
        "mask_s": np.where(causal_s, 0, NEG),
        "ones_s": same,
        "in_seq": (tok[:, None] // DT) == np.arange(DB)[None, :],
        "tri": k[:, None] <= k[None, :],
        "tri_s": causal_s,
    }
    rows = lambda t: np.concatenate([t, np.zeros((P - len(t), t.shape[1]))])
    return {"c_ident": np.eye(P, dtype=np.float32),
            "c_ssd": np.concatenate([rows(tables[n]) for n, _, _ in SSD_TABLES], axis=1).astype(np.float32)}
def alibi(h, dist):
    slope = np.float32(2.0 ** (-8.0 * (h + 1) / NH))
    count = sum(((dist >= 0) & (dist <= w) & (dist % r == 0)).astype(np.float64) for w, r in BRANCHES)
    return np.where(count > 0, -slope * dist + np.log(np.maximum(count, 1)), NEG).astype(np.float32)


def attention_constants():
    p = np.arange(P)[:, None]
    wide = SEQ - P + p - np.arange(SEQ)[None, :]
    table = np.stack([alibi(h, wide) for h in range(NH)])
    t = np.arange(DT)[:, None]
    past = np.concatenate([alibi(h, PAST + t - np.arange(PAST)[None, :]) for h in range(NH)])
    new = np.full((NH * DT, (2 * DB - 1) * DT), NEG, np.float32)
    own = np.concatenate([alibi(h, t - np.arange(DT)[None, :]) for h in range(NH)])
    new[:, (DB - 1) * DT:DB * DT] = own
    return {"c_alibi": table, "c_alibi_past": past, "c_alibi_new": new}


def load_keys(sp, io, Kc, loaded, b, s):
    sp.dma_start(Kc[:, s, :, :], io["cache_kT"][ds(b, 1)].squeeze(0)).then_inc(loaded[s], 16)


def load_values(sp, io, Vc, loaded, b, s):
    sp.dma_start(Vc[:, s, :, :], io["cache_v"][ds(b, 1)].squeeze(0).rearrange("(n p) f -> p n f", p=P)).then_inc(loaded[s], 16)


def stage_prompt_attention(nc, sem, io, ident, qT, kT, mixT, place, prefetch):
    qz = [place(f"pa_qz{u}", [P, SEQ]) for u in range(2)]
    table = place("pa_table", [P, 2, SEQ])
    V = [place(f"pa_V{u}", [P, NQB, P]) for u in range(2)]
    NZ = 4
    Z = place("pa_Z", [P, NZ, SEQ])
    PT = [place(f"pa_PT{s}", [P, NQB, P]) for s in range(2)]
    nmax, total, inv = (place("pa_" + n, [P, NZ, 1]) for n in ("nmax", "total", "inv"))
    S = {n: sem("pa_" + n) for n in ("zeroed", "qk", "z", "max", "exp", "inv", "norm", "turn", "pt", "pv")}
    out_done = [sem(f"pa_out{s}") for s in range(2)]
    staged = [sem(f"pa_staged{u}") for u in range(2)]
    loaded = [sem(f"pa_loaded{u}") for u in range(2)]
    ITEMS = 2 * NQB
    head_of = lambda m: m // NQB % 2
    block_of = lambda m: m % ITEMS if m % ITEMS < NQB else ITEMS - 1 - m % ITEMS
    pair_of = lambda i, m: i + m // ITEMS
    keys = lambda m: (block_of(m) + 1) * P
    groups = lambda m: -(-(block_of(m) + 1) // 4)
    groups_to = lambda m: sum(groups(k) for k in range(m))
    G_ALL = groups_to(ITEMS)

    def pipeline(engine, lead, first, second, third):
        def step(i, m, last):
            if not last or m + lead < ITEMS:
                first(i, m + lead)
            second(i, m)
            if not isinstance(i, int) or i * ITEMS + m:
                third(i, m - 1)

        for m in range(lead):
            first(0, m)
        for m in range(NZ):
            step(0, m, False)
        with engine.Fori(0, NPAIR - 1) as i:
            for m in range(NZ, ITEMS + NZ):
                step(i, m, False)
        for m in range(NZ, ITEMS):
            step(NPAIR - 1, m, True)
        third(NPAIR - 1, ITEMS - 1)

    no_step = lambda i, m: None

    with ExitStack() as ctx:
        pS = [ctx.enter_context(nc.psum_tensor(f"pa_S{s}", [P, SEQ], F32)) for s in range(2)]
        pT = [ctx.enter_context(nc.psum_tensor(f"pa_T{s}", [P, 4, P], F32)) for s in range(2)]
        pO = [ctx.enter_context(nc.psum_tensor(f"pa_O{s}", [P, P], F32)) for s in range(2)]
        block = ctx.enter_context(nc.Block())

        @block.sync
        def _(sp):
            def load(i, u):
                sp.dma_start(table[:, u, :], io["c_alibi"][ds(i * 2 + u, 1)].squeeze(0)).then_inc(loaded[u], 16)
                sp.dma_start(V[u][:, :, :], io["new_v"][0:SEQ, ds(i * P, P)].rearrange("(b p) f -> p b f", p=P))\
                    .then_inc(loaded[u], 16)

            load(0, 0)
            load(0, 1)
            with sp.Fori(0, NPAIR - 1) as i:
                for u in range(2):
                    sp.wait_ge(S["z"], i * ITEMS + (u + 1) * NQB)
                    sp.wait_ge(S["pv"], i * ITEMS + (u + 1) * NQB)
                    load(i + 1, u)
            prefetch(sp)

        @block.gpsimd
        def _(pool):
            for u in range(2):
                pool.memset(qz[u][(1 - u) * HD:(2 - u) * HD, :], 0.0).then_inc(S["zeroed"], 1)
                pool.wait_ge(S["zeroed"], u + 1)

            def norm(i, m):
                z = Z[:, m % NZ, 0:keys(m)]
                pool.wait_ge(S["inv"], i * ITEMS + (m + 1))
                pool.tensor_tensor(z, z, inv[:, m % NZ, :].to_broadcast([P, keys(m)]), ALU.mult).then_inc(S["norm"], 1)

            pipeline(pool, 0, no_step, norm, no_step)

        @block.vector
        def _(dve):
            def stage(pair, u):
                dve.tensor_copy(qz[u][u * HD:(u + 1) * HD, :],
                                qT[u * HD:(u + 1) * HD, ds(pair, 1), 0:SEQ].squeeze(1)).then_inc(staged[u], 1)

            def scores(i, m):
                n, u, at = keys(m), head_of(m), i * ITEMS + (m + 1)
                if m % NQB == 0:
                    dve.wait_ge(loaded[u], pair_of(i, m) * 32 + 32)
                dve.wait_ge(S["qk"], at)
                if m >= NZ:
                    dve.wait_ge(S["turn"], i * G_ALL + groups_to(m - NZ + 1))
                z = Z[:, m % NZ, 0:n]
                dve.scalar_tensor_tensor(z, pS[m % 2][:, 0:n], HD ** -0.5, table[:, u, SEQ - n:SEQ], ALU.mult,
                                         ALU.add).then_inc(S["z"], 1)
                dve.wait_ge(S["z"], at)
                dve.reduce_max(nmax[:, m % NZ, :], z, AX.X, negate=True).then_inc(S["max"], 1)

            def invert(i, m):
                dve.wait_ge(S["exp"], i * ITEMS + (m + 1))
                dve.reciprocal(inv[:, m % NZ, :], total[:, m % NZ, :]).then_inc(S["inv"], 1)
                if (m + 1) % NQB == 0 and not (isinstance(i, int) and i == NPAIR - 1):
                    dve.wait_ge(S["qk"], i * ITEMS + (m + 1))
                    stage(pair_of(i, m) + 1, head_of(m))

            stage(0, 0)
            stage(0, 1)
            pipeline(dve, 1, scores, invert, no_step)

        @block.scalar
        def _(act):
            def exps(i, m):
                z = Z[:, m % NZ, 0:keys(m)]
                act.wait_ge(S["max"], i * ITEMS + (m + 1))
                act.activation(z, z, ACT.Exp, bias=nmax[:, m % NZ, :], accum_out=total[:, m % NZ, :]).then_inc(S["exp"], 1)

            def read_turned(i, m):
                if m >= 2:
                    act.wait_ge(S["pv"], i * ITEMS + (m - 1))
                for g in range(groups(m)):
                    t = groups_to(m) + g
                    k = min(4, block_of(m) + 1 - 4 * g)
                    act.wait_ge(S["turn"], i * G_ALL + (t + 1))
                    act.activation(PT[m % 2][:, 4 * g:4 * g + k, :], pT[t % 2][:, 0:k, :], ACT.Copy).then_inc(S["pt"], 1)

            def out(i, m):
                u, b = head_of(m), block_of(m)
                act.wait_ge(S["pv"], i * ITEMS + (m + 1))
                act.activation(mixT[u * HD:(u + 1) * HD, ds(pair_of(i, m), 1), b * P:(b + 1) * P].squeeze(1),
                               pO[m % 2][u * HD:(u + 1) * HD, :], ACT.Copy).then_inc(out_done[m % 2], 1)

            pipeline(act, 2, exps, read_turned, out)

        @block.tensor
        def _(pe):
            def qk(i, m):
                u, b, n = head_of(m), block_of(m), keys(m)
                if m % NQB == 0:
                    pe.wait_ge(staged[u], pair_of(i, m) + 1)
                if m >= 2:
                    pe.wait_ge(S["z"], i * ITEMS + (m - 1))
                for c in range(0, n, 512):
                    w = min(512, n - c)
                    last = pe.matmul(pS[m % 2][:, c:c + w], qz[u][:, b * P:(b + 1) * P],
                                     kT[:, ds(pair_of(i, m), 1), c:c + w].squeeze(1), start=True, stop=True)
                last.then_inc(S["qk"], 1)

            def turn(i, m):
                pe.wait_ge(S["norm"], i * ITEMS + (m + 1))
                for g in range(groups(m)):
                    t = groups_to(m) + g
                    if t >= 2:
                        pe.wait_ge(S["pt"], i * G_ALL + (t - 1))
                    for k in range(min(4, block_of(m) + 1 - 4 * g)):
                        kb = 4 * g + k
                        last = pe.transpose(pT[t % 2][:, k, :], Z[:, m % NZ, kb * P:(kb + 1) * P], ident[:, :])
                    last.then_inc(S["turn"], 1)

            def pv(i, m):
                u, nk = head_of(m), block_of(m) + 1
                if m % NQB == 0:
                    pe.wait_ge(loaded[u], pair_of(i, m) * 32 + 32)
                pe.wait_ge(S["pt"], i * G_ALL + groups_to(m + 1))
                pe.wait_ge(out_done[m % 2], i * (ITEMS // 2) + m // 2)
                for kb in range(nk):
                    last = pe.matmul(pO[m % 2][:, :], V[u][:, kb, :], PT[m % 2][:, kb, :], start=(kb == 0), stop=(kb == nk - 1))
                last.then_inc(S["pv"], 1)

            pe.wait_ge(S["zeroed"], 2)
            pipeline(pe, 3, qk, turn, pv)


def stage_sample_attention(nc, sem, io, ident, qT, kT, mixT, Kc, Vc, keys_loaded, values_loaded, place, prefetch):
    R = NH * DT
    past, new = place("sa_past", [R, PAST]), place("sa_new", [R, (2 * DB - 1) * DT])
    Vn = place("sa_Vn", [NS, DA])
    Q = [place(f"sa_Q{s}", [P, NPAIR * (R + 2 * DT)]) for s in range(2)]
    Z = place("sa_Z", [R, 2, PAST + NS])
    PT = [place(f"sa_PT{s}", [P, NQB + 1, R]) for s in range(2)]
    O = place("sa_O", [R, DA])
    nmax, total, inv = (place("sa_" + n, [R, 2, 1]) for n in ("nmax", "total", "inv"))
    tables_loaded, turn_begun = sem("sa_tables_loaded"), sem("sa_turn_begun")
    two = lambda n: [sem(f"sa_{n}{s}") for s in range(2)]
    zeroed, q_ready, qk, z, mx, ex, iv, norm, turn, pt, pv, copied, o_turn, out = (
        two(n) for n in ("zeroed", "q_ready", "qk", "z", "max", "exp", "inv", "norm", "turn", "pt", "pv", "copied", "o_turn", "out"))

    def over_sequences(engine, first, second, third, fourth=nothing):
        def step(b, s, i):
            first(b + 1, 1 - s, i + s)
            second(b, s, i)
            third(b + 1, 1 - s, i + s)
            fourth(b, s, i)

        first(0, 0, 0)
        third(0, 0, 0)
        for s in range(2):
            step(s, s, 0)
        with engine.Fori(1, DB // 2 - 1) as i:
            for s in range(2):
                step(i * 2 + s, s, i)
        last = DB // 2 - 1
        step(DB - 2, 0, last)
        second(DB - 1, 1, last)
        fourth(DB - 1, 1, last)

    with ExitStack() as ctx:
        pS = ctx.enter_context(nc.psum_tensor("sa_S", [R, 3, 512], F32))
        pT = ctx.enter_context(nc.psum_tensor("sa_T", [P, 2, 512], F32))
        pO = ctx.enter_context(nc.psum_tensor("sa_pO", [R, DA], F32))
        pX = ctx.enter_context(nc.psum_tensor("sa_pX", [P, NPAIR * (R + 2 * DT)], F32))
        block = ctx.enter_context(nc.Block())

        @block.sync
        def _(sp):
            sp.dma_start(past[:, :], io["c_alibi_past"]).then_inc(tables_loaded, 16)
            sp.dma_start(new[:, :], io["c_alibi_new"]).then_inc(tables_loaded, 16)
            sp.dma_start(Vn[:, :], io["new_v"][SEQ:TOK, :]).then_inc(tables_loaded, 16)

            prefetch(sp)

            def keys(b, s, i):
                sp.wait_ge(qk[s], i)
                load_keys(sp, io, Kc, keys_loaded, b, s)

            def values(b, s, i):
                sp.wait_ge(pv[s], i)
                load_values(sp, io, Vc, values_loaded, b, s)

            keys(2, 0, 1)
            with sp.Fori(1, DB // 2 - 1) as i:
                keys(i * 2 + 1, 1, i)
                values(i * 2, 0, i)
                keys(i * 2 + 2, 0, i + 1)
                values(i * 2 + 1, 1, i)
            last = DB // 2 - 1
            keys(DB - 1, 1, last)
            values(DB - 2, 0, last)
            values(DB - 1, 1, last)

        @block.gpsimd
        def _(pool):
            for s in range(2):
                pool.memset(Q[s][:, :], 0.0).then_inc(zeroed[s], 1)

            pool.wait_ge(zeroed[0], 1)
            pool.wait_ge(zeroed[1], 1)

            def front(b, s, i):
                pool.wait_ge(qk[s], i)
                pool.wait_ge(q_ready[1 - s], (i + s) * 2)
                for u in range(2):
                    pool.wait_ge(q_ready[s], i * 2 + u)
                    pool.tensor_copy(Q[s][u * HD:(u + 1) * HD, :].rearrange("p (j x) -> p j x", j=NPAIR)[:, :, u * DT:(u + 1) * DT],
                                     qT[u * HD:(u + 1) * HD, :, ds(b * DT + SEQ, DT)]).then_inc(q_ready[s], 1)

            over_sequences(pool, front, nothing, nothing)

        @block.vector
        def _(dve):
            dve.wait_ge(tables_loaded, 48)

            def front(b, s, i):
                dve.wait_ge(qk[s], i + 1)
                dve.wait_ge(turn[s], i)
                dve.scalar_tensor_tensor(Z[:, s, 0:PAST], pS[:, 0:2, :].rearrange("p a b -> p (a b)"), HD ** -0.5, past[:, :],
                                         ALU.mult, ALU.add)
                dve.scalar_tensor_tensor(Z[:, s, PAST:], pS[:, 2, 0:NS], HD ** -0.5, new[:, ds(b * -DT + (DB - 1) * DT, NS)],
                                         ALU.mult, ALU.add).then_inc(z[s], 1)
                dve.wait_ge(z[s], i + 1)
                dve.reduce_max(nmax[:, s, :], Z[:, s, :], AX.X, negate=True).then_inc(mx[s], 1)

                dve.wait_ge(ex[s], i + 1)
                dve.reciprocal(inv[:, s, :], total[:, s, :]).then_inc(iv[s], 1)
                dve.wait_ge(iv[s], i + 1)
                dve.tensor_scalar(Z[:, s, :], Z[:, s, :], inv[:, s, :], None, ALU.mult).then_inc(norm[s], 1)

            def back(b, s, i):
                dve.wait_ge(o_turn[s], i + 1)
                for u in range(2):
                    last = dve.tensor_copy(mixT[u * HD:(u + 1) * HD, 0:NPAIR, ds(b * DT + SEQ, DT)],
                                           pX[u * HD:(u + 1) * HD, :].rearrange("p (j x) -> p j x", j=NPAIR)[:, :, u * DT:(u + 1) * DT])
                last.then_inc(out[s], 1)

            over_sequences(dve, front, back, nothing)

        @block.scalar
        def _(act):
            def front(b, s, i):
                act.wait_ge(mx[s], i + 1)
                act.activation(Z[:, s, :], Z[:, s, :], ACT.Exp, bias=nmax[:, s, :], accum_out=total[:, s, :]).then_inc(ex[s], 1)


            def copy_out(b, s, i):
                act.wait_ge(pv[s], i + 1)
                act.wait_ge(o_turn[1 - s], i + s)
                act.activation(O[:, :], pO[:, :], ACT.Copy).then_inc(copied[s], 1)

            def read_turned(b, s, i):
                act.wait_ge(turn[s], i + 1)
                act.wait_ge(pv[s], i)
                act.activation(PT[s][:, 0:NQB, :].rearrange("p n r -> p (n r)"), pT[:, 0, :], ACT.Copy)
                act.activation(PT[s][0:NS, NQB, :], pT[0:NS, 1, 0:R], ACT.Copy).then_inc(pt[s], 1)

            over_sequences(act, front, copy_out, read_turned)

        @block.tensor
        def _(pe):
            pe.wait_ge(tables_loaded, 48)

            def front(b, s, i):
                pe.wait_ge(keys_loaded[s], i * 16 + 16)
                pe.wait_ge(q_ready[s], i * 2 + 2)
                pe.wait_ge(z[1 - s], i + s)
                for c in range(3):
                    for j in range(NPAIR):
                        keys = Kc[:, s, j, c * 512:(c + 1) * 512] if c < 2 else kT[:, j, SEQ:TOK]
                        last = pe.matmul(pS[:, c, 0:512 if c < 2 else NS], Q[s][:, j * R:(j + 1) * R], keys,
                                         start=(j == 0), stop=(j == NPAIR - 1))
                last.then_inc(qk[s], 1)

            def turned(b, s, i):
                pe.wait_ge(norm[s], i + 1)
                pe.wait_ge(pt[1 - s], i + s)
                pe.sem_inc(turn_begun, 1)
                pe.wait_ge(turn_begun, 1)
                for n in range(NQB):
                    pe.transpose(pT[:, 0, n * R:(n + 1) * R], Z[:, s, n * P:(n + 1) * P], ident[0:R, 0:R])
                pe.transpose(pT[0:NS, 1, 0:R], Z[:, s, PAST:], ident[0:R, 0:R]).then_inc(turn[s], 1)

            def back(b, s, i):
                pe.wait_ge(pt[s], i + 1)
                pe.wait_ge(copied[1 - s], i + s)
                pe.wait_ge(values_loaded[s], i * 16 + 16)
                for n in range(NQB):
                    pe.matmul(pO[:, :], PT[s][:, n, :], Vc[:, s, n, :], start=(n == 0), stop=False)
                pe.matmul(pO[:, :], PT[s][0:NS, NQB, :], Vn[:, :], start=False, stop=True).then_inc(pv[s], 1)

            def turn_out(b, s, i):
                pe.wait_ge(copied[s], i + 1)
                pe.wait_ge(out[1 - s], i + s)
                pe.sem_inc(turn_begun, 1)
                pe.wait_ge(turn_begun, 1)
                for j in range(NPAIR):
                    last = pe.transpose(pX[:, j * R:(j + 1) * R], O[:, j * P:(j + 1) * P], ident[0:R, 0:R])
                last.then_inc(o_turn[s], 1)

            over_sequences(pe, front, back, turned, turn_out)
class ResidentWeight:

    def __init__(self, sem, place, place_raw, tag, dram, width, in_place=False):
        self.dram, self.chunks = dram, dram.shape[0] // P
        shape, start = [P, self.chunks, width], place_raw.offset
        self.raw = place_raw(tag + "_raw", shape)
        self.hi = place(tag + "_hi", shape, F32R)
        self.lo = (Place(place.nc, start) if in_place else place)(tag + "_lo", shape, F32R)
        self.loaded, self.hi_done, self.lo_done = (sem(f"{tag}_{n}") for n in ("loaded", "hi_done", "lo_done"))

    def load(self, sp):
        for k in range(self.chunks):
            sp.dma_start(self.raw[:, k, :], self.dram[k * P:(k + 1) * P, :]).then_inc(self.loaded, 16)

    def split_hi(self, act):
        act.wait_ge(self.loaded, 16 * self.chunks)
        for k in range(self.chunks):
            act.activation(self.hi[:, k, :], self.raw[:, k, :], ACT.Copy).then_inc(self.hi_done, 1)

    def split_lo_chunk(self, dve, k):
        dve.wait_ge(self.hi_done, k + 1)
        dve.tensor_tensor(self.lo[:, k, :], self.raw[:, k, :], self.hi[:, k, :].bitcast(F32),
                          ALU.subtract).then_inc(self.lo_done, 1)

    def split_lo(self, dve):
        for k in range(self.chunks):
            self.split_lo_chunk(dve, k)


def then_weight(front, split, engine):
    def step(s, i, r, n):
        front(s, i, r, n)
        if isinstance(n, int) and n == 0:
            split(engine)
    return step


def split_product(pe, out, weights_first, n_k, ready=nothing):
    for k in range(n_k):
        ready(k)
        a_hi, a_lo, b_hi, b_lo = weights_first(k)
        for part, (a, b) in enumerate(((a_hi, b_hi), (a_hi, b_lo), (a_lo, b_hi))):
            last = pe.matmul(out, a, b, start=(k == 0 and part == 0), stop=(k == n_k - 1 and part == 2))
    return last


def stage_output(nc, sem, io, ident, mixT, R, w, hT_hi, hT_lo, place, prefetch):
    ln = LayerNorm(sem, place, "op_ln")
    h0 = place("op_h0", [P, 2, D])
    m_hi = [place(f"op_m_hi{s}", [P, KD, P], F32R) for s in range(2)]
    m_lo = [place(f"op_m_lo{s}", [P, KD, P], F32R) for s in range(2)]
    two = lambda n: [sem(f"op_{n}{s}") for s in range(2)]
    h0_loaded, hi_done, lo_done, mm_done, x_done, scaled, turned, thi_done, tlo_done = (
        two(n) for n in ("h0_loaded", "hi_done", "lo_done", "mm_done", "x_done", "scaled", "turned", "thi_done", "tlo_done"))
    with ExitStack() as ctx:
        pM = [ctx.enter_context(nc.psum_tensor(f"op_M{s}", [P, 2, 512], F32)) for s in range(2)]
        pT = ctx.enter_context(nc.psum_tensor("op_T", [P, KD, P], F32))
        block = ctx.enter_context(nc.Block())
        row = lambda n, r: R[0:r, ds(n, 1), :].squeeze(1)

        @block.sync
        def _(sp):
            ln.load(sp, io["ln1_g"], io["ln1_b"])
            prefetch(sp)

            def front(s, i, r, n):
                sp.wait_ge(scaled[s], i)
                sp.wait_ge(turned[s], i)
                sp.dma_start(h0[0:r, s, :], io["h0"][ds(n * P, r), :]).then_inc(h0_loaded[s], 16)

            over_blocks(sp, (1, front))

        @block.gpsimd
        def _(pool):
            ln.constants(pool)

            def back(s, i, r, n):
                ln.inverse_root(pool, s, i, r)
                ln.gain(pool, row(n, r), s, i, r)

            over_blocks(pool, (0, back))

        @block.scalar
        def _(act):
            def front(s, i, r, n):
                act.wait_ge(mm_done[s], i)
                act.activation(m_hi[s][:, :, 0:r], mixT[:, :, ds(n * P, r)], ACT.Copy).then_inc(hi_done[s], 1)

            def normed(s, i, r, n):
                act.wait_ge(turned[s], i + 1)
                act.activation(hT_hi[:, :, ds(n * P, r)], pT[:, :, 0:r], ACT.Copy).then_inc(thi_done[s], 1)
                act.activation(row(n, r), h0[0:r, s, :], ACT.Copy, scale=ALPHA).then_inc(scaled[s], 1)

            over_blocks(act, (1, then_weight(front, w.split_hi, act)), (-1, normed), (0, lambda s, i, r, n: ln.normalise(act, row(n, r), row(n, r), s, i, r)))

        @block.vector
        def _(dve):
            def front(s, i, r, n):
                dve.wait_ge(hi_done[s], i + 1)
                dve.tensor_tensor(m_lo[s][:, :, 0:r], mixT[:, :, ds(n * P, r)], m_hi[s][:, :, 0:r].bitcast(F32),
                                  ALU.subtract).then_inc(lo_done[s], 1)

            def back(s, i, r, n):
                dve.wait_ge(mm_done[s], i + 1)
                dve.wait_ge(h0_loaded[s], i * 16 + 16)
                dve.scalar_tensor_tensor(row(n, r), h0[0:r, s, :], ALPHA, pM[s][0:r, :, :].rearrange("p a b -> p (a b)"),
                                         ALU.mult, ALU.add).then_inc(x_done[s], 1)
                dve.wait_ge(ln.loaded, 32)
                dve.wait_ge(x_done[s], i + 1)
                ln.statistics(dve, row(n, r), s, i, r)

            def normed_lo(s, i, r, n):
                dve.wait_ge(thi_done[s], i + 1)
                dve.tensor_tensor(hT_lo[:, :, ds(n * P, r)], pT[:, :, 0:r], hT_hi[:, :, ds(n * P, r)].bitcast(F32),
                                  ALU.subtract).then_inc(tlo_done[s], 1)

            def finish(s, i, r, n):
                ln.shift(dve, s, i, r)
                ln.bias(dve, row(n, r), s, i, r, h0[0:r, s, :])

            over_blocks(dve, (1, then_weight(front, w.split_lo, dve)), (0, back), (-1, normed_lo), (0, finish))

        @block.tensor
        def _(pe):
            def back(s, i, r, n):
                pe.wait_ge(lo_done[s], i + 1)
                pe.wait_ge(x_done[s], i)
                first = isinstance(n, int) and n == 0

                def ready(k):
                    if first:
                        pe.wait_ge(w.lo_done, k + 1)

                for half in range(2):
                    c = slice(half * 512, (half + 1) * 512)
                    last = split_product(pe, pM[s][0:r, half, :], lambda k: (
                        m_hi[s][:, k, 0:r], m_lo[s][:, k, 0:r], w.hi[:, k, c], w.lo[:, k, c]), KD, ready)
                last.then_inc(mm_done[s], 1)

            def turn(s, i, r, n):
                pe.wait_ge(ln.done[s], i + 1)
                if not (isinstance(n, int) and n == 0):
                    pe.wait_ge(tlo_done[1 - s], i + s)
                for k in range(KD):
                    last = pe.transpose(pT[:, k, 0:r], h0[0:r, s, k * P:(k + 1) * P], ident[0:r, 0:r])
                last.then_inc(turned[s], 1)

            over_blocks(pe, (0, back), (-1, turn))


class UpWeights:

    def __init__(self, sem, place, w_up):
        self.w_up, self.raw = w_up, place("ml_up_raw", [P, KD, P])
        self.loaded, self.lo_done = sem("ml_up_loaded"), sem("ml_up_lo_done")

    def load(self, sp, block):
        sp.wait_ge(self.lo_done, block)
        sp.dma_start(self.raw[:, :, :], w_raw_view(self.w_up, block * P, P)).then_inc(self.loaded, 16)


def stage_mlp(nc, sem, io, R, hT_hi, hT_lo, up, w_gate, place):
    FB = 4
    NC = DFF // (FB * P)
    UNITS = NB * 2
    u_hi = [place(f"ml_u_hi{f}", [P, TOK], F32R) for f in range(FB)]
    u_lo = [place(f"ml_u_lo{f}", [P, TOK], F32R) for f in range(FB)]
    up_raw, down_raw = up.raw, place("ml_down_raw", [P, D])
    up_hi = [place(f"ml_up_hi{s}", [P, KD, P], F32R) for s in range(2)]
    up_lo = [place(f"ml_up_lo{s}", [P, KD, P], F32R) for s in range(2)]
    down_hi, down_lo = place("ml_down_hi", [P, FB, D], F32R), place("ml_down_lo", [P, FB, D], F32R)
    relu, u = place("ml_relu", [P, TOK]), place("ml_u", [P, TOK])
    one = lambda *names: [sem("ml_" + n) for n in names]
    many = lambda n, k: [sem(f"ml_{n}{s}") for s in range(k)]
    up_loaded, up_lo_done = up.loaded, up.lo_done
    up_hi_done, down_loaded, down_hi_done, down_lo_done, down_used = one(
        "up_hi_done", "down_loaded", "down_hi_done", "down_lo_done", "down_used")
    up_mm, dn_mm, added = many("up_mm", 2), many("dn_mm", 2), many("added", 2)
    relu_done = [many(f"relu{s}_", 3) for s in range(2)]
    mul_done, sq_done, ulo_done = many("mul", 3), many("sq", 3), many("ulo", 3)

    def rows(n):
        return NS if n == NB - 1 else P

    with ExitStack() as ctx:
        pU = [ctx.enter_context(nc.psum_tensor(f"ml_U{s}", [P, 3, 512], F32)) for s in range(2)]
        pD = [ctx.enter_context(nc.psum_tensor(f"ml_D{s}", [P, 512], F32)) for s in range(2)]
        block = ctx.enter_context(nc.Block())

        def chunks(engine, chunk):
            chunk(0, False)
            with engine.Fori(1, NC - 1) as c:
                chunk(c, False)
            chunk(NC - 1, True)

        @block.sync
        def _(sp):
            def chunk(c, last):
                for f in range(FB):
                    if not (last and f >= 2):
                        up.load(sp, c * FB + (f + 2))
                    sp.wait_ge(down_lo_done, c * FB + f)
                    sp.dma_start(down_raw[:, :], io["w_down"][ds(c * (FB * P) + f * P, P), :]).then_inc(down_loaded, 16)

            up.load(sp, 1)
            chunks(sp, chunk)
            sp.wait_ge(up_mm[0], 3 * FB // 2 * NC)
            sp.wait_ge(up_mm[1], 3 * FB // 2 * NC)
            w_gate.load(sp)

        @block.gpsimd
        def _(pool):
            def chunk(c, last):
                for f in range(FB):
                    for g, (col, w) in enumerate(GROUPS):
                        pool.wait_ge(relu_done[f % 2][g], c * 2 + (f // 2 + 1))
                        pool.wait_ge(ulo_done[g], c * FB + f)
                        x = relu[:, col:col + w]
                        pool.tensor_tensor(u[:, col:col + w], x, x, ALU.mult).then_inc(mul_done[g], 1)

            chunks(pool, chunk)

        @block.scalar
        def _(act):
            def split_up(c, f):
                act.wait_ge(up_loaded, c * (16 * FB) + 16 * (f + 1))
                act.wait_ge(up_mm[f % 2], c * 6 + 3 * (f // 2))
                act.activation(up_hi[f % 2][:, :, :], up_raw[:, :, :], ACT.Copy).then_inc(up_hi_done, 1)

            def chunk(c, last):
                for f in range(FB):
                    s = f % 2
                    for g, (col, w) in enumerate(GROUPS):
                        act.wait_ge(up_mm[s], c * 6 + (3 * (f // 2) + g + 1))
                        act.wait_ge(mul_done[g], c * FB + f)
                        act.activation(relu[:, col:col + w], pU[s][:, g, 0:w], ACT.Relu).then_inc(relu_done[s][g], 1)
                        act.wait_ge(relu_done[s][g], c * 2 + (f // 2 + 1))
                        act.wait_ge(down_used, c)
                        act.activation(u_hi[f][:, col:col + w], relu[:, col:col + w], ACT.Square).then_inc(sq_done[g], 1)
                    if not (last and f >= 2):
                        split_up(c, f + 2)
                    act.wait_ge(down_loaded, c * (16 * FB) + 16 * (f + 1))
                    act.activation(down_hi[:, f, :], down_raw[:, :], ACT.Copy).then_inc(down_hi_done, 1)

            split_up(0, 0)
            split_up(0, 1)
            chunks(act, chunk)
            w_gate.split_hi(act)

        @block.vector
        def _(dve):
            def split_up(c, f):
                dve.wait_ge(up_hi_done, c * FB + (f + 1))
                dve.tensor_tensor(up_lo[f % 2][:, :, :], up_raw[:, :, :], up_hi[f % 2][:, :, :].bitcast(F32),
                                  ALU.subtract).then_inc(up_lo_done, 1)

            def chunk(c, last):
                for f in range(FB):
                    for g, (col, w) in enumerate(GROUPS):
                        dve.wait_ge(mul_done[g], c * FB + (f + 1))
                        dve.wait_ge(sq_done[g], c * FB + (f + 1))
                        dve.tensor_tensor(u_lo[f][:, col:col + w], u[:, col:col + w], u_hi[f][:, col:col + w].bitcast(F32),
                                          ALU.subtract).then_inc(ulo_done[g], 1)
                    if not (last and f >= 2):
                        split_up(c, f + 2)
                    dve.wait_ge(down_hi_done, c * FB + (f + 1))
                    dve.tensor_tensor(down_lo[:, f, :], down_raw[:, :], down_hi[:, f, :].bitcast(F32),
                                      ALU.subtract).then_inc(down_lo_done, 1)
                for v in range(UNITS):
                    n, half, s = v // 2, v % 2, v % 2
                    r = rows(n)
                    dve.wait_ge(dn_mm[s], c * NB + (v // 2 + 1))
                    dve.wait_ge(added[s], c * NB + v // 2)
                    acc = R[0:r, n, half * 512:(half + 1) * 512]
                    dve.tensor_tensor(acc, acc, pD[s][0:r, :], ALU.add).then_inc(added[s], 1)
                    if last and v >= UNITS - KD:
                        w_gate.split_lo_chunk(dve, v - (UNITS - KD))

            split_up(0, 0)
            split_up(0, 1)
            chunks(dve, chunk)

        @block.tensor
        def _(pe):
            def down(c, v, f):
                n, half, s = v // 2, v % 2, v % 2
                r = rows(n)
                cols, out = slice(half * 512, (half + 1) * 512), pD[s][0:r, :]
                a_hi, a_lo = u_hi[f][:, n * P:n * P + r], u_lo[f][:, n * P:n * P + r]
                for part, (a, b) in enumerate(((a_hi, down_hi), (a_hi, down_lo), (a_lo, down_hi))):
                    last = pe.matmul(out, a, b[:, f, cols], start=(f == 0 and part == 0), stop=(f == FB - 1 and part == 2))
                return last

            def chunk(c, last):
                for f in range(FB):
                    s = f % 2
                    pe.wait_ge(up_lo_done, c * FB + (f + 1))
                    for g, (col, w) in enumerate(GROUPS):
                        pe.wait_ge(relu_done[s][g], c * 2 + f // 2)
                        split_product(pe, pU[s][:, g, 0:w], lambda k: (
                            up_hi[s][:, k, :], up_lo[s][:, k, :], hT_hi[:, k, col:col + w], hT_lo[:, k, col:col + w]),
                            KD).then_inc(up_mm[s], 1)
                order = [(v, f) for f in range(FB - 1) for v in range(2)] + [(v, FB - 1) for v in range(2)]
                order += [(v, f) for v in range(2, UNITS) for f in range(FB)]
                for at, (v, f) in enumerate(order):
                    if f == 0:
                        pe.wait_ge(added[v % 2], c * NB + v // 2)
                    if v == 0:
                        pe.wait_ge(down_lo_done, c * FB + (f + 1))
                        for g in range(3):
                            pe.wait_ge(ulo_done[g], c * FB + (f + 1))
                    last_mm = down(c, v, f)
                    if f == FB - 1:
                        last_mm.then_inc(dn_mm[v % 2], 1)
                        if v == UNITS - 1:
                            pe.wait_ge(dn_mm[v % 2], c * NB + NB)
                            pe.sem_inc(down_used, 1)

            chunks(pe, chunk)


def stage_gate(nc, sem, io, ident, R, wg, wp, place):
    ln2, ln3 = LayerNorm(sem, place, "gt_ln2"), LayerNorm(sem, place, "gt_ln3")
    pe_raw = place("gt_pe", [P, 2, KPLE, P])
    h_hi = [place(f"gt_h_hi{s}", [P, KD, P], F32R) for s in range(2)]
    h_lo = [place(f"gt_h_lo{s}", [P, KD, P], F32R) for s in range(2)]
    p_hi = [place(f"gt_p_hi{s}", [P, KPLE, P], F32R) for s in range(2)]
    p_lo = [place(f"gt_p_lo{s}", [P, KPLE, P], F32R) for s in range(2)]
    H = place("gt_h", [P, 2, D])
    gate = wp.raw
    names = "pe_loaded staged turned hi lo phi plo gate_mm ple_mm sg gated x stored".split()
    S = {n: [sem(f"gt_{n}{s}") for s in range(2)] for n in names}
    with ExitStack() as ctx:
        pT = ctx.enter_context(nc.psum_tensor("gt_T", [P, KD, P], F32))
        pG = [ctx.enter_context(nc.psum_tensor(f"gt_G{s}", [P, 2, 512], F32)) for s in range(2)]
        pP = ctx.enter_context(nc.psum_tensor("gt_P", [P, 2, 512], F32))
        block = ctx.enter_context(nc.Block())
        row = lambda n, r: R[0:r, ds(n, 1), :].squeeze(1)
        flat = lambda t, r: t[0:r, :, :].rearrange("p a b -> p (a b)")

        @block.sync
        def _(sp):
            ln2.load(sp, io["ln2_g"], io["ln2_b"])
            wp.load(sp)
            ln3.load(sp, io["ln3_g"], io["ln3_b"])

            def load(s, i, r, n):
                sp.wait_ge(S["plo"][s], i)
                sp.dma_start(pe_raw[:, s, :, 0:r], io["pT"][:, ds(n * P, r)].rearrange("(k p) t -> p k t", p=P))\
                    .then_inc(S["pe_loaded"][s], 16)

            def store(s, i, r, n):
                sp.wait_ge(ln3.done[s], i + 1)
                sp.dma_start(io["y"][ds(n * P, r), :], gate[0:r, s, :]).then_inc(S["stored"][s], 16)

            over_blocks(sp, (2, load), (-1, store))
            sp.wait_ge(S["stored"][0], 16 * (NQB // 2 + 1))
            sp.wait_ge(S["stored"][1], 16 * (NQB // 2))

        @block.gpsimd
        def _(pool):
            ln2.constants(pool)
            ln3.constants(pool)
            over_blocks(pool, (2, lambda s, i, r, n: ln2.inverse_root(pool, s, i, r)),
                        (2, lambda s, i, r, n: ln2.gain(pool, row(n, r), s, i, r)),
                        (-1, lambda s, i, r, n: ln3.inverse_root(pool, s, i, r)),
                        (-1, lambda s, i, r, n: ln3.gain(pool, gate[0:r, s, :], s, i, r)))

        @block.scalar
        def _(act):
            def sigmoid(s, i, r, n):
                act.wait_ge(S["gate_mm"][s], i + 1)
                act.wait_ge(S["stored"][s], i * 16)
                if isinstance(n, int) and n < 2:
                    act.wait_ge(wp.lo_done, KPLE)
                act.activation(gate[0:r, s, :], flat(pG[s], r), ACT.Sigmoid).then_inc(S["sg"][s], 1)

            def split(s, i, r, n):
                act.wait_ge(S["turned"][s], i + 1)
                act.activation(h_hi[s][:, :, 0:r], pT[:, :, 0:r], ACT.Copy).then_inc(S["hi"][s], 1)
                act.wait_ge(S["pe_loaded"][s], i * 16 + 16)
                act.wait_ge(S["ple_mm"][s], i)
                act.activation(p_hi[s][:, :, 0:r], pe_raw[:, s, :, 0:r], ACT.Copy).then_inc(S["phi"][s], 1)

            def normalise2(s, i, r, n):
                ln2.normalise(act, row(n, r), row(n, r), s, i, r)

            def stage(s, i, r, n):
                act.wait_ge(ln2.done[s], i + 1)
                act.wait_ge(S["turned"][s], i)
                act.activation(H[0:r, s, :], row(n, r), ACT.Copy).then_inc(S["staged"][s], 1)

            over_blocks(act, (1, stage), (-1, sigmoid), (2, then_weight(normalise2, wp.split_hi, act)), (1, split),
                        (-1, lambda s, i, r, n: ln3.normalise(act, gate[0:r, s, :], gate[0:r, s, :], s, i, r)))

        @block.vector
        def _(dve):
            def product(s, i, r, n):
                dve.wait_ge(S["sg"][s], i + 1)
                dve.wait_ge(S["ple_mm"][s], i + 1)
                x = gate[0:r, s, :]
                dve.tensor_tensor(x, x, flat(pP, r), ALU.mult).then_inc(S["gated"][s], 1)
                dve.wait_ge(S["gated"][s], i + 1)
                dve.scalar_tensor_tensor(x, row(n, r), ALPHA, x, ALU.mult, ALU.add).then_inc(S["x"][s], 1)
                dve.wait_ge(S["x"][s], i + 1)
                dve.wait_ge(ln3.loaded, 32)
                ln3.statistics(dve, x, s, i, r)

            def split(s, i, r, n):
                dve.wait_ge(S["hi"][s], i + 1)
                dve.tensor_tensor(h_lo[s][:, :, 0:r], pT[:, :, 0:r], h_hi[s][:, :, 0:r].bitcast(F32),
                                  ALU.subtract).then_inc(S["lo"][s], 1)
                dve.wait_ge(S["phi"][s], i + 1)
                dve.tensor_tensor(p_lo[s][:, :, 0:r], pe_raw[:, s, :, 0:r], p_hi[s][:, :, 0:r].bitcast(F32),
                                  ALU.subtract).then_inc(S["plo"][s], 1)

            def bias2(s, i, r, n):
                ln2.bias(dve, row(n, r), s, i, r)

            over_blocks(dve, (2, lambda s, i, r, n: ln2.statistics(dve, row(n, r), s, i, r)),
                        (2, lambda s, i, r, n: ln2.shift(dve, s, i, r)), (-1, product), (1, split),
                        (2, then_weight(bias2, wp.split_lo, dve)),
                        (-1, lambda s, i, r, n: ln3.shift(dve, s, i, r)),
                        (-1, lambda s, i, r, n: ln3.bias(dve, gate[0:r, s, :], s, i, r)))

        @block.tensor
        def _(pe):
            def turn(s, i, r, n):
                pe.wait_ge(S["staged"][s], i + 1)
                if not (isinstance(n, int) and n == 0):
                    pe.wait_ge(S["lo"][1 - s], i + s)
                for k in range(KD):
                    last = pe.transpose(pT[:, k, 0:r], H[0:r, s, k * P:(k + 1) * P], ident[0:r, 0:r])
                last.then_inc(S["turned"][s], 1)

            def products(s, i, r, n):
                pe.wait_ge(S["lo"][s], i + 1)
                pe.wait_ge(S["sg"][s], i)
                first = isinstance(n, int) and n == 0
                if first:
                    pe.wait_ge(wg.lo_done, KD)
                for half in range(2):
                    c = slice(half * 512, (half + 1) * 512)
                    last = split_product(pe, pG[s][0:r, half, :], lambda k: (
                        h_hi[s][:, k, 0:r], h_lo[s][:, k, 0:r], wg.hi[:, k, c], wg.lo[:, k, c]), KD)
                last.then_inc(S["gate_mm"][s], 1)
                if first:
                    pe.wait_ge(wp.lo_done, KPLE)
                pe.wait_ge(S["plo"][s], i + 1)
                pe.wait_ge(S["gated"][1 - s], i + s)
                for half in range(2):
                    c = slice(half * 512, (half + 1) * 512)
                    last = split_product(pe, pP[0:r, half, :], lambda k: (
                        p_hi[s][:, k, 0:r], p_lo[s][:, k, 0:r], wp.hi[:, k, c], wp.lo[:, k, c]), KPLE)
                last.then_inc(S["ple_mm"][s], 1)

            over_blocks(pe, (1, turn), (0, products))
OUTPUTS = {"y": (TOK, D), "new_k": (TOK, DA), "new_v": (TOK, DA), "new_convT": (P, NXBC, (CW - 1) * (1 + DB)),
           "new_ssm_promptT": (NSTATE, DA), "new_ssm_sampleT": (NSTATE, DB, DA)}


SAMPLE_BYTES = 4 * (PAST + (2 * DB - 1) * DT + 2 * DA + 2 * NPAIR * (NH + 2) * DT + 2 * (PAST + NS) + 2 * (NQB + 1) * NH * DT + 192)


def build(nc, io):
    io = dict(io)
    io["h0"] = nc.dram_tensor("h0_scratch", [TOK, D], F32, kind="Internal").ap()
    io["z_act"] = nc.dram_tensor("z_act_scratch", [TOK, DA], F32, kind="Internal").ap()
    with ExitStack() as ctx:
        held, in_use = [ExitStack()], []

        def sem(name):
            in_use.append(held[0].enter_context(nc.semaphore(name)))
            return in_use[-1]

        def kept_sem(name):
            return ctx.enter_context(nc.semaphore(name))

        def clear_semaphores():
            with nc.Block() as block:
                @block.sync
                def _(sp):
                    for s in in_use[0::4]:
                        sp.sem_clear(s)

                @block.scalar
                def _(act):
                    for s in in_use[1::4]:
                        act.sem_clear(s)

                @block.vector
                def _(dve):
                    for s in in_use[2::4]:
                        dve.sem_clear(s)

                @block.gpsimd
                def _(pool):
                    for s in in_use[3::4]:
                        pool.sem_clear(s)
            held[0].close()
            held[0] = ExitStack()
            in_use.clear()

        ctx.callback(lambda: held[0].close())

        const = Place(nc, SBUF_START)
        ident = const("ident", [P, P])
        base = const.offset
        qk = Place(nc, base)
        qT, kT = qk("qT", [P, NPAIR, TOK]), qk("kT", [P, NPAIR, TOK])
        hT_hi, hT_lo = qk("hT_hi", [P, KD, TOK], F32R), qk("hT_lo", [P, KD, TOK], F32R)
        xbc_start = qk.offset
        Xt, Bt = qk("Xt", [P, NB, DA]), qk("Bt", [P, NB, NGROUP * NSTATE])
        BT, CT = qk("BT", [P, NGROUP, TOK]), qk("CT", [P, NGROUP, TOK])
        dt_raw = qk("dt_raw", [P, NB, NH])
        after_xbc = qk.offset
        late = Place(nc, base)
        R, mixT = late("R", [P, NB, D]), late("mixT", [P, KD, TOK])
        after_mix = late.offset

        consts_loaded = sem("consts_loaded")
        with nc.Block() as block:
            @block.sync
            def _(sp):
                sp.dma_start(ident[:, :], io["c_ident"]).then_inc(consts_loaded, 16)
                sp.wait_ge(consts_loaded, 16)

        projection = Place(nc, after_xbc)
        weights = ProjectionWeights(sem, projection, io["w_in"])
        stage_input_norm(nc, sem, io, ident, hT_hi, hT_lo, weights, Place(nc, xbc_start, after_xbc, projection.offset))
        stage_projection(nc, sem, io, ident, hT_hi, hT_lo, weights, qT, kT, Xt, Bt, BT, CT, dt_raw, projection)
        stage_ssd(nc, sem, io, ident, Xt, Bt, BT, CT, dt_raw, mixT, Place(nc, after_mix, xbc_start, after_xbc))
        clear_semaphores()
        attention = Place(nc, after_mix)
        Kc, Vc = attention("Kc", [P, 2, NPAIR, PAST]), attention("Vc", [P, 2, NQB, DA])
        keys_loaded, values_loaded = ([sem(f"cache_{n}_loaded{s}") for s in range(2)] for n in ("keys", "values"))
        after_cache = attention.offset

        def prefetch(sp):
            for b in range(2):
                load_keys(sp, io, Kc, keys_loaded, b, b)
                load_values(sp, io, Vc, values_loaded, b, b)

        stage_prompt_attention(nc, sem, io, ident, qT, kT, mixT, attention, prefetch)
        sample = Place(nc, after_cache)
        after_sample = after_cache + SAMPLE_BYTES
        for_raw = Place(nc, after_sample)
        w_out = ResidentWeight(kept_sem, Place(nc, after_mix), for_raw, "op_w", io["w_out"], D)
        stage_sample_attention(nc, sem, io, ident, qT, kT, mixT, Kc, Vc, keys_loaded, values_loaded, sample, w_out.load)
        assert sample.offset <= after_sample
        clear_semaphores()
        after_R = base + 4 * NB * D
        h1T_hi = Place(nc, after_R)("h1T_hi", [P, KD, TOK], F32R)
        last = Place(nc, after_sample)
        h1T_lo = last("h1T_lo", [P, KD, TOK], F32R)
        up = UpWeights(sem, last, io["w_up"])
        stage_output(nc, sem, io, ident, mixT, R, w_out, h1T_hi, h1T_lo, Place(nc, after_cache, after_sample, last.offset),
                     lambda sp: up.load(sp, 0))
        w_gate = ResidentWeight(sem, Place(nc, after_sample), Place(nc, after_R), "gt_wg", io["w_gate"], D, in_place=True)
        gate = Place(nc, after_mix, after_sample, last.offset)
        w_ple = ResidentWeight(sem, gate, gate, "gt_wp", io["w_ple"], D)
        stage_mlp(nc, sem, io, R, h1T_hi, h1T_lo, up, w_gate, Place(nc, after_mix, after_sample, last.offset))
        stage_gate(nc, sem, io, ident, R, w_gate, w_ple, gate)


def kernel(**inputs):
    import concourse.bacc as bacc
    from concourse.bass_utils import run_bass_kernel_spmd

    x = {k: np.asarray(v) for k, v in inputs.items()}

    def features_first(a):
        a = a.reshape(a.shape[:-1] + (-1, P))
        return np.moveaxis(a, (-1, -2), (0, 1))

    arrays = {
        "x_prompt": x["x_prompt"][0], "x_sample": x["x_sample"].reshape(NS, D),
        "cache_kT": x["cache_k"][0].reshape(DB, PAST, NPAIR, P).transpose(0, 3, 2, 1),
        "cache_v": x["cache_v"][0].reshape(DB, PAST, DA),
        "state_convT": features_first(x["state_conv"][0].reshape(DB * (CW - 1), CD)),
        "state_ssmT": x["state_ssm"][0].reshape(DB, DA, NSTATE).transpose(2, 0, 1),
        "pT": np.concatenate([x["p_prompt"][0, 0], x["p_sample"][0].reshape(NS, DPLE)]).T,
        "conv_wT": np.moveaxis(features_first(x["conv_w"][0]), 2, -1), "conv_bT": features_first(x["conv_b"][0]),
        "norm_wT": features_first(x["ssd_norm_w"][0]),
        **{k: x[k] for k in ("ln_in_g", "ln_in_b")},
        **{k: x[k][0] for k in ("w_in", "dt_bias", "a_log", "d_skip", "w_out", "ln1_g", "ln1_b", "w_up",
                                "w_down", "ln2_g", "ln2_b", "w_gate", "w_ple", "ln3_g", "ln3_b")},
        **shape_constants(), **attention_constants(),
    }
    arrays = {k: np.ascontiguousarray(v) for k, v in arrays.items()}
    nc = bacc.Bacc("TRN2", target_bir_lowering=False, num_devices=1)
    io = {k: nc.dram_tensor("in_" + k, v.shape, mybir.dt.from_np(v.dtype), kind="ExternalInput").ap() for k, v in arrays.items()}
    io.update({k: nc.dram_tensor("out_" + k, shape, F32, kind="ExternalOutput").ap() for k, shape in OUTPUTS.items()})
    build(nc, io)
    result = run_bass_kernel_spmd(nc, [{"in_" + k: v for k, v in arrays.items()}], core_ids=[0]).results[0]
    y, k, v, conv, ssm_p, ssm_s = (np.asarray(result["out_" + n]) for n in OUTPUTS)
    conv = conv.transpose(2, 1, 0).reshape(-1, CD)
    return (y[:SEQ].reshape(1, SEQ, D), y[SEQ:].reshape(DB, DT, D),
            k[:SEQ].reshape(1, 1, SEQ, NH, HD), v[:SEQ].reshape(1, 1, SEQ, NH, HD),
            k[SEQ:].reshape(1, DB, DT, NH, HD), v[SEQ:].reshape(1, DB, DT, NH, HD),
            conv[:CW - 1].reshape(1, 1, CW - 1, CD), conv[CW - 1:].reshape(1, DB, CW - 1, CD),
            ssm_p.T.reshape(1, 1, NH, HD, NSTATE), ssm_s.transpose(1, 2, 0).reshape(1, DB, NH, HD, NSTATE))
```
